# Optimizing a Trainium2 kernel written in Bass

```python
import jax, jax.numpy as jnp
from jax import lax
import numpy as np

D_MODEL = 1024
BATCH = 1
SEQ = 1024
DEPTH = 1

M_WIDTH = D_MODEL // 2
M_HEADS = 4
M_HEAD_DIM = M_WIDTH // M_HEADS
M_CHUNK = 64
M_CONV = 4
N_WIDTH = D_MODEL - M_WIDTH
N_HEADS = 8
N_KV_GROUPS = 2
N_HEAD_DIM = N_WIDTH // N_HEADS
KV_WIDTH = N_KV_GROUPS * N_HEAD_DIM
CMP_BLOCK = 32
CMP_STRIDE = 16
CMP_HIDDEN = 2 * N_HEAD_DIM
SLC_BLOCK = 64
SLC_TOPK = 16
WINDOW = 512
NSA_Q_BLOCK = 32
ROPE_THETA = 10000.0
MOE_GROUPS = 4
EXPERTS_PER_GROUP = 8
N_EXPERTS = MOE_GROUPS * EXPERTS_PER_GROUP
TOP_K_IN_GROUP = 2
EXPERT_FF = D_MODEL // 2
MOE_ROW_BLOCK = 128
RMS_EPS = 1e-6
IN_WIDTHS = (M_WIDTH, M_WIDTH, M_WIDTH, M_WIDTH, M_HEADS, M_HEADS, N_WIDTH, KV_WIDTH, KV_WIDTH, KV_WIDTH, KV_WIDTH, KV_WIDTH, KV_WIDTH, 3 * N_HEADS)
IN_WIDTH = sum(IN_WIDTHS)

kernel_name = 'hybrid_mlstm_nsa_hmoe_block'

def rms_norm(x, w):
    xf = x.astype(jnp.float32)
    y = xf * lax.rsqrt(jnp.mean(xf * xf, axis=-1, keepdims=True) + RMS_EPS)
    return (y * w.astype(jnp.float32)).astype(x.dtype)

def split_cols(z, widths):
    outs = []
    off = 0
    for w in widths:
        outs.append(z[..., off:off + w])
        off += w
    return outs

def rope(x, positions):
    half = x.shape[-1] // 2
    inv = ROPE_THETA ** (-jnp.arange(half, dtype=jnp.float32) / half)
    ang = positions.astype(jnp.float32)[..., None] * inv
    cos = jnp.cos(ang)[:, :, None, :].astype(x.dtype)
    sin = jnp.sin(ang)[:, :, None, :].astype(x.dtype)
    x1, x2 = x[..., :half], x[..., half:]
    return jnp.concatenate([x1 * cos - x2 * sin, x2 * cos + x1 * sin], axis=-1)

def causal_conv(x, w):
    K, C = w.shape
    return lax.conv_general_dilated(x, w[:, None, :].astype(x.dtype), window_strides=(1,), padding=[(K - 1, 0)], dimension_numbers=('NWC', 'WIO', 'NWC'), feature_group_count=C)

def mlstm_chunkwise(q, k, v, i_pre, f_pre):
    B, S, NH, DH = q.shape
    L = M_CHUNK
    NC = S // L
    f32 = jnp.float32

    def chunks(t):
        return jnp.moveaxis(t, 2, 1).reshape((B, NH, NC, L) + t.shape[3:])

    q = chunks(q).astype(f32)
    k = chunks(k).astype(f32) * (DH ** -0.5)
    v = chunks(v).astype(f32)
    ig = chunks(i_pre).astype(f32)
    lf = jax.nn.log_sigmoid(chunks(f_pre).astype(f32))
    b = jnp.cumsum(lf, axis=-1)
    g = b[..., -1]
    a = g[..., None] - b + ig
    m_loc = jnp.max(a, axis=-1)
    w = jnp.exp(a - m_loc[..., None])
    kv_c = jnp.einsum('bhcl,bhcld,bhcle->bhcde', w, k, v)
    n_c = jnp.einsum('bhcl,bhcld->bhcd', w, k)

    def step(carry, xs):
        C, n, m = carry
        kv_j, n_j, m_j, g_j = xs
        m_new = jnp.maximum(g_j + m, m_j)
        a_old = jnp.exp(g_j + m - m_new)
        a_new = jnp.exp(m_j - m_new)
        C_new = a_old[..., None, None] * C + a_new[..., None, None] * kv_j
        n_new = a_old[..., None] * n + a_new[..., None] * n_j
        return (C_new, n_new, m_new), (C, n, m)

    init = (jnp.zeros((B, NH, DH, DH), f32), jnp.zeros((B, NH, DH), f32), jnp.zeros((B, NH), f32))
    xs = (jnp.moveaxis(kv_c, 2, 0), jnp.moveaxis(n_c, 2, 0), jnp.moveaxis(m_loc, 2, 0), jnp.moveaxis(g, 2, 0))
    _, (C_prev, n_prev, m_prev) = lax.scan(step, init, xs)
    C_prev = jnp.moveaxis(C_prev, 0, 2)
    n_prev = jnp.moveaxis(n_prev, 0, 2)
    m_prev = jnp.moveaxis(m_prev, 0, 2)
    causal = jnp.tril(jnp.ones((L, L), dtype=bool))
    dlog = jnp.where(causal, b[..., :, None] - b[..., None, :] + ig[..., None, :], -jnp.inf)
    inter = b + m_prev[..., None]
    m_t = jnp.maximum(inter, jnp.max(dlog, axis=-1))
    wts = jnp.exp(dlog - m_t[..., None]) * jnp.einsum('bhcld,bhcsd->bhcls', q, k)
    dec = jnp.exp(inter - m_t)
    num = jnp.einsum('bhcls,bhcse->bhcle', wts, v) + dec[..., None] * jnp.einsum('bhcld,bhcde->bhcle', q, C_prev)
    den = jnp.sum(wts, axis=-1) + dec * jnp.einsum('bhcld,bhcd->bhcl', q, n_prev)
    h = num / jnp.maximum(jnp.abs(den), jnp.exp(-m_t))[..., None]
    return jnp.moveaxis(h.reshape(B, NH, S, DH), 1, 2)

def mlstm_mixer(q_pre, k_pre, v, o_pre, i_pre, f_pre, conv_w, gate_b, head_norm_w):
    B, S, _ = q_pre.shape
    qk = jax.nn.silu(causal_conv(jnp.concatenate([q_pre, k_pre], axis=-1), conv_w))
    q, k = qk[..., :M_WIDTH], qk[..., M_WIDTH:]
    shp = (B, S, M_HEADS, M_HEAD_DIM)
    h = mlstm_chunkwise(q.reshape(shp), k.reshape(shp), v.reshape(shp), i_pre + gate_b[:M_HEADS], f_pre + gate_b[M_HEADS:])
    h = rms_norm(h, head_norm_w.reshape(M_HEADS, M_HEAD_DIM)).reshape(B, S, M_WIDTH)
    return (jax.nn.sigmoid(o_pre.astype(jnp.float32)) * h).astype(q_pre.dtype)

def masked_softmax(s, mask):
    s = jnp.where(mask, s.astype(jnp.float32), -jnp.inf)
    m = jnp.max(s, axis=-1, keepdims=True)
    m = jnp.where(jnp.isfinite(m), m, 0.0)
    p = jnp.exp(s - m)
    return p / jnp.maximum(jnp.sum(p, axis=-1, keepdims=True), 1e-30)

def compress_kv(t, pe, w1, w2):
    B, S, G, Dh = t.shape
    n_cmp = (S - CMP_BLOCK) // CMP_STRIDE + 1
    idx = jnp.arange(n_cmp)[:, None] * CMP_STRIDE + jnp.arange(CMP_BLOCK)[None, :]
    blk = t[:, idx] + pe[None, None, :, None, :]
    blk = jnp.moveaxis(blk, 3, 2).reshape(B, n_cmp, G, CMP_BLOCK * Dh)
    return jax.nn.silu(blk @ w1) @ w2

def nsa_attention(q, k_cmp, v_cmp, k_slc, v_slc, k_win, v_win, gates):
    B, S, H, Dh = q.shape
    G = k_slc.shape[2]
    HPG = H // G
    QB = NSA_Q_BLOCK
    scale = Dh ** -0.5
    n_cmp = k_cmp.shape[1]
    n_slc = S // SLC_BLOCK
    n_top = min(SLC_TOPK, n_slc)
    cmp_end = jnp.arange(n_cmp) * CMP_STRIDE + CMP_BLOCK - 1
    js = np.arange(n_slc)[:, None] * SLC_BLOCK
    cs = np.arange(n_cmp)[None, :] * CMP_STRIDE
    ov = np.clip(np.minimum(js + SLC_BLOCK, cs + CMP_BLOCK) - np.maximum(js, cs), 0, None) / CMP_STRIDE
    ov = jnp.asarray(ov.astype(np.float32))
    ks_blk = k_slc.reshape(B, n_slc, SLC_BLOCK, G, Dh).transpose(0, 3, 1, 2, 4)
    vs_blk = v_slc.reshape(B, n_slc, SLC_BLOCK, G, Dh).transpose(0, 3, 1, 2, 4)
    kw_pad = jnp.pad(k_win, ((0, 0), (WINDOW, 0), (0, 0), (0, 0)))
    vw_pad = jnp.pad(v_win, ((0, 0), (WINDOW, 0), (0, 0), (0, 0)))
    b_idx = jnp.arange(B)[:, None, None, None]
    g_idx = jnp.arange(G)[None, :, None, None]
    j_ids = jnp.arange(n_slc)
    slc_start = j_ids * SLC_BLOCK
    n_qb = S // QB

    def block(args):
        qb, gb, q0 = args
        t = q0 + jnp.arange(QB)
        qg = qb.reshape(B, QB, G, HPG, Dh)
        s = jnp.einsum('bqghd,bngd->bqghn', qg, k_cmp) * scale
        p_c = masked_softmax(s, (cmp_end[None, :] <= t[:, None])[None, :, None, None, :])
        o_c = jnp.einsum('bqghn,bngd->bqghd', p_c.astype(v_cmp.dtype), v_cmp)
        imp = jnp.einsum('bqghn,jn->bqgj', p_c, ov)
        cur = t // SLC_BLOCK
        forced = (j_ids[None, :] == 0) | (j_ids[None, :] == cur[:, None]) | (j_ids[None, :] == cur[:, None] - 1)
        future = slc_start[None, :] > t[:, None]
        score = jnp.where(forced[None, :, None, :], jnp.inf, jnp.where(future[None, :, None, :], -jnp.inf, imp))
        _, sel = lax.top_k(score, n_top)
        sel = sel.transpose(0, 2, 1, 3)
        kg = ks_blk[b_idx, g_idx, sel].reshape(B, G, QB, n_top * SLC_BLOCK, Dh)
        vg = vs_blk[b_idx, g_idx, sel].reshape(B, G, QB, n_top * SLC_BLOCK, Dh)
        kpos = (sel[..., None] * SLC_BLOCK + jnp.arange(SLC_BLOCK)).reshape(B, G, QB, n_top * SLC_BLOCK)
        m_s = (kpos <= t[None, None, :, None]).transpose(0, 2, 1, 3)[:, :, :, None, :]
        s = jnp.einsum('bqghd,bgqkd->bqghk', qg, kg) * scale
        p_s = masked_softmax(s, m_s)
        o_s = jnp.einsum('bqghk,bgqkd->bqghd', p_s.astype(vg.dtype), vg)
        kw = lax.dynamic_slice_in_dim(kw_pad, q0, WINDOW + QB, axis=1)
        vw = lax.dynamic_slice_in_dim(vw_pad, q0, WINDOW + QB, axis=1)
        wpos = q0 - WINDOW + jnp.arange(WINDOW + QB)
        m_w = (wpos[None, :] <= t[:, None]) & (wpos[None, :] > t[:, None] - WINDOW) & (wpos[None, :] >= 0)
        s = jnp.einsum('bqghd,bkgd->bqghk', qg, kw) * scale
        p_w = masked_softmax(s, m_w[None, :, None, None, :])
        o_w = jnp.einsum('bqghk,bkgd->bqghd', p_w.astype(vw.dtype), vw)
        gb = gb.reshape(B, QB, G, HPG, 3)
        o = gb[..., 0:1] * o_c + gb[..., 1:2] * o_s + gb[..., 2:3] * o_w
        return o.reshape(B, QB, H * Dh)

    qs = q.reshape(B, n_qb, QB, H, Dh).swapaxes(0, 1)
    gs = gates.reshape(B, n_qb, QB, H, 3).swapaxes(0, 1)
    q0s = jnp.arange(n_qb, dtype=jnp.int32) * QB
    out = lax.map(block, (qs, gs, q0s))
    return out.swapaxes(0, 1).reshape(B, S, H * Dh)

def grouped_expert_ffn(hf, eidx, gate, w1, w3, w2):
    T, D = hf.shape
    E = w1.shape[0]
    R = MOE_ROW_BLOCK
    A = eidx.shape[0] * eidx.shape[1]
    e = eidx.reshape(A)
    g = gate.reshape(A)
    tok = jnp.repeat(jnp.arange(T, dtype=jnp.int32), eidx.shape[1])
    order = jnp.argsort(e)
    e_s, g_s, tok_s = e[order], g[order], tok[order]
    counts = jnp.zeros((E,), jnp.int32).at[e].add(1)
    padded = (counts + R - 1) // R * R
    starts = jnp.cumsum(counts) - counts
    pstarts = jnp.cumsum(padded) - padded
    dest = pstarts[e_s] + jnp.arange(A, dtype=jnp.int32) - starts[e_s]
    P = -(-A // R) * R + E * R
    row_tok = jnp.zeros((P,), jnp.int32).at[dest].set(tok_s)
    row_gate = jnp.zeros((P,), hf.dtype).at[dest].set(g_s)
    block_start = jnp.arange(P // R, dtype=jnp.int32) * R
    block_e = jnp.minimum(jnp.sum(block_start[:, None] >= (pstarts + padded)[None, :], axis=1), E - 1)

    def run_block(args):
        toks, gts, ei = args
        xb = hf[toks]
        hb = jax.nn.silu(xb @ w1[ei]) * (xb @ w3[ei])
        return (hb @ w2[ei]) * gts[:, None]

    ys = lax.map(run_block, (row_tok.reshape(-1, R), row_gate.reshape(-1, R), block_e))
    return jax.ops.segment_sum(ys.reshape(P, D), row_tok, num_segments=T)

def hier_moe(h, wg, bg, we, be, w1, w3, w2):
    B, S, D = h.shape
    T = B * S
    hf = h.reshape(T, D)
    p_grp = jax.nn.softmax((hf @ wg + bg).astype(jnp.float32), axis=-1)
    pg_top, grp = lax.top_k(p_grp, 1)
    grp = grp[:, 0]
    le = (hf @ we + be).astype(jnp.float32).reshape(T, MOE_GROUPS, EXPERTS_PER_GROUP)
    p_in = jax.nn.softmax(le[jnp.arange(T), grp], axis=-1)
    pe_top, e_in = lax.top_k(p_in, TOP_K_IN_GROUP)
    gate = pg_top * pe_top / jnp.sum(pe_top, axis=-1, keepdims=True)
    eidx = grp[:, None] * EXPERTS_PER_GROUP + e_in
    y = grouped_expert_ffn(hf, eidx, gate.astype(h.dtype), w1, w3, w2)
    return y.reshape(B, S, D)

def setup_inputs(seed: int = 0) -> dict:
    key = jax.random.key(seed)
    ks = jax.random.split(key, 32)
    f32 = jnp.float32
    L = DEPTH
    D = D_MODEL

    def nrm(k, shape, scale):
        return jax.random.normal(k, shape, f32) * scale

    f_bias = jnp.linspace(3.0, 6.0, M_HEADS, dtype=f32)
    return {
        'x': nrm(ks[0], (BATCH, SEQ, D), 1.0),
        'c': nrm(ks[1], (BATCH, D), 1.0),
        'positions': jnp.arange(SEQ, dtype=jnp.int32)[None, :] + jax.random.randint(ks[2], (BATCH, 1), 0, 1024, dtype=jnp.int32),
        'ada_w': nrm(ks[3], (L, D, 6 * D), 0.5 * D ** -0.5),
        'ada_b': nrm(ks[4], (L, 6 * D), 0.1),
        'norm_mix_pre': 1.0 + nrm(ks[5], (L, D), 0.05),
        'norm_mix_post': 1.0 + nrm(ks[6], (L, D), 0.05),
        'norm_ffn_pre': 1.0 + nrm(ks[7], (L, D), 0.05),
        'norm_ffn_post': 1.0 + nrm(ks[8], (L, D), 0.05),
        'w_in': nrm(ks[9], (L, D, IN_WIDTH), D ** -0.5),
        'mlstm_conv_w': nrm(ks[10], (L, M_CONV, 2 * M_WIDTH), M_CONV ** -0.5),
        'mlstm_gate_b': jnp.concatenate([nrm(ks[11], (L, M_HEADS), 0.1), f_bias[None, :] + nrm(ks[12], (L, M_HEADS), 0.1)], axis=-1),
        'mlstm_head_norm': 1.0 + nrm(ks[13], (L, M_WIDTH), 0.05),
        'cmp_pe_k': nrm(ks[14], (L, CMP_BLOCK, N_HEAD_DIM), 0.1),
        'cmp_w1_k': nrm(ks[15], (L, CMP_BLOCK * N_HEAD_DIM, CMP_HIDDEN), (CMP_BLOCK * N_HEAD_DIM) ** -0.5),
        'cmp_w2_k': nrm(ks[16], (L, CMP_HIDDEN, N_HEAD_DIM), CMP_HIDDEN ** -0.5),
        'cmp_pe_v': nrm(ks[17], (L, CMP_BLOCK, N_HEAD_DIM), 0.1),
        'cmp_w1_v': nrm(ks[18], (L, CMP_BLOCK * N_HEAD_DIM, CMP_HIDDEN), (CMP_BLOCK * N_HEAD_DIM) ** -0.5),
        'cmp_w2_v': nrm(ks[19], (L, CMP_HIDDEN, N_HEAD_DIM), CMP_HIDDEN ** -0.5),
        'w_out': nrm(ks[20], (L, D, D), D ** -0.5),
        'router_grp_w': nrm(ks[21], (L, D, MOE_GROUPS), D ** -0.5),
        'router_grp_b': nrm(ks[22], (L, MOE_GROUPS), 0.01),
        'router_exp_w': nrm(ks[23], (L, D, N_EXPERTS), D ** -0.5),
        'router_exp_b': nrm(ks[24], (L, N_EXPERTS), 0.01),
        'expert_w1': nrm(ks[25], (L, N_EXPERTS, D, EXPERT_FF), D ** -0.5),
        'expert_w3': nrm(ks[26], (L, N_EXPERTS, D, EXPERT_FF), D ** -0.5),
        'expert_w2': nrm(ks[27], (L, N_EXPERTS, EXPERT_FF, D), EXPERT_FF ** -0.5),
    }

def reference(x, c, positions, ada_w, ada_b, norm_mix_pre, norm_mix_post, norm_ffn_pre, norm_ffn_post, w_in, mlstm_conv_w, mlstm_gate_b, mlstm_head_norm, cmp_pe_k, cmp_w1_k, cmp_w2_k, cmp_pe_v, cmp_w1_v, cmp_w2_v, w_out, router_grp_w, router_grp_b, router_exp_w, router_exp_b, expert_w1, expert_w3, expert_w2):
    B, S, D = x.shape
    G, Dh = N_KV_GROUPS, N_HEAD_DIM

    def as_kv(t):
        return t.reshape(B, S, G, Dh)

    for l in range(DEPTH):
        mod = jax.nn.silu(c) @ ada_w[l] + ada_b[l]
        sh_m, sc_m, g_m, sh_f, sc_f, g_f = jnp.split(mod[:, None, :], 6, axis=-1)
        h = rms_norm(x, norm_mix_pre[l]) * (1.0 + sc_m) + sh_m
        (mq, mk, mv, mo, mi, mf, nq, kc, vc, ksl, vsl, kwn, vwn, ng) = split_cols(h @ w_in[l], IN_WIDTHS)
        y_m = mlstm_mixer(mq, mk, mv, mo, mi, mf, mlstm_conv_w[l], mlstm_gate_b[l], mlstm_head_norm[l])
        q = rope(nq.reshape(B, S, N_HEADS, Dh), positions)
        k_c = compress_kv(rope(as_kv(kc), positions), cmp_pe_k[l], cmp_w1_k[l], cmp_w2_k[l])
        v_c = compress_kv(as_kv(vc), cmp_pe_v[l], cmp_w1_v[l], cmp_w2_v[l])
        y_n = nsa_attention(q, k_c, v_c, rope(as_kv(ksl), positions), as_kv(vsl), rope(as_kv(kwn), positions), as_kv(vwn), jax.nn.sigmoid(ng.reshape(B, S, N_HEADS, 3)))
        y = jnp.concatenate([y_m, y_n], axis=-1) @ w_out[l]
        x = x + g_m * rms_norm(y, norm_mix_post[l])
        h = rms_norm(x, norm_ffn_pre[l]) * (1.0 + sc_f) + sh_f
        y = hier_moe(h, router_grp_w[l], router_grp_b[l], router_exp_w[l], router_exp_b[l], expert_w1[l], expert_w3[l], expert_w2[l])
        x = x + g_f * rms_norm(y, norm_ffn_post[l])
    return x


_drawn_inputs = setup_inputs


def setup_inputs(seed=0):
    import zlib

    import numpy as np

    out = dict(_drawn_inputs(seed))
    spreads = {}
    factors = {'norm_ffn_post': 4.078, 'cmp_pe_k': 5.809, 'router_exp_b': 2.739}
    for name, (base, spread) in spreads.items():
        noise = np.random.default_rng([zlib.crc32(name.encode()), seed]).standard_normal(out[name].shape)
        drawn = base * np.exp(spread * noise) if base else spread * noise
        out[name] = __import__('jax').numpy.asarray(drawn.astype(out[name].dtype))
    for name, factor in factors.items():
        out[name] = (out[name] * factor).astype(out[name].dtype)
    return out
```

```python
from contextlib import ExitStack

import numpy as np
import concourse.bass as bass
from concourse import mybir

F32 = mybir.dt.float32
I32 = mybir.dt.int32
ALU = mybir.AluOpType
ACT = mybir.ActivationFunctionType
AX = mybir.AxisListType

P = 128
S = D = 1024
NT = S // P
KT = D // P
CH = S // 512
HD = 64
NH = 8
MH = 4
MW = 512
NEG = -1e30
EPS = 1e-6
NCMP = 63
NE = 32
NOV = 15
FF = 512
OFF = dict(mq=0, mk=512, mv=1024, mo=1536, mi=2048, nq=2056, kc=2568, kwn=3080, ng=3336)

HT = 0
COS, SIN = 8192, 9216
CONV = 10240
MKT = 12294
V1 = MKT + 4096
RING2 = V1 + 4128
RING0 = RING2 + 4096
QT = RING0 + 8192
KSL, KWN, KCT, VCT = QT + 4096, QT + 5120, QT + 6144, QT + 7168
VV = QT + 8192
MQT = VV + 2048
YM = MQT + 4096
SMALL = YM + 4096
WORDS = 53200
W0, W1 = 0, MKT
MH_SCALE = float(np.float32(P ** -0.5))
TWO_PI = 2 * np.pi
PI2_MID = float(np.round((TWO_PI - 6.28125) * 2 ** 21) / 2 ** 21)
PI2 = (6.28125, PI2_MID, TWO_PI - 6.28125 - PI2_MID)
PI_IN = 3.1415925
ROUND = 1.5 * 2 ** 23
XN = MQT


def job_list():
    jobs = ["vec"] + [("ada", i) for i in range(4)]
    jobs += [("hT", c, k) for c in range(CH) for k in range(KT)]
    jobs += ["gates"] + [("q", j, c) for j in range(4) for c in range(CH)]
    jobs += ["gT"]
    jobs += [(n, c) for n in ("kc", "ksl", "vc", "vsl") for c in range(CH)]
    jobs += [(n, c) for n in ("kwn", "vwn") for c in range(CH)]
    jobs += ["gcol"]
    jobs += [("mq", j, c) for j in range(4) for c in range(CH)]
    jobs += [("mk", j, c) for j in range(4) for c in range(CH)]
    jobs += [("mv", t) for t in range(NT)] + [("mo", t) for t in range(NT)]
    jobs += [("ada", i) for i in range(4, 12)]
    jobs += [("chid", a, g) for a in range(2) for g in range(2)] + ["kcmp", "vcmp"]
    for c in range(NT):
        jobs += [("S", c), ("kr", c)] + [(n, c, p) for n in ("num", "int", "kv") for p in range(2)]
    jobs += [("row", i, n) for i in range(2) for n in range(2)]
    jobs += [("yT", 0, 0), ("yT", 0, 1)]
    for t in range(NT):
        jobs += [("yT", t + 1, n) for n in range(2) if t + 1 < NT] + [("out", t, n) for n in range(2)]
        jobs += [j for j in (("xT2", t - 1, 0), ("xT2", t - 1, 1), ("lg", t - 1)) if t]
    jobs += [("xT2", NT - 1, 0), ("xT2", NT - 1, 1), ("lg", NT - 1), "rank"]
    return {n: i for i, n in enumerate(jobs)}


def ring_items(d):
    w_in = d["w_in"].rearrange("(k p) n -> p k n", p=P)
    ada = d["ada_w"].rearrange("(k p) n -> p k n", p=P)
    w_out = d["w_out"].rearrange("(k p) n -> p k n", p=P)
    items = [[(0, 0, ada[:, :, 512 * i:512 * i + 512])] for i in range(4)]
    for n, w in (("nq", 512), ("kc", 512), ("kwn", 256), ("mq", 512), ("mk", 512), ("mv", 512), ("mo", 512)):
        if n == "nq":
            items.append([(P * j + HD * g, 0, w_in[:, :, OFF[n] + HD * (4 * g + j):OFF[n] + HD * (4 * g + j + 1)])
                          for j in range(4) for g in range(2)])
        else:
            items.append([(0, 0, w_in[:, :, OFF[n]:OFF[n] + w])])
    items += [[(0, 0, ada[:, :, 512 * i:512 * i + 512])] for i in range(4, 12)]
    for n in ("cmp_w1_k", "cmp_w1_v"):
        src = d[n].rearrange("(p d) n -> d p n", d=HD)
        items.append([(0, 0, src), (0, HD, src)])
    items += [[(0, 0, w_out[:, :, 512 * i:512 * i + 512])] for i in range(2)]
    return items


IT_NQ, IT_KC, IT_KWN, IT_MQ, IT_MK, IT_MV, IT_MO, IT_ADA2, IT_CMP, IT_WOUT = 4, 5, 6, 7, 8, 9, 10, 11, 19, 21


def build(nc, d, out):
    JOB = job_list()
    ITEMS = ring_items(d)
    with ExitStack() as ctx:
        def sem(name):
            return ctx.enter_context(nc.semaphore(name))

        arena = ctx.enter_context(nc.sbuf_tensor("arena", [P, WORDS], F32))
        ps = ctx.enter_context(nc.psum_tensor("ps", [P, 8, 512], F32))

        def view(at, *shape, parts=P):
            n = int(np.prod(shape))
            v = arena[0:parts, at:at + n]
            if len(shape) == 2:
                v = v.rearrange("p (a b) -> p a b", b=shape[1])
            if len(shape) == 3:
                v = v.rearrange("p (a b c) -> p a b c", b=shape[1], c=shape[2])
            return v

        small = [SMALL]

        def tiny(*shape, parts=P, dt=F32):
            at = small[0]
            small[0] += int(np.prod(shape))
            assert small[0] <= WORDS
            v = view(at, *shape, parts=parts)
            return v if dt is F32 else v.bitcast(dt)

        hT = view(HT, KT, S)
        cos, sin = view(COS, S), view(SIN, S)
        conv_raw = view(CONV, 2, S + 3)
        mkT, mqT = view(MKT, MH, S), view(MQT, MH, S)
        v1 = view(V1, NT, MH, P + 1)
        ring = [view(RING0, KT, 512), view(RING0 + 4096, KT, 512), view(RING2, KT, 512)]
        qT = view(QT, 4, S)
        kslT, kwnT, kcT, vcT = view(KSL, S), view(KWN, S), view(KCT, S), view(VCT, S)
        vv = view(VV, NT, 4 * HD)
        yn, ym = view(MQT, NT, MW), view(YM, NT, MW)
        xn = view(XN, NT, D)
        junk = view(V1, 2, D)
        swap = view(V1, 2, 512)
        turned = view(V1 + 1024, 2, 512)
        sc_ = [view(YM + P * i, P, parts=32) for i in range(12)]
        g_i, g_f, decay_b, u_, cmax, mx, dec_, em_, wp_, neg_mx, t_a, ones_r = sc_
        gi_cols, gf_cols = view(YM + 12 * P, MH, NT), view(YM + 12 * P + 32, MH, NT)
        gall = view(YM + 13 * P, NT, 32)
        abs_f = view(YM + 15 * P, P, parts=32)
        bc = view(HT, MH, NT, P)
        at = [4096]

        def temp(*shape):
            v = view(at[0], *shape)
            at[0] += int(np.prod(shape))
            assert at[0] <= MKT
            return v

        wts, kw = [temp(MH, P) for _ in range(2)], [temp(MH, P) for _ in range(2)]
        num, hh, sq = [temp(MH, P + 1) for _ in range(2)], temp(MH, P), temp(MH, P)
        state = temp(MH, P + 1)

        ident = tiny(P)
        causal = tiny(P)
        behind = tiny(P)
        cmask = tiny(NT, NCMP)
        cols = tiny(124)
        mod = tiny(48)
        scale1, shift1, scale2, shift2 = (tiny(KT) for _ in range(4))
        sc_col = tiny(KT)
        sum_sq, rstd = tiny(NT), tiny(NT)
        wg = view(V1 + 2304, KT, 32)
        gate_b = tiny(8)
        sgate = tiny(NT, 24)
        gcols = tiny(4, 32)
        a_old = tiny(32)
        k_cmp = tiny(64)
        v_cmp = tiny(2, HD)
        w2c = tiny(2, HD)
        pe_cols = tiny(2, 32)
        hbias = tiny(2, 2)
        freq = tiny(2)
        gm_col = tiny(2, KT)
        den, ssq4, rs4 = tiny(MH), tiny(MH), tiny(MH)
        nmax = tiny(4)
        sums = tiny(4, 3)
        rsum = tiny(3)
        hop = tiny(2, parts=32)
        hop2 = tiny(3, parts=32)
        hop4 = tiny(8, 2, parts=4)
        hop5 = tiny(8, 2, parts=4)
        gm32 = tiny(1, parts=32)
        vec = view(V1 + 2048, P, parts=124)
        hid = temp(2, 2, 64)
        pos_i, pos_f, ang, turns = view(MKT, S).bitcast(I32), view(MKT + S, S), view(MKT + 2 * S, S), view(MKT + 3 * S, S)

        d_hop = nc.dram_tensor("d_hop", (32, 2), F32).ap()
        d_hop2 = nc.dram_tensor("d_hop2", (32, 2), F32).ap()
        d_nmx = nc.dram_tensor("d_nmx", (32, P), F32).ap()
        d_old = nc.dram_tensor("d_old", (32, 1), F32).ap()

        psum_ready = sem("psum_ready")
        bank_read = [sem(f"bank_read{i}") for i in range(8)]
        ring_in = [sem(f"ring_in{i}") for i in range(3)]
        ring_used = sem("ring_used")
        vec_in, x_in, const_in = sem("vec_in"), [sem(f"x_in{t}") for t in range(NT)], sem("const_in")
        wg_in = sem("wg_in")
        pool_const = sem("pool_const")
        sq_done, norm_ms, norm_sqrt, xn_done = sem("sq_done"), sem("norm_ms"), sem("norm_sqrt"), sem("xn_done")
        mod_ready = sem("mod_ready")
        silu_c = sem("silu_c")
        angle, trig = sem("angle"), sem("trig")
        swapped, roped = sem("swapped"), sem("roped")
        raw_ready, conv_done = sem("raw_ready"), sem("conv_done")
        gates_in_cols, gates_scanned = sem("gates_in_cols"), sem("gates_scanned")
        exp_f, ln_f = sem("exp_f"), sem("ln_f")
        exp_in, exp_out = sem("exp_in"), sem("exp_out")
        hop_out, hop_in = sem("hop_out"), sem("hop_in")
        sg_done = sem("sg_done")
        act_step, dve_step, pool_step = sem("act_step"), sem("dve_step"), sem("pool_step")
        stage_end = [sem(f"stage_end{c}") for c in "ABCDE"]
        hbias_ready, hid_ready = sem("hbias_ready"), sem("hid_ready")
        decay_in, decay_masked, decay_exp = sem("decay_in"), sem("decay_masked"), sem("decay_exp")
        wts_ready, h_ms, h_sqrt, state_zero = sem("wts_ready"), sem("h_ms"), sem("h_sqrt"), sem("state_zero")
        out_done = sem("out_done")

        small[0] = SMALL + 3 * P
        late_end = small[0] + NT * NCMP
        NU = NT * NH * 3
        probs = [view(MKT + S * i, S) for i in range(2)]
        probs_T = [view(MKT + 2 * S + 512 * i, 512) for i in range(2)]
        branches = view(MKT + 3 * S, 3, HD)
        zero_row = view(MKT + 4 * S, D)
        ones_sq, upper = view(MKT + 9472, P), view(MKT + 9600, P)
        E0 = MKT
        xt = [view(E0 + D * i, D) for i in range(2)]
        yT = [view(E0 + D * (2 + i), KT, P) for i in range(2)]
        y_row, junk_e = view(E0 + 4 * D, D), view(E0 + 5 * D, D)
        xn2 = [view(E0 + D * (6 + i), D) for i in range(2)]
        h2T = view(E0 + 8 * D, KT, P)
        logits = view(MKT + 9728, NT, 36)
        w_router = view(MKT + 10016, KT, 36)
        b_router = view(MKT + 10304, 36)
        zeros48 = view(MKT + 10340, 48).bitcast(I32)
        iota32, iota8, iota4 = view(MKT + 10388, NE), view(MKT + 10420, 8), view(MKT + 10428, 4)
        iota8m, iota4m = view(MKT + 10432, 8), view(MKT + 10440, 4)
        iota15 = view(MKT + 10444, NOV)
        tok_id = view(MKT + 10460, NT).bitcast(I32)
        x2 = view(QT, NT, D)
        gm_row, gf_row = view(VV, D), view(VV + D, D)
        diag = [yT[0], yT[1]]
        ys, rs_y, xs_, rs_x = tiny(1), tiny(1), tiny(1), tiny(1)
        gates2 = tiny(2, NT)
        dest = tiny(2, NT, dt=I32)
        slot = tiny(2, NT, dt=I32)
        row_tok = tiny(48, dt=I32)
        block_tab = tiny(64, parts=1, dt=I32)
        ra = [YM]

        def route(*shape, dt=F32):
            v = view(ra[0], *shape)
            ra[0] += int(np.prod(shape))
            assert ra[0] <= SMALL
            return v if dt is F32 else v.bitcast(dt)

        mg, sg_, ig, m1, i1, m2, i2, e2 = (route(NT) for _ in range(8))
        dg, eqg, ohg = route(NT, 4), route(NT, 4), route(NT, 4)
        lin, eqe, cand, oh1, oh2 = (route(NT, 8) for _ in range(5))
        prod = route(NT, 4, 8)
        hot = [route(NT, 4, 8) for _ in range(2)]
        hots, before, prefix, rank = route(NT, NE), route(NT, NE), route(NT, NE), route(NT, NE)
        total, over, over_inc, off_e, ones32 = (route(NE) for _ in range(5))
        rk, ex, ofs, big = route(2, NT), route(2, NT), route(2, NT), route(2, NT)
        ov_cmp = route(NOV, NE)
        tabf = route(64)
        laneslot = route(2, NT, dt=I32)
        w13 = [[view(W + 4096 * n, KT, FF) for n in range(2)] for W in (W0, W1)]
        w2s = [view(W + 8192, 4, D) for W in (W0, W1)]
        xg = [view(RING0 + D * i, D) for i in range(2)]
        xgT = [view(RING0 + D * (2 + i), KT, P) for i in range(2)]
        yo = [view(RING0 + D * (4 + i), D) for i in range(2)]
        act1 = [view(RING0 + D * 6 + 512 * i, 4, P) for i in range(2)]
        hid_e = [view(RING0 + D * 7 + 512 * i, 4, P) for i in range(2)]
        idx_col = [tiny(1, dt=I32) for _ in range(2)]
        assert small[0] <= late_end
        y1 = [view(W0 + D * i, D) for i in range(2)]
        y2 = [view(W0 + D * (2 + i), D) for i in range(2)]
        junk_g = view(W0 + 4 * D, D)
        NB = 48
        d_xn = nc.dram_tensor("d_xn", (S, D), F32).ap()
        d_rt = nc.dram_tensor("d_rt", (P * NB, 1), I32).ap()
        d_y = nc.dram_tensor("d_y", (NB * P, D), F32).ap()

        scores_ready, row_max, probs_ready = sem("scores_ready"), sem("row_max"), sem("probs_ready")
        turned_ready, turned_read = sem("turned_ready"), [sem(f"turned_read{i}") for i in range(2)]
        pv_done, out_read = sem("pv_done"), sem("out_read")
        wout_scaled, pool_e, router_in, xt_in = sem("wout_scaled"), sem("pool_e"), sem("router_in"), [sem(f"xt_in{i}") for i in range(2)]
        diag_ready = sem("diag_ready")
        y_copied, y_sq, y_ms, y_sqrt, x2_done = sem("y_copied"), sem("y_sq"), sem("y_ms"), sem("y_sqrt"), sem("x2_done")
        x_sq, x_ms, x_sqrt, xn2_done = sem("x_sq"), sem("x_ms"), sem("x_sqrt"), sem("xn2_done")
        xn_stored = [sem(f"xn_stored{i}") for i in range(2)]
        x2T_read = sem("x2T_read")
        exp_args, exps_done, hots_ready, dest_ready = sem("exp_args"), sem("exps_done"), sem("hots_ready"), sem("dest_ready")
        rt_zeroed, rt_scattered, rt_in = sem("rt_zeroed"), sem("rt_scattered"), sem("rt_in")
        w13_in = [sem(f"w13_in{i}") for i in range(2)]
        w2_in = [sem(f"w2_in{i}") for i in range(2)]
        idx_ready = [sem(f"idx_ready{i}") for i in range(2)]
        xg_in = [sem(f"xg_in{i}") for i in range(2)]
        xg_turned = [sem(f"xg_turned{i}") for i in range(2)]
        xgT_act, xgT_dve = [sem(f"xgT_act{i}") for i in range(2)], [sem(f"xgT_dve{i}") for i in range(2)]
        up_part, silu_part, hid_part = ([sem(f"{n}{i}") for i in range(2)] for n in ("up_part", "silu_part", "hid_part"))
        down_done = [sem(f"down_done{i}") for i in range(2)]
        yo_act, yo_dve = [sem(f"yo_act{i}") for i in range(2)], [sem(f"yo_dve{i}") for i in range(2)]
        y_stored = sem("y_stored")
        stage_f, y_zeroed = sem("stage_f"), sem("y_zeroed")
        idx_seen, store_seen = sem("idx_seen"), sem("store_seen")
        y_in = [sem(f"y_in{i}") for i in range(2)]
        g_sq, g_ms, g_sqrt, g_done = sem("g_sq"), sem("g_ms"), sem("g_sqrt"), sem("g_done")
        out_stored = [sem(f"out_stored{i}") for i in range(2)]

        def unit(u):
            t, h, br = u // 24, u // 3 % NH, u % 3
            if br == 0:
                return t, h, br, 0, 1, min(NCMP, 8 * t + 7)
            first = max(0, t - 4) if br == 2 else 0
            return t, h, br, first, t + 1 - first, P * (t + 1 - first)

        GROUPS = [0]
        for u in range(NU):
            GROUPS.append(GROUPS[-1] + (unit(u)[4] + 3) // 4)

        def scores(u):
            return ps[:, 2 * (u % 2):2 * (u % 2) + 2, :].rearrange("p a b -> p (a b)")

        def evacuate_turned(eng, copy, u, mine):
            t, h, br, first, blocks, keys = unit(u)
            for n, q in enumerate(range(GROUPS[u], GROUPS[u + 1])):
                if q % 2 != mine:
                    continue
                eng.wait_ge(turned_ready, q + 1)
                if q >= 2:
                    eng.wait_ge(pv_done, q - 1)
                w = P * min(4, blocks - 4 * n)
                rows = keys if br == 0 else P
                copy(probs_T[q % 2][0:rows, 0:w], ps[0:rows, 4 + q % 2, 0:w]).then_inc(turned_read[q % 2], 1)

        def bank(name):
            return ps[:, JOB[name] % 8, :]

        def claim(eng, name):
            j = JOB[name]
            if j >= 8:
                eng.wait_ge(bank_read[j % 8], j // 8)
            return bank(name)

        def ready(eng, name):
            eng.wait_ge(psum_ready, JOB[name] + 1)
            return bank(name)

        def read(ins, name):
            ins.then_inc(bank_read[JOB[name] % 8], 1)

        def was_read(eng, name):
            eng.wait_ge(bank_read[JOB[name] % 8], JOB[name] // 8 + 1)

        ring_total, ring_want = [0, 0, 0], []
        for i, it in enumerate(ITEMS):
            ring_total[i % 3] += 16 * len(it)
            ring_want.append(ring_total[i % 3])

        def end_stage(eng, k):
            eng.drain().then_inc(stage_end[k], 1)
            eng.wait_ge(stage_end[k], 4)

        def chain(eng, step):
            count = [0]

            def link(ins):
                count[0] += 1
                ins.then_inc(step, 1)
                eng.wait_ge(step, count[0])
            return link

        block = ctx.enter_context(nc.Block())

        last_job = [("ada", i) for i in range(4)] + [("q", 3, 1), ("vsl", 1), ("vwn", 1), ("mq", 3, 1), ("mk", 3, 1),
                                                     ("mv", NT - 1), ("mo", NT - 1)]
        last_job += [("ada", i) for i in range(4, 12)] + [("chid", 0, 1), ("chid", 1, 1)]

        @block.sync
        def _(sp):
            rows = [(0, "ada_b"), (48, "norm_mix_pre"), (56, "norm_mix_post"), (64, "norm_ffn_pre"),
                    (72, "norm_ffn_post"), (80, "c"), (88, "mlstm_head_norm")]
            for at_row, name in rows:
                src = d[name].rearrange("(r p) -> r p", p=P)
                sp.dma_start(vec[at_row:at_row + src.shape[0], :], src).then_inc(vec_in, 16)
            sp.dma_start(vec[92:124, :], d["mlstm_conv_w"].rearrange("j (r p) -> (j r) p", p=P)).then_inc(vec_in, 16)

            def load_ring(i):
                if i >= 3:
                    sp.wait_ge(psum_ready, JOB[last_job[i - 3]] + 1)
                for col, part, src in ITEMS[i]:
                    dst = ring[i % 3]
                    if i in (IT_CMP, IT_CMP + 1):
                        dst = dst.rearrange("p k n -> p (k n)").rearrange("p (k n) -> p k n", n=P)[part:part + HD]
                    sp.dma_start(dst[:, :, col:col + src.shape[2]], src).then_inc(ring_in[i % 3], 16)

            for i in range(3):
                load_ring(i)
            for t in range(NT):
                sp.dma_start(xn[:, t, :], d["x"][t * P:(t + 1) * P, :]).then_inc(x_in[t], 16)
            w_in = d["w_in"].rearrange("(k p) n -> p k n", p=P)
            with nc.allow_non_contiguous_dma(reason="small gate weights and columns, once"):
                sp.dma_start(wg[:, :, 0:8], w_in[:, :, OFF["mi"]:OFF["mi"] + 8]).then_inc(wg_in, 16)
                sp.dma_start(wg[:, :, 8:32], w_in[:, :, OFF["ng"]:OFF["ng"] + 24]).then_inc(wg_in, 16)
                for a, n in enumerate("kv"):
                    src = d["cmp_pe_" + n].rearrange("j d -> d j")
                    for half in range(2):
                        sp.dma_start(pe_cols[half * HD:(half + 1) * HD, a, :], src).then_inc(const_in, 16)
            sp.dma_start(w2c[:, 0, :], d["cmp_w2_k"]).then_inc(const_in, 16)
            sp.dma_start(w2c[:, 1, :], d["cmp_w2_v"]).then_inc(const_in, 16)
            sp.dma_start(gate_b, d["mlstm_gate_b"].broadcast_to([P, 8])).then_inc(const_in, 16)
            sp.dma_start(freq, d["rope_cols"]).then_inc(const_in, 16)
            sp.dma_start(pos_i, d["positions"].broadcast_to([P, S])).then_inc(const_in, 16)
            for i in range(3, IT_WOUT):
                load_ring(i)
            sp.wait_ge(stage_end[1], 4)
            sp.dma_start(bc, d_nmx.rearrange("r l -> (r l)").rearrange("(a n) -> a n", a=1).broadcast_to([P, 32 * P])
                         .rearrange("p (h c l) -> p h c l", h=MH, c=NT)).then_inc(decay_in, 16)
            sp.dma_start(a_old, d_old.rearrange("r a -> a r").broadcast_to([P, 32])).then_inc(decay_in, 16)
            for i in range(IT_WOUT, IT_WOUT + 2):
                load_ring(i)
            def load_expert(s, w1_, w3_, w2_):
                for n, src in enumerate((w1_, w3_)):
                    sp.dma_start(w13[s][n], src.rearrange("(k p) n -> p k n", p=P)).then_inc(w13_in[s], 16)
                sp.dma_start(w2s[s], w2_.rearrange("(k p) n -> p k n", p=P)).then_inc(w2_in[s], 16)

            sp.wait_ge(stage_end[2], 4)
            load_expert(0, d["expert_w1"][0], d["expert_w3"][0], d["expert_w2"][0])
            with nc.allow_non_contiguous_dma(reason="router weights, once"):
                sp.dma_start(w_router[:, :, 0:4], d["router_grp_w"].rearrange("(k p) n -> p k n", p=P)).then_inc(router_in, 16)
                sp.dma_start(w_router[:, :, 4:36], d["router_exp_w"].rearrange("(k p) n -> p k n", p=P)).then_inc(router_in, 16)
            sp.dma_start(b_router[:, 0:4], d["router_grp_b"].broadcast_to([P, 4])).then_inc(router_in, 16)
            sp.dma_start(b_router[:, 4:36], d["router_exp_b"].broadcast_to([P, NE])).then_inc(router_in, 16)
            sp.wait_ge(pool_e, 1)
            for b in range(NE, NB):
                sp.dma_start(d_y[b * P:(b + 1) * P, :], zero_row).then_inc(y_zeroed, 16)
            sp.dma_start(d_rt.rearrange("(p b) a -> p (b a)", p=P), zeros48).then_inc(rt_zeroed, 16)
            sp.wait_ge(stage_end[3], 4)
            for t in range(2):
                sp.dma_start(xt[t], d["x"][t * P:(t + 1) * P, :]).then_inc(xt_in[t], 16)
            for t in range(NT):
                sp.wait_ge(x2_done, t + 1)
                if t + 2 < NT:
                    sp.dma_start(xt[t % 2], d["x"][(t + 2) * P:(t + 3) * P, :]).then_inc(xt_in[t % 2], 16)
                sp.wait_ge(xn2_done, t + 1)
                sp.dma_start(d_xn[t * P:(t + 1) * P, :], xn2[t % 2]).then_inc(xn_stored[t % 2], 16)
            sp.wait_ge(stage_end[4], 4)
            load_expert(1, d["expert_w1"][1], d["expert_w3"][1], d["expert_w2"][1])
            sp_blocks = sp.value_load(block_tab[0:1, 48:49], min_val=NE, max_val=NB)
            with sp.Fori(1, NB // 2) as i:
                for s in range(2):
                    with sp.If(2 * i + s < sp_blocks):
                        e = sp.value_load(block_tab[0:1, bass.ds(2 * i + s, 1)], min_val=0, max_val=NE - 1)
                        sp.wait_ge(up_part[s], 4 * i + 1)
                        for n, name in enumerate(("expert_w1", "expert_w3")):
                            sp.dma_start(w13[s][n], d[name][bass.ds(e, 1)].rearrange("a (k p) n -> p (a k) n", p=P))\
                              .then_inc(w13_in[s], 16)
                        sp.wait_ge(down_done[s], i + 1)
                        sp.dma_start(w2s[s], d["expert_w2"][bass.ds(e, 1)].rearrange("a (k p) n -> p (a k) n", p=P))\
                          .then_inc(w2_in[s], 16)
            for t in range(NT):
                sp.wait_ge(g_done, t + 1)
                sp.dma_start(out[t * P:(t + 1) * P, :], y1[t % 2]).then_inc(out_stored[t % 2], 16)
            for s in range(2):
                sp.wait_ge(out_stored[s], 16 * NT // 2)

        @block.gpsimd
        def _(pool):
            link = chain(pool, pool_step)
            link(nc.gpsimd.memset(ident, 0.0))
            link(nc.gpsimd.affine_select(out=ident, in_=ident, compare_op=ALU.not_equal, fill=1.0, base=0,
                                         pattern=[[-1, P]], channel_multiplier=1))
            link(nc.gpsimd.memset(causal, 0.0))
            link(nc.gpsimd.affine_select(out=causal, in_=causal, compare_op=ALU.is_ge, fill=NEG, base=0,
                                         pattern=[[-1, P]], channel_multiplier=1))
            link(nc.gpsimd.memset(behind, 0.0))
            link(nc.gpsimd.affine_select(out=behind, in_=behind, compare_op=ALU.is_gt, fill=NEG, base=0,
                                         pattern=[[1, P]], channel_multiplier=-1))
            link(nc.gpsimd.memset(cmask, 0.0))
            nc.gpsimd.affine_select(out=cmask, in_=cmask, compare_op=ALU.is_ge, fill=NEG, base=-31,
                                    pattern=[[P, NT], [-16, NCMP]], channel_multiplier=1).then_inc(pool_const, 1)
            end_stage(pool, 0)
            nc.gpsimd.memset(conv_raw[:, :, 0:3], 0.0).then_inc(pool_const, 1)
            pool.wait_ge(hop_out, 1)
            with nc.allow_non_contiguous_dma(reason="64 values each"):
                pool.dma_start(d_hop, hop).then_inc(hop_in, 16)
                pool.wait_ge(hop_in, 16)
                pool.dma_start(hop4, d_hop.rearrange("(h c) a -> h c a", h=MH)).then_inc(hop_in, 16)
                pool.wait_ge(hop_out, 2)
                pool.dma_start(d_hop2.rearrange("(h c) a -> h c a", h=MH), hop5).then_inc(hop_in, 16)
                pool.wait_ge(hop_in, 48)
                pool.dma_start(hop2[:, 0:2], d_hop2).then_inc(hop_in, 16)
                pool.wait_ge(exp_out, 1)
                pool.dma_start(d_nmx, neg_mx).then_inc(hop_in, 16)
                pool.dma_start(d_old, hop2[:, 2:3]).then_inc(hop_in, 16)
                pool.wait_ge(hop_in, 96)
            pool.wait_ge(roped, 14)
            nc.gpsimd.memset(v1[:, :, :, P:P + 1], MH_SCALE)
            end_stage(pool, 1)
            nc.gpsimd.memset(state, 0.0).then_inc(state_zero, 1)
            pool.wait_ge(decay_in, 32)
            for c in range(NT):
                nc.gpsimd.affine_select(out=bc[:, :, c, :], in_=bc[:, :, c, :], compare_op=ALU.is_ge, fill=NEG, base=0,
                                        pattern=[[0, MH], [1, P]], channel_multiplier=-1).then_inc(decay_masked, 1)
            end_stage(pool, 2)
            link(nc.gpsimd.memset(zero_row, 0.0))
            nc.gpsimd.memset(zeros48, 0).then_inc(pool_e, 1)
            link(nc.gpsimd.memset(ones_sq, 1.0))
            link(nc.gpsimd.affine_select(out=upper, in_=ones_sq, compare_op=ALU.is_gt, fill=0.0, base=0,
                                         pattern=[[1, P]], channel_multiplier=-1))
            for v_, n_, b_ in ((iota32, NE, 0), (iota8, 8, 0), (iota4, 4, 0), (iota8m, 8, -64), (iota4m, 4, -64),
                               (iota15, NOV, 0)):
                nc.gpsimd.iota(v_, [[1, n_]], base=b_, channel_multiplier=0, allow_small_or_imprecise_dtypes=True)
            link(nc.gpsimd.iota(tok_id, [[P, NT]], base=0, channel_multiplier=1))
            for n in range(2):
                pool.wait_ge(ring_in[(IT_WOUT + n) % 3], ring_want[IT_WOUT + n])
                for k in range(4):
                    w = ring[(IT_WOUT + n) % 3][:, k, :]
                    nc.gpsimd.tensor_scalar(w, w, cols[:, 88 + k:89 + k], None, ALU.mult).then_inc(wout_scaled, 1)
            pool.wait_ge(y_zeroed, 16 * (NB - NE))
            end_stage(pool, 3)
            pool.wait_ge(rt_zeroed, 16)
            pool.wait_ge(dest_ready, 1)
            for k in range(2):
                for t in range(NT):
                    pool.indirect_dma_start(d_rt, bass.IndirectOffsetOnAxis(ap=slot[:, k, t:t + 1], axis=0),
                                            tok_id[:, t:t + 1], None).then_inc(rt_scattered, 16)
            pool.wait_ge(rt_scattered, 16 * 2 * NT)
            pool.dma_start(row_tok, d_rt.rearrange("(p b) a -> p (b a)", p=P)).then_inc(rt_in, 16)
            pool.wait_ge(rt_in, 16)
            for s in range(2):
                pool.wait_ge(xn_stored[s], 16 * NT // 2)
            end_stage(pool, 4)
            p_blocks = pool.value_load(block_tab[0:1, 48:49], min_val=NE, max_val=NB)
            with pool.Fori(0, NB // 2) as i:
                for s in range(2):
                    with pool.If(2 * i + s < p_blocks):
                        pool.wait_ge(xg_turned[s], i + 1)
                        nc.gpsimd.tensor_copy(idx_col[s], row_tok[:, bass.ds(2 * i + s, 1)]).then_inc(idx_ready[s], 1)
                        pool.wait_ge(idx_ready[s], i + 1)
                        pool.sem_inc(idx_seen, 1)
                        pool.indirect_dma_start(xg[s], None, d_xn,
                                                bass.IndirectOffsetOnAxis(ap=idx_col[s], axis=0)).then_inc(xg_in[s], 16)
            pool.drain().then_inc(stage_f, 1)
            pool.wait_ge(stage_f, 4)
            for t in range(NT):
                if t >= 2:
                    pool.wait_ge(out_stored[t % 2], 16 * (t // 2))
                for k, y in enumerate((y1, y2)):
                    pool.indirect_dma_start(y[t % 2], None, d_y,
                                            bass.IndirectOffsetOnAxis(ap=dest[:, k, t:t + 1], axis=0)).then_inc(y_in[t % 2], 16)

        @block.scalar
        def _(act):
            link = chain(act, act_step)
            was_read(act, "vec")
            nc.scalar.activation(sc_col, cols[:, 80:88], ACT.Silu).then_inc(silu_c, 1)
            for c in range(CH):
                for t in range(4 * c, 4 * c + 4):
                    act.wait_ge(x_in[t], 16)
                    if t >= 2:
                        act.wait_ge(sq_done, t - 1)
                    nc.scalar.activation(junk[:, t % 2, :], xn[:, t, :], ACT.Square,
                                         accum_out=sum_sq[:, t:t + 1]).then_inc(sq_done, 1)
                act.wait_ge(norm_ms, c + 1)
                nc.scalar.activation(rstd[:, 4 * c:4 * c + 4], rstd[:, 4 * c:4 * c + 4], ACT.Sqrt).then_inc(norm_sqrt, 1)
            act.wait_ge(mod_ready, 1)
            for c in range(CH):
                for k in range(1, KT, 2):
                    b = ready(act, ("hT", c, k))
                    read(nc.scalar.activation(hT[:, k, 512 * c:512 * c + 512], b, ACT.Identity,
                                              scale=scale1[:, k:k + 1], bias=mod[:, k:k + 1]), ("hT", c, k))
            end_stage(act, 0)

            act.wait_ge(angle, 1)
            nc.scalar.activation(sin, sin, ACT.Sin).then_inc(trig, 1)
            act.wait_ge(angle, 2)
            nc.scalar.activation(cos, cos, ACT.Sin).then_inc(trig, 1)
            n_rope = [0]

            def silu_conv(m):
                act.wait_ge(conv_done, m + 1)
                x_ = (mqT, mkT)[m // 4][:, m % 4, :]
                nc.scalar.activation(x_, x_, ACT.Silu)

            def exchange_halves(name, scale):
                n = n_rope[0]
                b = ready(act, name)
                if n >= 2:
                    act.wait_ge(roped, n - 1)
                for q in range(4):
                    o = q ^ 1
                    last = nc.scalar.activation(swap[32 * q:32 * q + 32, n % 2, :], b[32 * o:32 * o + 32, :], ACT.Copy,
                                                scale=scale)
                last.then_inc(swapped, 1)
                n_rope[0] += 1

            was_read(act, "gates")
            nc.scalar.activation(sgate, gall[:, :, 8:32], ACT.Sigmoid).then_inc(sg_done, 1)
            for j in range(4):
                for c in range(CH):
                    exchange_halves(("q", j, c), HD ** -0.5)
            for n in ("kc", "ksl"):
                for c in range(CH):
                    exchange_halves((n, c), 1.0)
            act.wait_ge(exp_f, 1)
            link(nc.scalar.activation(t_a, abs_f, ACT.Exp, scale=-1.0))
            nc.scalar.activation(t_a, t_a, ACT.Ln, bias=1.0).then_inc(ln_f, 1)
            for c in range(CH):
                b = ready(act, ("vc", c))
                read(nc.scalar.copy(vcT[:, 512 * c:512 * c + 512], b), ("vc", c))
            for n, at_ in (("vsl", 0), ("vwn", 128)):
                if n == "vwn":
                    for c in range(CH):
                        exchange_halves(("kwn", c), 1.0)
                for c in range(CH):
                    b = ready(act, (n, c))
                    read(nc.scalar.copy(vv[:, 4 * c:4 * c + 4, at_:at_ + P], b.rearrange("p (t n) -> p t n", n=P)), (n, c))
            act.wait_ge(exp_in, 1)
            for n, (o, i_) in enumerate(((dec_, dec_), (em_, em_), (wp_, wp_), (hop2[:, 2:3], hop2[:, 2:3]))):
                last = nc.scalar.activation(o, i_, ACT.Exp)
            last.then_inc(exp_out, 1)
            act.wait_ge(pool_const, 2)
            for i, n in enumerate(("mq", "mk")):
                dst = (mqT, mkT)[i]
                for j in range(4):
                    m = 4 * i + j
                    if m >= 2:
                        act.wait_ge(conv_done, m - 1)
                    for c in range(CH):
                        b = ready(act, (n, j, c))
                        read(nc.scalar.copy(conv_raw[:, m % 2, 3 + 512 * c:515 + 512 * c], b), (n, j, c))
                    if m >= 1:
                        silu_conv(m - 1)
            silu_conv(7)
            act.wait_ge(roped, 14)
            for t in range(NT):
                b = ready(act, ("mv", t))
                read(nc.scalar.activation(v1[:, t, :, 0:P], b.rearrange("p (h n) -> p h n", h=MH), ACT.Copy,
                                          scale=MH_SCALE), ("mv", t))
            act.wait_ge(hop_in, 96)
            for t in range(NT):
                b = ready(act, ("mo", t))
                read(nc.scalar.activation(ym[:, t, :], b, ACT.Sigmoid), ("mo", t))
            end_stage(act, 1)

            for a in range(2):
                for g in range(2):
                    act.wait_ge(hbias_ready, 2 * a + g + 1)
                    b = ready(act, ("chid", a, g))
                    read(nc.scalar.activation(hid[:, a, g, 0:NCMP], b[:, 0:NCMP], ACT.Silu,
                                              bias=hbias[:, a, g:g + 1]), ("chid", a, g))
            b = ready(act, "vcmp")
            read(nc.scalar.copy(v_cmp[0:NCMP], b[0:NCMP, 0:P].rearrange("p (g n) -> p g n", g=2)), "vcmp")
            for c in range(NT):
                act.wait_ge(decay_masked, c + 1)
                for h in range(MH):
                    last = nc.scalar.activation(bc[:, h, c, :], bc[:, h, c, :], ACT.Exp,
                                                bias=gcols[:, 0, 8 * h + c:8 * h + c + 1])
                last.then_inc(decay_exp, 1)
            for c in range(NT):
                if c >= 2:
                    act.wait_ge(h_ms, c - 1)
                for p in range(2):
                    b = ready(act, ("num", c, p))
                    read(nc.scalar.copy(num[c % 2][:, 2 * p:2 * p + 2, :],
                                        b[:, 0:2 * (P + 1)].rearrange("p (h n) -> p h n", h=2)), ("num", c, p))
                act.wait_ge(h_ms, c + 1)
                nc.scalar.activation(rs4, ssq4, ACT.Sqrt).then_inc(h_sqrt, 1)
            end_stage(act, 2)
            def exponential(u):
                t, h, br, first, blocks, keys = unit(u)
                act.wait_ge(row_max, u + 1)
                if u >= 2:
                    act.wait_ge(turned_ready, GROUPS[u - 1])
                if u // 3 >= 4:
                    act.wait_ge(out_read, u // 3 - 3)
                nc.scalar.activation(probs[u % 2][:, 0:keys], scores(u)[:, 0:keys], ACT.Exp, bias=nmax[:, u % 4:u % 4 + 1],
                                     accum_out=sums[:, u // 3 % 4, br:br + 1]).then_inc(probs_ready, 1)

            exponential(0)
            for u in range(NU):
                if u + 1 < NU:
                    exponential(u + 1)
                evacuate_turned(act, nc.scalar.copy, u, 0)
            end_stage(act, 3)

            def e_turned(t):
                b = ready(act, ("yT", t, 0))
                if t >= 2:
                    act.wait_ge(psum_ready, JOB[("out", t - 2, 1)] + 1)
                read(nc.scalar.copy(yT[t % 2][:, 0:4, :], b.rearrange("p (k n) -> p k n", n=P)), ("yT", t, 0))

            def e_router(t):
                b = ready(act, ("xT2", t, 0))
                if t >= 1:
                    act.wait_ge(psum_ready, JOB[("lg", t - 1)] + 1)
                for k in range(4):
                    last = nc.scalar.activation(h2T[:, k, :], b[:, P * k:P * k + P], ACT.Identity,
                                                scale=scale2[:, k:k + 1], bias=mod[:, 24 + k:25 + k])
                read(last, ("xT2", t, 0))

            e_turned(0)
            for t in range(NT):
                if t + 1 < NT:
                    e_turned(t + 1)
                if t:
                    act.wait_ge(x2_done, t)
                for n in range(2):
                    b = ready(act, ("out", t, n))
                    read(nc.scalar.copy(y_row[:, 512 * n:512 * n + 512], b), ("out", t, n))
                for n in range(2):
                    was_read(act, ("out", t, n))
                if t:
                    act.wait_ge(x_sq, t)
                nc.scalar.activation(junk_e, y_row, ACT.Square, accum_out=ys).then_inc(y_sq, 1)
                act.wait_ge(y_ms, t + 1)
                nc.scalar.activation(rs_y, ys, ACT.Sqrt).then_inc(y_sqrt, 1)
                act.wait_ge(x2_done, t + 1)
                act.wait_ge(y_sq, t + 1)
                nc.scalar.activation(junk_e, x2[:, t, :], ACT.Square, accum_out=xs_).then_inc(x_sq, 1)
                act.wait_ge(x_ms, t + 1)
                nc.scalar.activation(rs_x, xs_, ACT.Sqrt).then_inc(x_sqrt, 1)
                if t:
                    e_router(t - 1)
            e_router(NT - 1)
            act.wait_ge(exp_args, 1)
            nc.scalar.activation(dg, dg, ACT.Exp).then_inc(exps_done, 1)
            nc.scalar.activation(e2, e2, ACT.Exp).then_inc(exps_done, 1)
            end_stage(act, 4)

            def f_turned(s, n):
                act.wait_ge(xg_turned[s], n + 2)
                act.wait_ge(up_part[s], 4 * n + 1)
                for k in range(4):
                    last = nc.scalar.activation(xgT[s][:, k, :], ps[:, 0, P * k:P * k + P], ACT.Identity,
                                                scale=scale2[:, k:k + 1], bias=mod[:, 24 + k:25 + k])
                last.then_inc(xgT_act[s], 1)

            for s in range(2):
                act.sem_inc(yo_act[s], 1)
            a_blocks = act.value_load(block_tab[0:1, 48:49], min_val=NE, max_val=NB)
            f_turned(0, 0)
            with act.Fori(0, NB // 2) as i:
                for s in range(2):
                    with act.If(2 * i + s < a_blocks):
                        for m in range(4):
                            act.wait_ge(up_part[s], 4 * i + m + 2)
                            nc.scalar.activation(act1[s][:, m, :], ps[:, 2 + m % 2, 0:P], ACT.Silu)\
                              .then_inc(silu_part[s], 1)
                    with act.If(2 * i + s + 1 < a_blocks):
                        f_turned(1 - s, i + s)
                    with act.If(2 * i + s < a_blocks):
                        act.wait_ge(down_done[s], i + 2)
                        nc.scalar.copy(yo[s][:, 0:512], ps[:, 6, :]).then_inc(yo_act[s], 1)
                        act.wait_ge(yo_act[s], i + 2)
                        act.wait_ge(yo_dve[s], i + 2)
                        act.dma_start(d_y[bass.ds(256 * i + P * s, P), :], yo[s]).then_inc(y_stored, 16)
                        act.wait_ge(y_stored, 32 * i + 16 * s + 16)
                        act.sem_inc(store_seen, 1)
            act.drain().then_inc(stage_f, 1)
            act.wait_ge(stage_f, 4)

            for t in range(NT):
                act.wait_ge(g_ms, 2 * t + 1)
                nc.scalar.activation(junk_g, y1[t % 2], ACT.Square, accum_out=ys).then_inc(g_sq, 1)
                act.wait_ge(g_ms, 2 * t + 2)
                nc.scalar.activation(rs_y, ys, ACT.Sqrt).then_inc(g_sqrt, 1)

        @block.tensor
        def _(pe):
            def last_of(ins):
                ins.then_inc(psum_ready, 1)

            def item(i):
                pe.wait_ge(ring_in[i % 3], ring_want[i])
                return ring[i % 3]

            def modulation(i, k_item):
                w = item(k_item)
                b = claim(pe, ("ada", i))
                for m in range(4):
                    for k in range(KT):
                        last = nc.tensor.matmul(b[:, m:m + 1], w[:, k, P * m:P * m + P], sc_col[:, k:k + 1],
                                                start=(k == 0), stop=(k == KT - 1))
                last_of(last)

            pe.wait_ge(vec_in, 128)
            pe.wait_ge(pool_const, 1)
            b = claim(pe, "vec")
            last_of(nc.tensor.transpose(b[:, 0:124], vec, ident[0:124, 0:124]))
            pe.wait_ge(silu_c, 1)
            for i in range(4):
                modulation(i, i)
            for c in range(CH):
                pe.wait_ge(xn_done, 4 * c + 4)
                for k in range(KT):
                    b = claim(pe, ("hT", c, k))
                    for t in range(4):
                        last = nc.tensor.transpose(b[:, P * t:P * t + P], xn[:, 4 * c + t, P * k:P * k + P], ident)
                    last_of(last)
            end_stage(pe, 0)

            def features(name, w, c):
                b = claim(pe, name)
                for k in range(KT):
                    last = nc.tensor.matmul(b, w(k), hT[:, k, 512 * c:512 * c + 512], start=(k == 0), stop=(k == KT - 1))
                last_of(last)

            def tokens(name, w, at_col, width, tiles):
                b = claim(pe, name)
                for n, t in enumerate(tiles):
                    for k in range(KT):
                        last = nc.tensor.matmul(b[:, n * width:(n + 1) * width], hT[:, k, P * t:P * t + P],
                                                w[:, k, at_col:at_col + width], start=(k == 0), stop=(k == KT - 1))
                last_of(last)

            pe.wait_ge(wg_in, 32)
            tokens("gates", wg, 0, 32, range(NT))
            w = item(IT_NQ)
            for j in range(4):
                for c in range(CH):
                    features(("q", j, c), lambda k: w[:, k, P * j:P * j + P], c)
            pe.wait_ge(gates_in_cols, 1)
            b = claim(pe, "gT")
            nc.tensor.transpose(b[0:32, 0:P], gi_cols.rearrange("p h c -> p (h c)"), ident)
            last_of(nc.tensor.transpose(b[0:32, P:2 * P], gf_cols.rearrange("p h c -> p (h c)"), ident))
            w = item(IT_KC)
            for n, at_ in (("kc", 0), ("ksl", 256), ("vc", 128)):
                for c in range(CH):
                    features((n, c), lambda k: w[:, k, at_:at_ + P], c)
            for c in range(CH):
                tokens(("vsl", c), w, 384, P, range(4 * c, 4 * c + 4))
            w = item(IT_KWN)
            for c in range(CH):
                features(("kwn", c), lambda k: w[:, k, 0:P], c)
            for c in range(CH):
                tokens(("vwn", c), w, P, P, range(4 * c, 4 * c + 4))
            pe.wait_ge(exp_out, 1)
            b = claim(pe, "gcol")
            for n, a in enumerate((u_, dec_, em_, wp_)):
                last = nc.tensor.transpose(b[:, 32 * n:32 * n + 32], a, ident[0:32, 0:32])
            last_of(last)
            for n, it in (("mq", IT_MQ), ("mk", IT_MK)):
                w = item(it)
                for j in range(4):
                    for c in range(CH):
                        features((n, j, c), lambda k: w[:, k, P * j:P * j + P], c)
            for n, it in (("mv", IT_MV), ("mo", IT_MO)):
                w = item(it)
                for t in range(NT):
                    tokens((n, t), w, 0, 512, [t])
            for i in range(4, 12):
                modulation(i, IT_ADA2 + i - 4)
            end_stage(pe, 1)

            pe.wait_ge(const_in, 144)
            for a in range(2):
                w = item(IT_CMP + a).rearrange("p k n -> p (k n)").rearrange("p (k n) -> p k n", n=P)
                src = (kcT, vcT)[a]
                for g in range(2):
                    half = slice(HD * g, HD * g + HD)
                    b = claim(pe, ("chid", a, g))
                    for j in range(32):
                        nc.tensor.matmul(b[:, 0:NCMP], w[half, j, :], src[half, j:j + 16 * (NCMP - 1) + 1:16],
                                         start=(j == 0), stop=(j == 31))
                    for j in range(32):
                        last = nc.tensor.matmul(b[:, 64:65], w[half, j, :], pe_cols[half, a, j:j + 1],
                                                start=(j == 0), stop=(j == 31))
                    last_of(last)
            was_read(pe, ("chid", 0, 1))
            b = claim(pe, "kcmp")
            for g in range(2):
                last = nc.tensor.matmul(b[HD * g:HD * g + HD, 0:NCMP], w2c[:, 0, :], hid[:, 0, g, 0:NCMP],
                                        start=True, stop=True)
            last_of(last)
            was_read(pe, ("chid", 1, 1))
            b = claim(pe, "vcmp")
            for g in range(2):
                last = nc.tensor.matmul(b[0:NCMP, HD * g:HD * g + HD], hid[:, 1, g, 0:NCMP], w2c[:, 1, :],
                                        start=True, stop=True)
            last_of(last)
            pe.wait_ge(state_zero, 1)
            for c in range(NT):
                at_c = slice(P * c, P * c + P)
                b = claim(pe, ("S", c))
                for h in range(MH):
                    last = nc.tensor.matmul(b[:, P * h:P * h + P], mkT[:, h, at_c], mqT[:, h, at_c], start=True, stop=True)
                last_of(last)
                b = claim(pe, ("kr", c))
                for h in range(MH):
                    last = nc.tensor.transpose(b[:, P * h:P * h + P], mkT[:, h, at_c], ident)
                last_of(last)
                was_read(pe, ("S", c))
                for p in range(2):
                    b = claim(pe, ("num", c, p))
                    for h in range(2):
                        last = nc.tensor.matmul(b[:, 129 * h:129 * h + 129], wts[c % 2][:, 2 * p + h, :],
                                                v1[:, c, 2 * p + h, :], start=True, stop=True)
                    last_of(last)
                if c:
                    was_read(pe, ("kv", c - 1, 1))
                for p in range(2):
                    b = claim(pe, ("int", c, p))
                    for h in range(2):
                        last = nc.tensor.matmul(b[:, 129 * h:129 * h + 129], mqT[:, 2 * p + h, at_c],
                                                state[:, 2 * p + h, :], start=True, stop=True)
                    last_of(last)
                was_read(pe, ("kr", c))
                for p in range(2):
                    b = claim(pe, ("kv", c, p))
                    for h in range(2):
                        last = nc.tensor.matmul(b[:, 129 * h:129 * h + 129], kw[c % 2][:, 2 * p + h, :],
                                                v1[:, c, 2 * p + h, :], start=True, stop=True)
                    last_of(last)
            end_stage(pe, 2)
            def qk(u):
                t, h, br, first, blocks, keys = unit(u)
                if u >= 2:
                    pe.wait_ge(probs_ready, u - 1)
                half = slice(HD * (h // 4), HD * (h // 4) + HD)
                src = (k_cmp[half, 0:NCMP], kslT[half, :], kwnT[half, P * first:])[br]
                for at_ in range(0, keys, 512):
                    w = min(512, keys - at_)
                    last = nc.tensor.matmul(scores(u)[:, at_:at_ + w], qT[half, h % 4, P * t:P * t + P],
                                            src[:, at_:at_ + w], start=True, stop=True)
                last.then_inc(scores_ready, 1)

            def pv(u):
                t, h, br, first, blocks, keys = unit(u)
                hh_ = u // 3
                o = ps[:, 6 + hh_ % 2, HD * br:HD * br + HD]
                pe.wait_ge(probs_ready, u + 1)
                for n, q in enumerate(range(GROUPS[u], GROUPS[u + 1])):
                    if q >= 2:
                        pe.wait_ge(turned_read[q % 2], q // 2)
                    for m in range(min(4, blocks - 4 * n)):
                        at_ = P * (4 * n + m)
                        w = keys if br == 0 else P
                        last = nc.tensor.transpose(ps[0:w, 4 + q % 2, P * m:P * m + P], probs[u % 2][:, at_:at_ + w], ident)
                    last.then_inc(turned_ready, 1)
                if br == 0 and hh_ >= 2:
                    pe.wait_ge(out_read, hh_ - 1)
                for n, q in enumerate(range(GROUPS[u], GROUPS[u + 1])):
                    pe.wait_ge(turned_read[q % 2], q // 2 + 1)
                    for m in range(min(4, blocks - 4 * n)):
                        blk = 4 * n + m
                        if br == 0:
                            lhs, rhs = probs_T[q % 2][0:keys, 0:P], v_cmp[0:keys, h // 4, :]
                        else:
                            col = P * (br - 1) + HD * (h // 4)
                            lhs, rhs = probs_T[q % 2][:, P * m:P * m + P], vv[:, first + blk, col:col + HD]
                        last = nc.tensor.matmul(o, lhs, rhs, start=(blk == 0), stop=(blk == blocks - 1))
                    last.then_inc(pv_done, 1)

            qk(0)
            for u in range(NU):
                if u + 1 < NU:
                    qk(u + 1)
                pv(u)
            end_stage(pe, 3)

            pe.wait_ge(diag_ready, 1)
            for i in range(2):
                dgr = diag[i].rearrange("p k n -> p (k n)")
                for n in range(2):
                    b = claim(pe, ("row", i, n))
                    last_of(nc.tensor.matmul(b, ones_sq, dgr[:, 512 * n:512 * n + 512], start=True, stop=True))

            def e_turn(t):
                for n, y in enumerate((ym, yn)):
                    b = claim(pe, ("yT", t, n))
                    for k in range(4):
                        last = nc.tensor.transpose(b[:, P * k:P * k + P], y[:, t, P * k:P * k + P], ident)
                    last_of(last)

            def e_router(t):
                pe.wait_ge(xn2_done, t + 1)
                for n in range(2):
                    b = claim(pe, ("xT2", t, n))
                    for k in range(4):
                        last = nc.tensor.transpose(b[:, P * k:P * k + P], xn2[t % 2][:, P * (4 * n + k):P * (4 * n + k) + P], ident)
                    last_of(last)
                b = claim(pe, ("lg", t))
                for n in range(2):
                    was_read(pe, ("xT2", t, n))
                for k in range(KT):
                    last = nc.tensor.matmul(b[:, 0:36], h2T[:, k, :], w_router[:, k, :], start=(k == 0), stop=(k == KT - 1))
                last_of(last)

            pe.wait_ge(router_in, 64)
            pe.wait_ge(wout_scaled, 8)
            e_turn(0)
            for t in range(NT):
                if t + 1 < NT:
                    e_turn(t + 1)
                for n in range(2):
                    was_read(pe, ("yT", t, n))
                for n in range(2):
                    b = claim(pe, ("out", t, n))
                    w = ring[(IT_WOUT + n) % 3]
                    for k in range(KT):
                        last = nc.tensor.matmul(b, yT[t % 2][:, k, :], w[:, k, :], start=(k == 0), stop=(k == KT - 1))
                    last_of(last)
                if t:
                    e_router(t - 1)
            e_router(NT - 1)
            pe.wait_ge(hots_ready, 1)
            b = claim(pe, "rank")
            hv = hots.rearrange("p t e -> p (t e)")
            nc.tensor.matmul(b[:, 0:256], upper, hv, start=True, stop=True)
            last_of(nc.tensor.matmul(b[:, 256:512], ones_sq, hv, start=True, stop=True))
            end_stage(pe, 4)

            def f_turn(s, n, other):
                pe.wait_ge(xg_in[s], 16 * n + 16)
                if other is not None:
                    pe.wait_ge(xgT_act[1 - s], other)
                    pe.wait_ge(xgT_dve[1 - s], other)
                for k in range(KT):
                    last = nc.tensor.transpose(ps[:, k // 4, P * (k % 4):P * (k % 4) + P], xg[s][:, P * k:P * k + P], ident)
                last.then_inc(xg_turned[s], 1)

            e_blocks = pe.value_load(block_tab[0:1, 48:49], min_val=NE, max_val=NB)
            for s in range(2):
                for credit in (up_part, xg_turned, down_done):
                    pe.sem_inc(credit[s], 1)
            f_turn(0, 0, None)
            with pe.Fori(0, NB // 2) as i:
                for s in range(2):
                    with pe.If(2 * i + s < e_blocks):
                        pe.wait_ge(w13_in[s], 32 * i + 32)
                        pe.wait_ge(xgT_act[s], i + 1)
                        pe.wait_ge(xgT_dve[s], i + 1)
                        for m in range(4):
                            if m >= 2:
                                pe.wait_ge(hid_part[s], 4 * i + m)
                            for n in range(2):
                                for k in range(KT):
                                    last = nc.tensor.matmul(ps[:, 2 + 2 * n + m % 2, 0:P],
                                                            w13[s][n][:, k, P * m:P * m + P], xgT[s][:, k, :],
                                                            start=(k == 0), stop=(k == KT - 1))
                            last.then_inc(up_part[s], 1)
                    with pe.If(2 * i + s + 1 < e_blocks):
                        f_turn(1 - s, i + s, i + 1)
                    with pe.If(2 * i + s < e_blocks):
                        pe.wait_ge(w2_in[s], 16 * i + 16)
                        pe.wait_ge(yo_act[1 - s], i + s + 1)
                        pe.wait_ge(yo_dve[1 - s], i + s + 1)
                        for k in range(4):
                            pe.wait_ge(hid_part[s], 4 * i + k + 2)
                            for n in range(2):
                                last = nc.tensor.matmul(ps[:, 6 + n, :], hid_e[s][:, k, :], w2s[s][:, k, 512 * n:512 * n + 512],
                                                        start=(k == 0), stop=(k == 3))
                        last.then_inc(down_done[s], 1)
            pe.drain().then_inc(stage_f, 1)

        @block.vector
        def _(dve):
            link = chain(dve, dve_step)
            V = nc.vector
            b = ready(dve, "vec")
            read(V.tensor_copy(cols, b[:, 0:124]), "vec")
            was_read(dve, "vec")
            for c in range(CH):
                dve.wait_ge(sq_done, 4 * c + 4)
                V.tensor_scalar(rstd[:, 4 * c:4 * c + 4], sum_sq[:, 4 * c:4 * c + 4], 1.0 / D, EPS,
                                ALU.mult, ALU.add).then_inc(norm_ms, 1)
                dve.wait_ge(norm_sqrt, c + 1)
                link(V.reciprocal(rstd[:, 4 * c:4 * c + 4], rstd[:, 4 * c:4 * c + 4]))
                for t in range(4 * c, 4 * c + 4):
                    V.tensor_scalar(xn[:, t, :], xn[:, t, :], rstd[:, t:t + 1], None, ALU.mult).then_inc(xn_done, 1)

            def modulation(i):
                b = ready(dve, ("ada", i))
                read(V.tensor_tensor(mod[:, 4 * i:4 * i + 4], b[:, 0:4], cols[:, 4 * i:4 * i + 4], ALU.add), ("ada", i))

            for i in range(4):
                modulation(i)
            was_read(dve, ("ada", 3))
            V.scalar_tensor_tensor(scale1, mod[:, 8:16], 1.0, cols[:, 48:56], ALU.add, ALU.mult).then_inc(mod_ready, 1)
            dve.wait_ge(mod_ready, 1)
            for c in range(CH):
                for k in range(0, KT, 2):
                    b = ready(dve, ("hT", c, k))
                    read(V.tensor_scalar(hT[:, k, 512 * c:512 * c + 512], b, scale1[:, k:k + 1], mod[:, k:k + 1],
                                         ALU.mult, ALU.add), ("hT", c, k))
            dve.wait_ge(const_in, 144)
            link(V.tensor_copy(pos_f, pos_i))
            link(V.tensor_scalar(ang, pos_f, freq[:, 0:1], None, ALU.mult))
            for n, (dst, turn, back) in enumerate(((sin, 0.0, 0.0), (cos, 0.25, float(np.pi / 2)))):
                link(V.tensor_scalar(turns, ang, 1.0 / TWO_PI, turn, ALU.mult, ALU.add))
                link(V.tensor_scalar(turns, turns, ROUND, None, ALU.add))
                link(V.tensor_scalar(turns, turns, ROUND, None, ALU.subtract))
                link(V.scalar_tensor_tensor(dst, turns, -PI2[0], ang, ALU.mult, ALU.add))
                link(V.scalar_tensor_tensor(dst, turns, -PI2[1], dst, ALU.mult, ALU.add))
                link(V.scalar_tensor_tensor(dst, turns, -PI2[2], dst, ALU.mult, ALU.add))
                link(V.tensor_scalar(dst, dst, back, PI_IN, ALU.add, ALU.min))
                V.tensor_scalar(dst, dst, -PI_IN, None, ALU.max).then_inc(angle, 1)
            end_stage(dve, 0)

            dve.wait_ge(trig, 1)
            link(V.tensor_scalar(sin, sin, freq[:, 1:2], None, ALU.mult))
            dve.wait_ge(trig, 2)
            b = ready(dve, "gates")
            read(V.tensor_copy(gall, b[:, 0:256].rearrange("p (t n) -> p t n", n=32)), "gates")
            was_read(dve, "gates")
            g = gall.rearrange("p c n -> p n c")
            V.tensor_tensor(gi_cols, g[:, 0:MH, :], gate_b[:, 0:MH].unsqueeze(2).broadcast_to([P, MH, NT]), ALU.add)
            V.tensor_tensor(gf_cols, g[:, MH:2 * MH, :], gate_b[:, MH:2 * MH].unsqueeze(2).broadcast_to([P, MH, NT]),
                            ALU.add).then_inc(gates_in_cols, 1)
            n_rope = [0]

            def rope(name, dst, c, scale):
                n = n_rope[0]
                dve.wait_ge(swapped, n + 1)
                b = ready(dve, name)
                read(V.scalar_tensor_tensor(turned[:, n % 2, :], b, scale, cos[:, 512 * c:512 * c + 512],
                                            ALU.mult, ALU.mult), name)
                link(V.tensor_tensor(swap[:, n % 2, :], swap[:, n % 2, :], sin[:, 512 * c:512 * c + 512], ALU.mult))
                was_read(dve, name)
                V.tensor_tensor(dst[:, 512 * c:512 * c + 512], turned[:, n % 2, :], swap[:, n % 2, :],
                                ALU.add).then_inc(roped, 1)
                n_rope[0] += 1

            for j in range(4):
                for c in range(CH):
                    rope(("q", j, c), qT[:, j, :], c, HD ** -0.5)
            b = ready(dve, "gT")
            V.tensor_copy(g_i, b[0:32, 0:P])
            read(V.tensor_copy(g_f, b[0:32, P:2 * P]), "gT")
            was_read(dve, "gT")
            V.scalar_tensor_tensor(abs_f, g_f, -1.0, g_f, ALU.mult, ALU.max).then_inc(exp_f, 1)
            for n, dst in (("kc", kcT), ("ksl", kslT)):
                for c in range(CH):
                    rope((n, c), dst, c, 1.0)
            link(V.memset(ones_r, 1.0))
            dve.wait_ge(ln_f, 1)
            link(V.scalar_tensor_tensor(g_f, g_f, 0.0, t_a, ALU.min, ALU.subtract))
            link(V.tensor_tensor_scan(decay_b, ones_r, g_f, 0.0, ALU.mult, ALU.add))
            link(V.tensor_tensor(u_, g_i, decay_b, ALU.subtract))
            link(V.tensor_tensor_scan(cmax, u_, u_, -3e38, ALU.max, ALU.max))
            V.tensor_copy(hop[:, 0:1], decay_b[:, P - 1:P])
            V.tensor_tensor(hop[:, 1:2], decay_b[:, P - 1:P], cmax[:, P - 1:P], ALU.add).then_inc(hop_out, 1)
            for c in range(CH):
                rope(("kwn", c), kwnT, c, 1.0)
            dve.wait_ge(hop_in, 32)
            link(V.memset(hop5, 0.0))
            link(V.tensor_tensor_scan(hop5[:, :, 1], hop4[:, :, 0], hop4[:, :, 1], 0.0, ALU.add, ALU.max))
            V.tensor_copy(hop5[:, 1:8, 0], hop5[:, 0:7, 1]).then_inc(hop_out, 1)
            dve.wait_ge(hop_in, 64)
            m_old, m_new = hop2[:, 0:1], hop2[:, 1:2]
            link(V.tensor_scalar(mx, cmax, m_old, None, ALU.max))
            V.tensor_scalar(neg_mx, mx, -1.0, None, ALU.mult)
            V.tensor_scalar(dec_, mx, -1.0, m_old, ALU.mult, ALU.add)
            link(V.tensor_tensor(gm32, hop[:, 0:1], m_new, ALU.subtract))
            link(V.scalar_tensor_tensor(em_, mx, -1.0, decay_b, ALU.mult, ALU.subtract))
            link(V.tensor_scalar(wp_, u_, gm32, None, ALU.add))
            V.tensor_tensor(hop2[:, 2:3], gm32, m_old, ALU.add).then_inc(exp_in, 1)
            dve.wait_ge(exp_out, 1)
            b = ready(dve, "gcol")
            read(V.tensor_copy(gcols, b[:, 0:P].rearrange("p (a r) -> p a r", a=4)), "gcol")
            for i, n in enumerate(("mq", "mk")):
                dst = (mqT, mkT)[i]
                for j in range(4):
                    m = 4 * i + j
                    was_read(dve, (n, j, 0))
                    was_read(dve, (n, j, 1))
                    tap = lambda s: cols[:, 92 + 8 * s + m:93 + 8 * s + m]
                    link(V.tensor_scalar(dst[:, j, :], conv_raw[:, m % 2, 0:S], tap(0), None, ALU.mult))
                    for s in range(1, 4):
                        ins = V.scalar_tensor_tensor(dst[:, j, :], conv_raw[:, m % 2, s:s + S], tap(s), dst[:, j, :],
                                                     ALU.mult, ALU.add)
                        if s < 3:
                            link(ins)
                    ins.then_inc(conv_done, 1)
            for i in range(4, 12):
                modulation(i)
            end_stage(dve, 1)

            link(V.scalar_tensor_tensor(scale2, mod[:, 32:40], 1.0, cols[:, 64:72], ALU.add, ALU.mult))
            link(V.tensor_tensor(gm_col[:, 0, :], mod[:, 16:24], cols[:, 56:64], ALU.mult))
            link(V.tensor_tensor(gm_col[:, 1, :], mod[:, 40:48], cols[:, 72:80], ALU.mult))
            for a in range(2):
                for g in range(2):
                    b = ready(dve, ("chid", a, g))
                    V.tensor_copy(hbias[:, a, g:g + 1], b[:, 64:65]).then_inc(hbias_ready, 1)
            b = ready(dve, "kcmp")
            read(V.tensor_copy(k_cmp[:, 0:NCMP], b[:, 0:NCMP]), "kcmp")
            for c in range(NT):
                decay = bc[:, :, c, :]
                dve.wait_ge(decay_exp, c + 1)
                b = ready(dve, ("S", c))
                if c >= 2:
                    dve.wait_ge(psum_ready, JOB[("kv", c - 2, 1)] + 1)
                read(V.tensor_tensor(wts[c % 2], b.rearrange("p (h n) -> p h n", h=MH), decay, ALU.mult), ("S", c))
                b = ready(dve, ("kr", c))
                col = lambda a: gcols[:, a, c:32:8]
                read(V.tensor_tensor(kw[c % 2], b.rearrange("p (h n) -> p h n", h=MH),
                                     col(3).unsqueeze(2).broadcast_to([P, MH, P]), ALU.mult), ("kr", c))
                n_ = num[c % 2]
                for p in range(2):
                    was_read(dve, ("num", c, p))
                for p in range(2):
                    b = ready(dve, ("int", c, p))
                    for h in range(2):
                        last = V.scalar_tensor_tensor(n_[:, 2 * p + h, :], b[:, 129 * h:129 * h + 129],
                                                      gcols[:, 1, 8 * (2 * p + h) + c:8 * (2 * p + h) + c + 1],
                                                      n_[:, 2 * p + h, :], ALU.mult, ALU.add)
                    read(last, ("int", c, p))
                for p in range(2):
                    b = ready(dve, ("kv", c, p))
                    for h in range(2):
                        r = 8 * (2 * p + h) + c
                        last = V.scalar_tensor_tensor(state[:, 2 * p + h, :], state[:, 2 * p + h, :], a_old[:, r:r + 1],
                                                      b[:, 129 * h:129 * h + 129], ALU.mult, ALU.add)
                    read(last, ("kv", c, p))
                was_read(dve, ("int", c, 1))
                dn = n_[:, :, P]
                link(V.scalar_tensor_tensor(den, dn, -1.0, dn, ALU.mult, ALU.max))
                link(V.tensor_tensor(den, den, col(2), ALU.max))
                link(V.reciprocal(den, den))
                link(V.tensor_tensor(hh, n_[:, :, 0:P], den.unsqueeze(2).broadcast_to([P, MH, P]), ALU.mult))
                link(V.tensor_tensor(sq, hh, hh, ALU.mult))
                link(V.tensor_reduce(ssq4, sq, AX.X, ALU.add))
                V.tensor_scalar(ssq4, ssq4, 1.0 / P, EPS, ALU.mult, ALU.add).then_inc(h_ms, 1)
                dve.wait_ge(h_sqrt, c + 1)
                link(V.reciprocal(rs4, rs4))
                link(V.tensor_tensor(hh, hh, rs4.unsqueeze(2).broadcast_to([P, MH, P]), ALU.mult))
                y = ym[:, c, :].rearrange("p (h n) -> p h n", h=MH)
                link(V.tensor_tensor(y, y, hh, ALU.mult))
            end_stage(dve, 2)
            def maximum(u):
                t, h, br, first, blocks, keys = unit(u)
                sc = scores(u)
                dve.wait_ge(scores_ready, u + 1)
                if br == 0:
                    n0 = max(0, 8 * t - 1)
                    link(V.tensor_tensor(sc[:, n0:keys], sc[:, n0:keys], cmask[:, t, n0:keys], ALU.add))
                else:
                    ins = V.tensor_tensor(sc[:, keys - P:keys], sc[:, keys - P:keys], causal, ALU.add)
                    if br == 2 and t >= 4:
                        link(ins)
                        ins = V.tensor_tensor(sc[:, 0:P], sc[:, 0:P], behind, ALU.add)
                    link(ins)
                m = nmax[:, u % 4:u % 4 + 1]
                ins = V.tensor_reduce(m, sc[:, 0:keys], AX.X, ALU.max, negate=True)
                if br == 0 and t == 0:
                    link(ins)
                    ins = V.tensor_scalar(m, m, 1e20, None, ALU.min)
                ins.then_inc(row_max, 1)

            def finish_head(hh_):
                t, h = divmod(hh_, NH)
                dve.wait_ge(pv_done, GROUPS[3 * hh_ + 3])
                dve.wait_ge(probs_ready, 3 * hh_ + 3)
                s_ = sums[:, hh_ % 4, :]
                if t == 0:
                    link(V.tensor_scalar(s_, s_, 1e-30, None, ALU.max))
                link(V.reciprocal(rsum, s_))
                link(V.tensor_tensor(rsum, rsum, sgate[:, t, 3 * h:3 * h + 3], ALU.mult))
                o = ps[:, 6 + hh_ % 2, 0:3 * HD].rearrange("p (b n) -> p b n", b=3)
                V.tensor_tensor(branches, o, rsum.unsqueeze(2).broadcast_to([P, 3, HD]), ALU.mult).then_inc(out_read, 1)
                dve.wait_ge(out_read, hh_ + 1)
                link(V.tensor_reduce(yn[:, t, HD * h:HD * h + HD], branches.rearrange("p b n -> p n b"), AX.X, ALU.add))

            maximum(0)
            for u in range(NU):
                if u + 1 < NU:
                    maximum(u + 1)
                evacuate_turned(dve, V.tensor_copy, u, 1)
                if u % 3 == 2:
                    finish_head(u // 3)
            end_stage(dve, 3)

            bc_id = ident.unsqueeze(1).broadcast_to([P, KT, P])
            for i in range(2):
                ins = V.tensor_tensor(diag[i], bc_id, gm_col[:, i, :].unsqueeze(2).broadcast_to([P, KT, P]), ALU.mult)
            ins.then_inc(diag_ready, 1)
            for i, dst in enumerate((gm_row, gf_row)):
                for n in range(2):
                    b = ready(dve, ("row", i, n))
                    read(V.tensor_copy(dst[:, 512 * n:512 * n + 512], b), ("row", i, n))
            for n in range(2):
                was_read(dve, ("row", 1, n))

            def e_turned(t):
                b = ready(dve, ("yT", t, 1))
                if t >= 2:
                    dve.wait_ge(psum_ready, JOB[("out", t - 2, 1)] + 1)
                read(V.tensor_copy(yT[t % 2][:, 4:8, :], b.rearrange("p (k n) -> p k n", n=P)), ("yT", t, 1))

            def e_router(t):
                b = ready(dve, ("xT2", t, 1))
                if t >= 1:
                    dve.wait_ge(psum_ready, JOB[("lg", t - 1)] + 1)
                for k in range(4, 8):
                    last = V.tensor_scalar(h2T[:, k, :], b[:, P * (k - 4):P * (k - 4) + P], scale2[:, k:k + 1],
                                           mod[:, 24 + k:25 + k], ALU.mult, ALU.add)
                read(last, ("xT2", t, 1))
                b = ready(dve, ("lg", t))
                read(V.tensor_tensor(logits[:, t, :], b[:, 0:36], b_router, ALU.add), ("lg", t))

            e_turned(0)
            dve.wait_ge(router_in, 64)
            for t in range(NT):
                if t + 1 < NT:
                    e_turned(t + 1)
                dve.wait_ge(y_sq, t + 1)
                V.tensor_scalar(ys, ys, 1.0 / D, EPS, ALU.mult, ALU.add).then_inc(y_ms, 1)
                dve.wait_ge(y_sqrt, t + 1)
                link(V.reciprocal(rs_y, rs_y))
                link(V.scalar_tensor_tensor(y_row, y_row, rs_y, gm_row, ALU.mult, ALU.mult))
                dve.wait_ge(xt_in[t % 2], 16 * (t // 2) + 16)
                V.tensor_tensor(x2[:, t, :], y_row, xt[t % 2], ALU.add).then_inc(x2_done, 1)
                dve.wait_ge(x2_done, t + 1)
                dve.wait_ge(x_sq, t + 1)
                V.tensor_scalar(xs_, xs_, 1.0 / D, EPS, ALU.mult, ALU.add).then_inc(x_ms, 1)
                dve.wait_ge(x_sqrt, t + 1)
                link(V.reciprocal(rs_x, rs_x))
                if t >= 2:
                    dve.wait_ge(xn_stored[t % 2], 16 * (t // 2))
                    dve.wait_ge(psum_ready, JOB[("xT2", t - 2, 1)] + 1)
                V.tensor_scalar(xn2[t % 2], x2[:, t, :], rs_x, None, ALU.mult).then_inc(xn2_done, 1)
                if t:
                    e_router(t - 1)
            e_router(NT - 1)
            was_read(dve, ("lg", NT - 1))

            lg = logits[:, :, 0:4]
            le = logits[:, :, 4:36].rearrange("p t (g e) -> p t g e", g=4)

            def over_last(v, n):
                return v.unsqueeze(2).broadcast_to([P, NT, n])

            def first_hot(onehot, index, values, best, eq, scratch, n, io, iom):
                link(V.tensor_reduce(best, values, AX.X, ALU.max))
                link(V.tensor_tensor(eq, values, over_last(best, n), ALU.is_equal))
                link(V.scalar_tensor_tensor(scratch, eq, -64.0, io.unsqueeze(1).broadcast_to([P, NT, n]), ALU.mult, ALU.add))
                link(V.tensor_reduce(index, scratch, AX.X, ALU.min))
                link(V.tensor_tensor(onehot, iom.unsqueeze(1).broadcast_to([P, NT, n]), over_last(index, n), ALU.is_equal))

            first_hot(ohg, ig, lg, mg, eqg, dg, 4, iota4, iota4m)
            link(V.tensor_tensor(dg, lg, over_last(mg, 4), ALU.subtract))
            link(V.tensor_tensor(prod, le, ohg.unsqueeze(3).broadcast_to([P, NT, 4, 8]), ALU.mult))
            link(V.tensor_reduce(lin, prod.rearrange("p t g e -> p t e g"), AX.X, ALU.add))
            first_hot(oh1, i1, lin, m1, eqe, cand, 8, iota8, iota8m)
            link(V.scalar_tensor_tensor(lin, oh1, NEG, lin, ALU.mult, ALU.add))
            first_hot(oh2, i2, lin, m2, eqe, cand, 8, iota8, iota8m)
            V.tensor_tensor(e2, m2, m1, ALU.subtract).then_inc(exp_args, 1)
            for k, oh in enumerate((oh1, oh2)):
                link(V.tensor_tensor(hot[k], ohg.unsqueeze(3).broadcast_to([P, NT, 4, 8]),
                                     oh.unsqueeze(2).broadcast_to([P, NT, 4, 8]), ALU.mult))
            h0, h1_ = (v.rearrange("p t g e -> p t (g e)") for v in hot)
            V.tensor_tensor(hots, h0, h1_, ALU.add).then_inc(hots_ready, 1)
            dve.wait_ge(exps_done, 2)
            link(V.tensor_reduce(sg_, dg, AX.X, ALU.add))
            link(V.scalar_tensor_tensor(sg_, e2, 1.0, sg_, ALU.add, ALU.mult))
            link(V.reciprocal(gates2[:, 0, :], sg_))
            link(V.tensor_tensor(gates2[:, 1, :], gates2[:, 0, :], e2, ALU.mult))
            b = ready(dve, "rank")
            link(V.tensor_copy(before, b[:, 256:512].rearrange("p (t e) -> p t e", e=NE)))
            link(V.memset(prefix[:, 0, :], 0.0))
            for t in range(1, NT):
                link(V.tensor_tensor(prefix[:, t, :], prefix[:, t - 1, :], before[:, t - 1, :], ALU.add))
            link(V.tensor_tensor(total, prefix[:, NT - 1, :], before[:, NT - 1, :], ALU.add))
            read(V.tensor_tensor(rank, b[:, 0:256].rearrange("p (t e) -> p t e", e=NE), prefix, ALU.add), "rank")
            was_read(dve, "rank")
            link(V.memset(ones32, 1.0))
            link(V.tensor_scalar(over, total, float(P), None, ALU.is_gt))
            for j in range(2, NT):
                link(V.scalar_tensor_tensor(over, total, float(P * j), over, ALU.is_gt, ALU.add))
            link(V.tensor_tensor_scan(over_inc, ones32, over, 0.0, ALU.mult, ALU.add))
            link(V.tensor_tensor(off_e, over_inc, over, ALU.subtract))
            link(V.tensor_tensor(off_e, off_e, iota32, ALU.subtract))
            link(V.tensor_scalar(off_e, off_e, float(NE - 1), float(P), ALU.add, ALU.mult))
            for k, hk in enumerate((h0, h1_)):
                for dst, src in ((rk, rank), (ex, iota32), (ofs, off_e)):
                    if src is not rank:
                        src = src.unsqueeze(1).broadcast_to([P, NT, NE])
                    link(V.tensor_tensor(before, hk, src, ALU.mult))
                    link(V.tensor_reduce(dst[:, k, :], before, AX.X, ALU.add))
            link(V.tensor_scalar(big, rk, float(P), None, ALU.is_ge))
            link(V.tensor_tensor(big, big, ofs, ALU.mult))
            link(V.scalar_tensor_tensor(ex, ex, float(P), rk, ALU.mult, ALU.add))
            link(V.tensor_tensor(dest, ex, big, ALU.add))
            link(V.tensor_single_scalar(laneslot, dest, P - 1, ALU.bitwise_and))
            link(V.tensor_single_scalar(slot, dest, 7, ALU.logical_shift_right))
            link(V.scalar_tensor_tensor(slot, laneslot, float(NB), slot, ALU.mult, ALU.add))
            link(V.memset(tabf[0:1, 0:64], 0.0))
            link(V.tensor_copy(tabf[0:1, 0:NE], iota32[0:1, :]))
            one = lambda v, *s: v[0:1, :].unsqueeze(s[0]).broadcast_to([1, NOV, NE])
            link(V.tensor_tensor(ov_cmp[0:1], one(over_inc, 1), one(iota15, 2), ALU.is_le))
            link(V.tensor_reduce(tabf[0:1, NE:NE + NOV], ov_cmp[0:1], AX.X, ALU.add))
            link(V.tensor_scalar(tabf[0:1, 0:NB], tabf[0:1, 0:NB], float(NE - 1), None, ALU.min))
            link(V.tensor_scalar(tabf[0:1, 48:49], over_inc[0:1, NE - 1:NE], float(NE), None, ALU.add))
            V.tensor_copy(block_tab, tabf[0:1, 0:64]).then_inc(dest_ready, 1)
            end_stage(dve, 4)

            def f_turned(s, n):
                dve.wait_ge(xg_turned[s], n + 2)
                dve.wait_ge(up_part[s], 4 * n + 1)
                for k in range(4, 8):
                    last = V.tensor_scalar(xgT[s][:, k, :], ps[:, 1, P * (k - 4):P * (k - 4) + P], scale2[:, k:k + 1],
                                           mod[:, 24 + k:25 + k], ALU.mult, ALU.add)
                last.then_inc(xgT_dve[s], 1)

            for s in range(2):
                for credit in (hid_part, yo_dve):
                    dve.sem_inc(credit[s], 1)
            v_blocks = dve.value_load(block_tab[0:1, 48:49], min_val=NE, max_val=NB)
            f_turned(0, 0)
            with dve.Fori(0, NB // 2) as i:
                for s in range(2):
                    with dve.If(2 * i + s < v_blocks):
                        for m in range(4):
                            dve.wait_ge(silu_part[s], 4 * i + m + 1)
                            V.tensor_tensor(hid_e[s][:, m, :], act1[s][:, m, :], ps[:, 4 + m % 2, 0:P],
                                            ALU.mult).then_inc(hid_part[s], 1)
                    with dve.If(2 * i + s + 1 < v_blocks):
                        f_turned(1 - s, i + s)
                    with dve.If(2 * i + s < v_blocks):
                        dve.wait_ge(down_done[s], i + 2)
                        V.tensor_copy(yo[s][:, 512:1024], ps[:, 7, :]).then_inc(yo_dve[s], 1)
            dve.drain().then_inc(stage_f, 1)
            dve.wait_ge(stage_f, 4)

            for t in range(NT):
                a, b = y1[t % 2], y2[t % 2]
                dve.wait_ge(y_in[t % 2], 32 * (t // 2) + 32)
                link(V.tensor_scalar(a, a, gates2[:, 0, t:t + 1], None, ALU.mult))
                V.scalar_tensor_tensor(a, b, gates2[:, 1, t:t + 1], a, ALU.mult, ALU.add).then_inc(g_ms, 1)
                dve.wait_ge(g_sq, t + 1)
                V.tensor_scalar(ys, ys, 1.0 / D, EPS, ALU.mult, ALU.add).then_inc(g_ms, 1)
                dve.wait_ge(g_sqrt, t + 1)
                link(V.reciprocal(rs_y, rs_y))
                link(V.scalar_tensor_tensor(a, a, rs_y, gf_row, ALU.mult, ALU.mult))
                V.tensor_tensor(a, a, x2[:, t, :], ALU.add).then_inc(g_done, 1)


def kernel(**inputs):
    import concourse.bacc as bacc
    from concourse.bass_utils import run_bass_kernel_spmd

    nc = bacc.Bacc("TRN2", target_bir_lowering=False, num_devices=1)
    lane = np.arange(P) % HD
    inv = (10000.0 ** (-(lane % 32) / 32.0)).astype(np.float32)
    arrays = {"rope_cols": np.stack([inv, np.where(lane < 32, -1.0, 1.0).astype(np.float32)], 1)}
    for name, a in inputs.items():
        a = np.asarray(a)
        arrays[name] = np.ascontiguousarray(a if name in ("positions", "mlstm_gate_b", "c", "router_grp_b", "router_exp_b") else a[0])
    for name in ("ada_b", "norm_mix_pre", "norm_mix_post", "norm_ffn_pre", "norm_ffn_post", "c", "mlstm_head_norm"):
        arrays[name] = arrays[name].reshape(-1)
    d = {n: nc.dram_tensor(n, a.shape, mybir.dt.from_np(a.dtype), kind="ExternalInput").ap() for n, a in arrays.items()}
    out = nc.dram_tensor("out", (S, D), F32, kind="ExternalOutput").ap()
    build(nc, d, out)
    r = run_bass_kernel_spmd(nc, [arrays], core_ids=[0])
    return r.results[0]["out"].reshape(1, *(S, D))
```

```python
from contextlib import ExitStack

import numpy as np
import concourse.bass as bass
from concourse import mybir

F32 = mybir.dt.float32
I32 = mybir.dt.int32
BF16 = mybir.dt.bfloat16
ALU = mybir.AluOpType
ACT = mybir.ActivationFunctionType
AX = mybir.AxisListType

P = 128
S = D = 1024
NT = S // P
KT = D // P
CH = S // 512
HD = 64
NH = 8
MH = 4
MW = 512
NEG = -1e30
EPS = 1e-6
NCMP = 63
NE = 32
NOV = 15
FF = 512
OFF = dict(mq=0, mk=512, mv=1024, mo=1536, mi=2048, nq=2056, kc=2568, kwn=3080, ng=3336)

HT = 0
COS, SIN = 8192, 9216
CONV = 10240
MKT = 12294
V1 = MKT + 4096
RING2 = V1 + 4128
RING0 = RING2 + 4096
QT = RING0 + 8192
KSL, KWN, KCT, VCT = QT + 4096, QT + 5120, QT + 6144, QT + 7168
VV = QT + 8192
MQT = VV + 2048
YM = MQT + 4096
SMALL = YM + 4096
WORDS = 53200
W0, W1 = 0, MKT
MH_SCALE = float(np.float32(P ** -0.5))
TWO_PI = 2 * np.pi
PI2_MID = float(np.round((TWO_PI - 6.28125) * 2 ** 21) / 2 ** 21)
PI2 = (6.28125, PI2_MID, TWO_PI - 6.28125 - PI2_MID)
PI_IN = 3.1415925
ROUND = 1.5 * 2 ** 23
XN = MQT


def job_list():
    jobs = ["vec"] + [("ada", i) for i in range(4)]
    jobs += [("hT", c, k) for c in range(CH) for k in range(KT)]
    jobs += ["gates"] + [("q", j, c) for j in range(4) for c in range(CH)]
    jobs += ["gT"]
    jobs += [(n, c) for n in ("kc", "ksl", "vc", "vsl") for c in range(CH)]
    jobs += [(n, c) for n in ("kwn", "vwn") for c in range(CH)]
    jobs += ["gcol"]
    jobs += [("mq", j, c) for j in range(4) for c in range(CH)]
    jobs += [("mk", j, c) for j in range(4) for c in range(CH)]
    jobs += [("mv", t) for t in range(NT)] + [("mo", t) for t in range(NT)]
    jobs += [("ada", i) for i in range(4, 12)]
    jobs += [("chid", a, g) for a in range(2) for g in range(2)] + ["kcmp", "vcmp"]
    for c in range(NT):
        jobs += [("S", c), ("kr", c)] + [(n, c, p) for n in ("num", "int", "kv") for p in range(2)]
    jobs += [("row", i, n) for i in range(2) for n in range(2)]
    jobs += [("yT", 0, 0), ("yT", 0, 1)]
    for t in range(NT):
        jobs += [("yT", t + 1, n) for n in range(2) if t + 1 < NT] + [("out", t, n) for n in range(2)]
        jobs += [j for j in (("xT2", t - 1, 0), ("xT2", t - 1, 1), ("lg", t - 1)) if t]
    jobs += [("xT2", NT - 1, 0), ("xT2", NT - 1, 1), ("lg", NT - 1), "rank"]
    return {n: i for i, n in enumerate(jobs)}


def ring_items(d):
    w_in = d["w_in"].rearrange("(k p) n -> p k n", p=P)
    ada = d["ada_w"].rearrange("(k p) n -> p k n", p=P)
    w_out = d["w_out"].rearrange("(k p) n -> p k n", p=P)
    items = [[(0, 0, ada[:, :, 512 * i:512 * i + 512])] for i in range(4)]
    for n, w in (("nq", 512), ("kc", 512), ("kwn", 256), ("mq", 512), ("mk", 512), ("mv", 512), ("mo", 512)):
        if n == "nq":
            items.append([(P * j + HD * g, 0, w_in[:, :, OFF[n] + HD * (4 * g + j):OFF[n] + HD * (4 * g + j + 1)])
                          for j in range(4) for g in range(2)])
        else:
            items.append([(0, 0, w_in[:, :, OFF[n]:OFF[n] + w])])
    items += [[(0, 0, ada[:, :, 512 * i:512 * i + 512])] for i in range(4, 12)]
    for n in ("cmp_w1_k", "cmp_w1_v"):
        src = d[n].rearrange("(p d) n -> d p n", d=HD)
        items.append([(0, 0, src), (0, HD, src)])
    items += [[(0, 0, w_out[:, :, 512 * i:512 * i + 512])] for i in range(2)]
    return items


IT_NQ, IT_KC, IT_KWN, IT_MQ, IT_MK, IT_MV, IT_MO, IT_ADA2, IT_CMP, IT_WOUT = 4, 5, 6, 7, 8, 9, 10, 11, 19, 21


def build(nc, d, out):
    JOB = job_list()
    ITEMS = ring_items(d)
    with ExitStack() as ctx:
        def sem(name):
            return ctx.enter_context(nc.semaphore(name))

        arena = ctx.enter_context(nc.sbuf_tensor("arena", [P, WORDS], F32))
        ps = ctx.enter_context(nc.psum_tensor("ps", [P, 8, 512], F32))

        def view(at, *shape, parts=P):
            n = int(np.prod(shape))
            v = arena[0:parts, at:at + n]
            if len(shape) == 2:
                v = v.rearrange("p (a b) -> p a b", b=shape[1])
            if len(shape) == 3:
                v = v.rearrange("p (a b c) -> p a b c", b=shape[1], c=shape[2])
            return v

        small = [SMALL]

        def tiny(*shape, parts=P, dt=F32):
            at = small[0]
            small[0] += int(np.prod(shape))
            assert small[0] <= WORDS
            v = view(at, *shape, parts=parts)
            return v if dt is F32 else v.bitcast(dt)

        hT = view(HT, KT, S)
        cos, sin = view(COS, S), view(SIN, S)
        conv_raw = view(CONV, 2, S + 3)
        mkT, mqT = view(MKT, MH, S), view(MQT, MH, S)
        v1 = view(V1, NT, MH, P + 1)
        ring = [view(RING0, KT, 512), view(RING0 + 4096, KT, 512), view(RING2, KT, 512)]
        qT = view(QT, 4, S)
        kslT, kwnT, kcT, vcT = view(KSL, S), view(KWN, S), view(KCT, S), view(VCT, S)
        vv = view(VV, NT, 4 * HD)
        yn, ym = view(MQT, NT, MW), view(YM, NT, MW)
        xn = view(XN, NT, D)
        junk = view(V1, 2, D)
        swap = view(V1, 2, 512)
        turned = view(V1 + 1024, 2, 512)
        sc_ = [view(YM + P * i, P, parts=32) for i in range(12)]
        g_i, g_f, decay_b, u_, cmax, mx, dec_, em_, wp_, neg_mx, t_a, ones_r = sc_
        gi_cols, gf_cols = view(YM + 12 * P, MH, NT), view(YM + 12 * P + 32, MH, NT)
        gall = view(YM + 13 * P, NT, 32)
        abs_f = view(YM + 15 * P, P, parts=32)
        bc = view(HT, MH, NT, P)
        at = [4096]

        def temp(*shape):
            v = view(at[0], *shape)
            at[0] += int(np.prod(shape))
            assert at[0] <= MKT
            return v

        wts, kw = [temp(MH, P) for _ in range(2)], [temp(MH, P) for _ in range(2)]
        num, hh, sq = [temp(MH, P + 1) for _ in range(2)], temp(MH, P), temp(MH, P)
        state = temp(MH, P + 1)

        ident = tiny(P)
        ident_b = tiny(P // 2).bitcast(BF16)
        masks_at = small[0]
        causal = tiny(P // 2).bitcast(BF16)
        behind = tiny(P // 2).bitcast(BF16)
        cmask = tiny(NT * HD // 2).bitcast(BF16).rearrange("p (t n) -> p t n", n=HD)
        masks_end = small[0]
        cols = tiny(124)
        mod = tiny(48)
        scale1, shift1, scale2, shift2 = (tiny(KT) for _ in range(4))
        sc_col = tiny(KT)
        sum_sq, rstd = tiny(NT), tiny(NT)
        wg = view(V1 + 2304, KT, 32)
        gate_b = tiny(8)
        sgate = tiny(NT, 24)
        gcols = tiny(4, 32)
        a_old = tiny(32)
        k_cmp = tiny(64)
        v_cmp = tiny(2, HD)
        w2c = tiny(2, HD)
        pe_cols = tiny(2, 32)
        hbias = tiny(2, 2)
        freq = tiny(2)
        gm_col = tiny(2, KT)
        den, ssq4, rs4 = tiny(MH), tiny(MH), tiny(MH)
        nmax = tiny(4, 4)
        sums = tiny(2, 3, 4)
        rsum = tiny(3, 4)
        hop = tiny(2, parts=32)
        hop2 = tiny(3, parts=32)
        hop4 = tiny(8, 2, parts=4)
        hop5 = tiny(8, 2, parts=4)
        gm32 = tiny(1, parts=32)
        vec = view(V1 + 2048, P, parts=124)
        hid = temp(2, 2, 64)
        pos_i, pos_f, ang, turns = view(MKT, S).bitcast(I32), view(MKT + S, S), view(MKT + 2 * S, S), view(MKT + 3 * S, S)

        d_hop = nc.dram_tensor("d_hop", (32, 2), F32).ap()
        d_hop2 = nc.dram_tensor("d_hop2", (32, 2), F32).ap()
        d_nmx = nc.dram_tensor("d_nmx", (32, P), F32).ap()
        d_old = nc.dram_tensor("d_old", (32, 1), F32).ap()

        psum_ready = sem("psum_ready")
        bank_read = [sem(f"bank_read{i}") for i in range(8)]
        ring_in = [sem(f"ring_in{i}") for i in range(3)]
        ring_used = sem("ring_used")
        vec_in, x_in, const_in = sem("vec_in"), [sem(f"x_in{t}") for t in range(NT)], sem("const_in")
        wg_in = sem("wg_in")
        pool_const = sem("pool_const")
        sq_done, norm_ms, norm_sqrt, xn_done = sem("sq_done"), sem("norm_ms"), sem("norm_sqrt"), sem("xn_done")
        mod_ready = sem("mod_ready")
        silu_c = sem("silu_c")
        angle, trig = sem("angle"), sem("trig")
        swapped, roped = sem("swapped"), sem("roped")
        raw_ready, conv_done = sem("raw_ready"), sem("conv_done")
        gates_in_cols, gates_scanned = sem("gates_in_cols"), sem("gates_scanned")
        exp_f, ln_f = sem("exp_f"), sem("ln_f")
        exp_in, exp_out = sem("exp_in"), sem("exp_out")
        hop_out, hop_in = sem("hop_out"), sem("hop_in")
        sg_done = sem("sg_done")
        act_step, dve_step, pool_step = sem("act_step"), sem("dve_step"), sem("pool_step")
        stage_end = [sem(f"stage_end{c}") for c in "ABCDE"]
        hbias_ready, hid_ready = sem("hbias_ready"), sem("hid_ready")
        decay_in, decay_masked, decay_exp = sem("decay_in"), sem("decay_masked"), sem("decay_exp")
        wts_ready, h_ms, h_sqrt, state_zero = sem("wts_ready"), sem("h_ms"), sem("h_sqrt"), sem("state_zero")
        out_done = sem("out_done")

        small[0], late_end = masks_at, masks_end
        probs = {"s": [view(MKT + S * h, S) for h in range(4)],
                 "w": [view(MKT + 4 * S + 640 * h, 640) for h in range(4)],
                 "c": [view(KCT + HD * h, HD) for h in range(4)]}
        probs_T = [view(MKT + 4 * S + 4 * 640 + 512 * i, 512) for i in range(2)]
        out_T = view(MKT + 5 * S + 4 * 640, 512)
        scaled = view(KCT + 1280, 4, 2, HD)
        zero_row = view(KCT + 1792, 256)
        ones_sq, upper = view(MKT + 9472, P), view(MKT + 9600, P)
        E0 = MKT
        xt = [view(E0 + D * i, D) for i in range(2)]
        yT = [view(E0 + D * (2 + i), KT, P) for i in range(2)]
        y_row, junk_e = view(E0 + 4 * D, D), view(E0 + 5 * D, D)
        xn2 = [view(E0 + D * (6 + i), D) for i in range(2)]
        h2T = view(E0 + 8 * D, KT, P)
        logits = view(MKT + 9728, NT, 36)
        w_router = view(MKT + 10016, KT, 36)
        b_router = view(MKT + 10304, 36)
        zeros48 = view(MKT + 10340, 48).bitcast(I32)
        iota32, iota8, iota4 = view(MKT + 10388, NE), view(MKT + 10420, 8), view(MKT + 10428, 4)
        iota8m, iota4m = view(MKT + 10432, 8), view(MKT + 10440, 4)
        iota15 = view(MKT + 10444, NOV)
        tok_id = view(MKT + 10460, NT).bitcast(I32)
        x2 = view(QT, NT, D)
        gm_row, gf_row = view(VV, D), view(VV + D, D)
        diag = [yT[0], yT[1]]
        ys, rs_y, xs_, rs_x = tiny(1), tiny(1), tiny(1), tiny(1)
        gates2 = tiny(2, NT)
        dest = tiny(2, NT, dt=I32)
        slot = tiny(2, NT, dt=I32)
        row_tok = tiny(48, dt=I32)
        block_tab = tiny(64, parts=1, dt=I32)
        ra = [YM]

        def route(*shape, dt=F32):
            v = view(ra[0], *shape)
            ra[0] += int(np.prod(shape))
            assert ra[0] <= SMALL
            return v if dt is F32 else v.bitcast(dt)

        mg, sg_, ig, m1, i1, m2, i2, e2 = (route(NT) for _ in range(8))
        dg, eqg, ohg = route(NT, 4), route(NT, 4), route(NT, 4)
        lin, eqe, cand, oh1, oh2 = (route(NT, 8) for _ in range(5))
        prod = route(NT, 4, 8)
        hot = [route(NT, 4, 8) for _ in range(2)]
        hots, before, prefix, rank = route(NT, NE), route(NT, NE), route(NT, NE), route(NT, NE)
        total, over, over_inc, off_e, ones32 = (route(NE) for _ in range(5))
        rk, ex, ofs, big = route(2, NT), route(2, NT), route(2, NT), route(2, NT)
        ov_cmp = route(NOV, NE)
        tabf = route(64)
        laneslot = route(2, NT, dt=I32)
        w13 = [[view(W + 4096 * n, KT, FF) for n in range(2)] for W in (W0, W1)]
        w2s = [view(W + 8192, 4, D) for W in (W0, W1)]
        xg = [view(RING0 + D * i, D) for i in range(2)]
        xgT = [view(RING0 + D * (2 + i), KT, P) for i in range(2)]
        yo = [view(RING0 + D * (4 + i), D) for i in range(2)]
        act1 = [view(RING0 + D * 6 + 512 * i, FF) for i in range(2)]
        hid_e = [view(RING0 + D * 7 + 512 * i, FF) for i in range(2)]
        hid_T = [view(MQT + 512 * i, 4, P) for i in range(2)]
        idx_col = [tiny(1, dt=I32) for _ in range(2)]
        assert small[0] <= late_end
        NG = 4
        y1 = [view(W0 + D * i, D) for i in range(NG)]
        y2 = [view(W0 + D * (NG + i), D) for i in range(NG)]
        junk_g = view(W0 + 2 * NG * D, D)
        NB = 48
        d_xn = nc.dram_tensor("d_xn", (S, D), F32).ap()
        d_rt = nc.dram_tensor("d_rt", (P * NB, 1), I32).ap()
        d_y = nc.dram_tensor("d_y", (NB * P, D), F32).ap()

        scores_ready, row_max, probs_ready = sem("scores_ready"), sem("row_max"), sem("probs_ready")
        turned_ready, turned_read = sem("turned_ready"), [sem(f"turned_read{i}") for i in range(2)]
        pv_done, out_copied, heads_done = sem("pv_done"), sem("out_copied"), sem("heads_done")
        wout_scaled, pool_e, router_in, xt_in = sem("wout_scaled"), sem("pool_e"), sem("router_in"), [sem(f"xt_in{i}") for i in range(2)]
        diag_ready = sem("diag_ready")
        y_copied, y_sq, y_ms, y_sqrt, x2_done = sem("y_copied"), sem("y_sq"), sem("y_ms"), sem("y_sqrt"), sem("x2_done")
        x_sq, x_ms, x_sqrt, xn2_done = sem("x_sq"), sem("x_ms"), sem("x_sqrt"), sem("xn2_done")
        xn_stored = [sem(f"xn_stored{i}") for i in range(2)]
        x2T_read = sem("x2T_read")
        exp_args, exps_done, hots_ready, dest_ready = sem("exp_args"), sem("exps_done"), sem("hots_ready"), sem("dest_ready")
        rt_zeroed, rt_scattered, rt_in = sem("rt_zeroed"), sem("rt_scattered"), sem("rt_in")
        w13_in = [[sem(f"w{2 * n + 1}_in{i}") for n in range(2)] for i in range(2)]
        w2_in = [sem(f"w2_in{i}") for i in range(2)]
        idx_ready = [sem(f"idx_ready{i}") for i in range(2)]
        xg_in = [sem(f"xg_in{i}") for i in range(2)]
        xg_turned = [sem(f"xg_turned{i}") for i in range(2)]
        xgT_ready, yo_ready = [sem(f"xgT_ready{i}") for i in range(2)], [sem(f"yo_ready{i}") for i in range(2)]
        up_part, silu_part, hid_part = ([sem(f"{n}{i}") for i in range(2)] for n in ("up_part", "silu_part", "hid_part"))
        hid_turned, hidT_read = ([sem(f"{n}{i}") for i in range(2)] for n in ("hid_turned", "hidT_read"))
        down_done = [sem(f"down_done{i}") for i in range(2)]
        y_stored = [sem(f"y_stored{i}") for i in range(2)]
        stage_f, y_zeroed = sem("stage_f"), sem("y_zeroed")
        idx_seen, store_seen = sem("idx_seen"), sem("store_seen")
        y_in = [sem(f"y_in{i}") for i in range(4)]
        g_sq, g_ms, g_sqrt, g_done = sem("g_sq"), sem("g_ms"), sem("g_sqrt"), sem("g_done")
        out_stored = [sem(f"out_stored{i}") for i in range(4)]

        def key_blocks(x, kind):
            t = x // 2
            return [0] if kind == "c" else list(range(max(0, t - 4) if kind == "w" else 0, t + 1))

        def key_count(x, kind):
            return min(NCMP, 8 * (x // 2) + 7) if kind == "c" else P * len(key_blocks(x, kind))

        def heads_of(kind):
            return [None] if kind == "c" else [0, 1, 2, 3]

        EVENTS, UNIT, TURN, PV_AT, LAST_TURN = [], {}, {}, {}, {}

        def event(*e):
            if e[0] == "scores":
                UNIT[e[1:]] = len(UNIT)
            if e[0] in ("turn", "out_turn"):
                TURN[e] = len(TURN)
                LAST_TURN[e[1:3]] = len(TURN)
            if e[0] == "values":
                PV_AT[e[1:]] = len(PV_AT)
            EVENTS.append(e)

        phases = [(x, kind) for x in range(2 * NT) for kind in "csw"]
        for h in heads_of("c"):
            event("scores", 0, "c", h)
        for i, (x, kind) in enumerate(phases):
            blocks = key_blocks(x, kind)
            nxt = [(*phases[i + 1], h) for h in heads_of(phases[i + 1][1])] if i + 1 < len(phases) else []
            event("turn", x, kind, 0)
            if kind == "c" and x:
                event("out_turn", x - 1, "o")
            for b in range(len(blocks)):
                if b + 1 < len(blocks):
                    event("turn", x, kind, b + 1)
                for j, n in enumerate(nxt):
                    if j * len(blocks) // len(nxt) == b:
                        event("scores", *n)
                event("values", x, kind, b)
            if kind == "w":
                event("out_copy", x)
        event("out_turn", 2 * NT - 1, "o")

        def scores(u):
            return ps[:, 2 * (u % 2):2 * (u % 2) + 2, :].rearrange("p a b -> p (a b)")

        def evacuate_turned(eng, copy, e, mine):
            q = TURN[e]
            if q % 2 != mine:
                return
            _, x, kind, b = e
            eng.wait_ge(turned_ready, q + 1)
            if q >= 2:
                before = [PV_AT[f[1:]] for f in TURN if TURN[f] == q - 2 and f[0] == "turn"]
                if before:
                    eng.wait_ge(pv_done, before[0] + 1)
            rows = key_count(x, kind) if kind == "c" else P
            copy(probs_T[q % 2][0:rows, :], ps[0:rows, 4 + q % 2, :]).then_inc(turned_read[q % 2], 1)

        def bank(name):
            return ps[:, JOB[name] % 8, :]

        def claim(eng, name):
            j = JOB[name]
            if j >= 8:
                eng.wait_ge(bank_read[j % 8], j // 8)
            return bank(name)

        def ready(eng, name):
            eng.wait_ge(psum_ready, JOB[name] + 1)
            return bank(name)

        def read(ins, name):
            ins.then_inc(bank_read[JOB[name] % 8], 1)

        def was_read(eng, name):
            eng.wait_ge(bank_read[JOB[name] % 8], JOB[name] // 8 + 1)

        ring_total, ring_want = [0, 0, 0], []
        for i, it in enumerate(ITEMS):
            ring_total[i % 3] += 16 * len(it)
            ring_want.append(ring_total[i % 3])

        def end_stage(eng, k):
            eng.drain().then_inc(stage_end[k], 1)
            eng.wait_ge(stage_end[k], 4)

        def chain(eng, step):
            count = [0]

            def link(ins):
                count[0] += 1
                ins.then_inc(step, 1)
                eng.wait_ge(step, count[0])
            return link

        block = ctx.enter_context(nc.Block())

        last_job = [("ada", i) for i in range(4)] + [("q", 3, 1), ("vsl", 1), ("vwn", 1), ("mq", 3, 1), ("mk", 3, 1),
                                                     ("mv", NT - 1), ("mo", NT - 1)]
        last_job += [("ada", i) for i in range(4, 12)] + [("chid", 0, 1), ("chid", 1, 1)]

        @block.sync
        def _(sp):
            rows = [(0, "ada_b"), (48, "norm_mix_pre"), (56, "norm_mix_post"), (64, "norm_ffn_pre"),
                    (72, "norm_ffn_post"), (80, "c"), (88, "mlstm_head_norm")]
            for at_row, name in rows:
                src = d[name].rearrange("(r p) -> r p", p=P)
                sp.dma_start(vec[at_row:at_row + src.shape[0], :], src).then_inc(vec_in, 16)
            sp.dma_start(vec[92:124, :], d["mlstm_conv_w"].rearrange("j (r p) -> (j r) p", p=P)).then_inc(vec_in, 16)

            def load_ring(i):
                if i >= 3:
                    sp.wait_ge(psum_ready, JOB[last_job[i - 3]] + 1)
                for col, part, src in ITEMS[i]:
                    dst = ring[i % 3]
                    if i in (IT_CMP, IT_CMP + 1):
                        dst = dst.rearrange("p k n -> p (k n)").rearrange("p (k n) -> p k n", n=P)[part:part + HD]
                    sp.dma_start(dst[:, :, col:col + src.shape[2]], src).then_inc(ring_in[i % 3], 16)

            for i in range(3):
                load_ring(i)
            for t in range(NT):
                sp.dma_start(xn[:, t, :], d["x"][t * P:(t + 1) * P, :]).then_inc(x_in[t], 16)
            w_in = d["w_in"].rearrange("(k p) n -> p k n", p=P)
            with nc.allow_non_contiguous_dma(reason="small gate weights and columns, once"):
                sp.dma_start(wg[:, :, 0:8], w_in[:, :, OFF["mi"]:OFF["mi"] + 8]).then_inc(wg_in, 16)
                sp.dma_start(wg[:, :, 8:32], w_in[:, :, OFF["ng"]:OFF["ng"] + 24]).then_inc(wg_in, 16)
                for a, n in enumerate("kv"):
                    src = d["cmp_pe_" + n].rearrange("j d -> d j")
                    for half in range(2):
                        sp.dma_start(pe_cols[half * HD:(half + 1) * HD, a, :], src).then_inc(const_in, 16)
            sp.dma_start(w2c[:, 0, :], d["cmp_w2_k"]).then_inc(const_in, 16)
            sp.dma_start(w2c[:, 1, :], d["cmp_w2_v"]).then_inc(const_in, 16)
            sp.dma_start(gate_b, d["mlstm_gate_b"].broadcast_to([P, 8])).then_inc(const_in, 16)
            sp.dma_start(freq, d["rope_cols"]).then_inc(const_in, 16)
            sp.dma_start(pos_i, d["positions"].broadcast_to([P, S])).then_inc(const_in, 16)
            for i in range(3, IT_WOUT):
                load_ring(i)
            sp.wait_ge(stage_end[1], 4)
            sp.dma_start(bc, d_nmx.rearrange("r l -> (r l)").rearrange("(a n) -> a n", a=1).broadcast_to([P, 32 * P])
                         .rearrange("p (h c l) -> p h c l", h=MH, c=NT)).then_inc(decay_in, 16)
            sp.dma_start(a_old, d_old.rearrange("r a -> a r").broadcast_to([P, 32])).then_inc(decay_in, 16)
            for i in range(IT_WOUT, IT_WOUT + 2):
                load_ring(i)
            def load_expert(s, w1_, w3_, w2_):
                for n, src in enumerate((w1_, w3_)):
                    sp.dma_start(w13[s][n], src.rearrange("(k p) n -> p k n", p=P)).then_inc(w13_in[s][n], 16)
                sp.dma_start(w2s[s], w2_.rearrange("(k p) n -> p k n", p=P)).then_inc(w2_in[s], 16)

            sp.wait_ge(stage_end[2], 4)
            load_expert(0, d["expert_w1"][0], d["expert_w3"][0], d["expert_w2"][0])
            with nc.allow_non_contiguous_dma(reason="router weights, once"):
                sp.dma_start(w_router[:, :, 0:4], d["router_grp_w"].rearrange("(k p) n -> p k n", p=P)).then_inc(router_in, 16)
                sp.dma_start(w_router[:, :, 4:36], d["router_exp_w"].rearrange("(k p) n -> p k n", p=P)).then_inc(router_in, 16)
            sp.dma_start(b_router[:, 0:4], d["router_grp_b"].broadcast_to([P, 4])).then_inc(router_in, 16)
            sp.dma_start(b_router[:, 4:36], d["router_exp_b"].broadcast_to([P, NE])).then_inc(router_in, 16)
            sp.wait_ge(pool_e, 1)
            for b in range(NE, NB):
                sp.dma_start(d_y[b * P:(b + 1) * P, :].rearrange("p (a n) -> p a n", a=4),
                             zero_row.unsqueeze(1).broadcast_to([P, 4, 256])).then_inc(y_zeroed, 16)
            sp.dma_start(d_rt.rearrange("(p b) a -> p (b a)", p=P), zeros48).then_inc(rt_zeroed, 16)
            sp.wait_ge(stage_end[3], 4)
            for t in range(2):
                sp.dma_start(xt[t], d["x"][t * P:(t + 1) * P, :]).then_inc(xt_in[t], 16)
            for t in range(NT):
                sp.wait_ge(x2_done, t + 1)
                if t + 2 < NT:
                    sp.dma_start(xt[t % 2], d["x"][(t + 2) * P:(t + 3) * P, :]).then_inc(xt_in[t % 2], 16)
                sp.wait_ge(xn2_done, t + 1)
                sp.dma_start(d_xn[t * P:(t + 1) * P, :], xn2[t % 2]).then_inc(xn_stored[t % 2], 16)
            sp.wait_ge(stage_end[4], 4)
            load_expert(1, d["expert_w1"][1], d["expert_w3"][1], d["expert_w2"][1])
            sp_blocks = sp.value_load(block_tab[0:1, 48:49], min_val=NE, max_val=NB)
            with sp.Fori(1, NB // 2) as i:
                for s in range(2):
                    with sp.If(2 * i + s < sp_blocks):
                        e = sp.value_load(block_tab[0:1, bass.ds(2 * i + s, 1)], min_val=0, max_val=NE - 1)
                        sp.wait_ge(up_part[s], 2 * i + 1)
                        for n, name in enumerate(("expert_w1", "expert_w3")):
                            sp.dma_start(w13[s][n], d[name][bass.ds(e, 1)].rearrange("a (k p) n -> p (a k) n", p=P))\
                              .then_inc(w13_in[s][n], 16)
                        sp.wait_ge(down_done[s], i + 1)
                        sp.dma_start(w2s[s], d["expert_w2"][bass.ds(e, 1)].rearrange("a (k p) n -> p (a k) n", p=P))\
                          .then_inc(w2_in[s], 16)
            for t in range(NT):
                sp.wait_ge(g_done, t + 1)
                sp.dma_start(out[t * P:(t + 1) * P, :], y1[t % NG]).then_inc(out_stored[t % NG], 16)
            for s in range(NG):
                sp.wait_ge(out_stored[s], 16 * NT // NG)

        @block.gpsimd
        def _(pool):
            link = chain(pool, pool_step)
            link(nc.gpsimd.memset(ident, 0.0))
            link(nc.gpsimd.affine_select(out=ident, in_=ident, compare_op=ALU.not_equal, fill=1.0, base=0,
                                         pattern=[[-1, P]], channel_multiplier=1))
            link(nc.gpsimd.tensor_copy(ident_b, ident))
            link(nc.gpsimd.memset(causal, 0.0))
            link(nc.gpsimd.affine_select(out=causal, in_=causal, compare_op=ALU.is_ge, fill=NEG, base=0,
                                         pattern=[[-1, P]], channel_multiplier=1))
            link(nc.gpsimd.memset(behind, 0.0))
            link(nc.gpsimd.affine_select(out=behind, in_=behind, compare_op=ALU.is_gt, fill=NEG, base=0,
                                         pattern=[[1, P]], channel_multiplier=-1))
            link(nc.gpsimd.memset(cmask, 0.0))
            nc.gpsimd.affine_select(out=cmask, in_=cmask, compare_op=ALU.is_ge, fill=NEG, base=-31,
                                    pattern=[[P, NT], [-16, HD]], channel_multiplier=1).then_inc(pool_const, 1)
            end_stage(pool, 0)
            nc.gpsimd.memset(conv_raw[:, :, 0:3], 0.0).then_inc(pool_const, 1)
            pool.wait_ge(hop_out, 1)
            with nc.allow_non_contiguous_dma(reason="64 values each"):
                pool.dma_start(d_hop, hop).then_inc(hop_in, 16)
                pool.wait_ge(hop_in, 16)
                pool.dma_start(hop4, d_hop.rearrange("(h c) a -> h c a", h=MH)).then_inc(hop_in, 16)
                pool.wait_ge(hop_out, 2)
                pool.dma_start(d_hop2.rearrange("(h c) a -> h c a", h=MH), hop5).then_inc(hop_in, 16)
                pool.wait_ge(hop_in, 48)
                pool.dma_start(hop2[:, 0:2], d_hop2).then_inc(hop_in, 16)
                pool.wait_ge(exp_out, 1)
                pool.dma_start(d_nmx, neg_mx).then_inc(hop_in, 16)
                pool.dma_start(d_old, hop2[:, 2:3]).then_inc(hop_in, 16)
                pool.wait_ge(hop_in, 96)
            pool.wait_ge(roped, 14)
            nc.gpsimd.memset(v1[:, :, :, P:P + 1], MH_SCALE)
            end_stage(pool, 1)
            nc.gpsimd.memset(state, 0.0).then_inc(state_zero, 1)
            pool.wait_ge(decay_in, 32)
            for c in range(NT):
                nc.gpsimd.affine_select(out=bc[:, :, c, :], in_=bc[:, :, c, :], compare_op=ALU.is_ge, fill=NEG, base=0,
                                        pattern=[[0, MH], [1, P]], channel_multiplier=-1).then_inc(decay_masked, 1)
            end_stage(pool, 2)
            link(nc.gpsimd.memset(zero_row, 0.0))
            nc.gpsimd.memset(zeros48, 0).then_inc(pool_e, 1)
            link(nc.gpsimd.memset(ones_sq, 1.0))
            link(nc.gpsimd.affine_select(out=upper, in_=ones_sq, compare_op=ALU.is_gt, fill=0.0, base=0,
                                         pattern=[[1, P]], channel_multiplier=-1))
            for v_, n_, b_ in ((iota32, NE, 0), (iota8, 8, 0), (iota4, 4, 0), (iota8m, 8, -64), (iota4m, 4, -64),
                               (iota15, NOV, 0)):
                nc.gpsimd.iota(v_, [[1, n_]], base=b_, channel_multiplier=0, allow_small_or_imprecise_dtypes=True)
            link(nc.gpsimd.iota(tok_id, [[P, NT]], base=0, channel_multiplier=1))
            for n in range(2):
                pool.wait_ge(ring_in[(IT_WOUT + n) % 3], ring_want[IT_WOUT + n])
                for k in range(4):
                    w = ring[(IT_WOUT + n) % 3][:, k, :]
                    nc.gpsimd.tensor_scalar(w, w, cols[:, 88 + k:89 + k], None, ALU.mult).then_inc(wout_scaled, 1)
            pool.wait_ge(y_zeroed, 16 * (NB - NE))
            end_stage(pool, 3)
            pool.wait_ge(rt_zeroed, 16)
            pool.wait_ge(dest_ready, 1)
            for k in range(2):
                for t in range(NT):
                    pool.indirect_dma_start(d_rt, bass.IndirectOffsetOnAxis(ap=slot[:, k, t:t + 1], axis=0),
                                            tok_id[:, t:t + 1], None).then_inc(rt_scattered, 16)
            pool.wait_ge(rt_scattered, 16 * 2 * NT)
            pool.dma_start(row_tok, d_rt.rearrange("(p b) a -> p (b a)", p=P)).then_inc(rt_in, 16)
            pool.wait_ge(rt_in, 16)
            for s in range(2):
                pool.wait_ge(xn_stored[s], 16 * NT // 2)
            end_stage(pool, 4)
            p_blocks = pool.value_load(block_tab[0:1, 48:49], min_val=NE, max_val=NB)
            with pool.Fori(0, NB // 2) as i:
                for s in range(2):
                    with pool.If(2 * i + s < p_blocks):
                        pool.wait_ge(xg_turned[s], i + 1)
                        nc.gpsimd.tensor_copy(idx_col[s], row_tok[:, bass.ds(2 * i + s, 1)]).then_inc(idx_ready[s], 1)
                        pool.wait_ge(idx_ready[s], i + 1)
                        pool.sem_inc(idx_seen, 1)
                        pool.indirect_dma_start(xg[s], None, d_xn,
                                                bass.IndirectOffsetOnAxis(ap=idx_col[s], axis=0)).then_inc(xg_in[s], 16)
            pool.drain().then_inc(stage_f, 1)
            pool.wait_ge(stage_f, 4)
            for t in range(NT):
                if t >= NG:
                    pool.wait_ge(out_stored[t % NG], 16 * (t // NG))
                for k, y in enumerate((y1, y2)):
                    pool.indirect_dma_start(y[t % NG], None, d_y,
                                            bass.IndirectOffsetOnAxis(ap=dest[:, k, t:t + 1], axis=0)).then_inc(y_in[t % NG], 16)

        @block.scalar
        def _(act):
            link = chain(act, act_step)
            was_read(act, "vec")
            nc.scalar.activation(sc_col, cols[:, 80:88], ACT.Silu).then_inc(silu_c, 1)
            for c in range(CH):
                for t in range(4 * c, 4 * c + 4):
                    act.wait_ge(x_in[t], 16)
                    if t >= 2:
                        act.wait_ge(sq_done, t - 1)
                    nc.scalar.activation(junk[:, t % 2, :], xn[:, t, :], ACT.Square,
                                         accum_out=sum_sq[:, t:t + 1]).then_inc(sq_done, 1)
                act.wait_ge(norm_ms, c + 1)
                nc.scalar.activation(rstd[:, 4 * c:4 * c + 4], rstd[:, 4 * c:4 * c + 4], ACT.Sqrt).then_inc(norm_sqrt, 1)
            act.wait_ge(mod_ready, 1)
            for c in range(CH):
                for k in range(1, KT, 2):
                    b = ready(act, ("hT", c, k))
                    read(nc.scalar.activation(hT[:, k, 512 * c:512 * c + 512], b, ACT.Identity,
                                              scale=scale1[:, k:k + 1], bias=mod[:, k:k + 1]), ("hT", c, k))
            end_stage(act, 0)

            act.wait_ge(angle, 1)
            nc.scalar.activation(sin, sin, ACT.Sin).then_inc(trig, 1)
            act.wait_ge(angle, 2)
            nc.scalar.activation(cos, cos, ACT.Sin).then_inc(trig, 1)
            n_rope = [0]

            def silu_conv(m):
                act.wait_ge(conv_done, m + 1)
                x_ = (mqT, mkT)[m // 4][:, m % 4, :]
                nc.scalar.activation(x_, x_, ACT.Silu)

            def exchange_halves(name, scale):
                n = n_rope[0]
                b = ready(act, name)
                if n >= 2:
                    act.wait_ge(roped, n - 1)
                for q in range(4):
                    o = q ^ 1
                    last = nc.scalar.activation(swap[32 * q:32 * q + 32, n % 2, :], b[32 * o:32 * o + 32, :], ACT.Copy,
                                                scale=scale)
                last.then_inc(swapped, 1)
                n_rope[0] += 1

            was_read(act, "gates")
            nc.scalar.activation(sgate, gall[:, :, 8:32], ACT.Sigmoid).then_inc(sg_done, 1)
            for j in range(4):
                for c in range(CH):
                    exchange_halves(("q", j, c), HD ** -0.5)
            for n in ("kc", "ksl"):
                for c in range(CH):
                    exchange_halves((n, c), 1.0)
            act.wait_ge(exp_f, 1)
            link(nc.scalar.activation(t_a, abs_f, ACT.Exp, scale=-1.0))
            nc.scalar.activation(t_a, t_a, ACT.Ln, bias=1.0).then_inc(ln_f, 1)
            for c in range(CH):
                b = ready(act, ("vc", c))
                read(nc.scalar.copy(vcT[:, 512 * c:512 * c + 512], b), ("vc", c))
            for n, at_ in (("vsl", 0), ("vwn", 128)):
                if n == "vwn":
                    for c in range(CH):
                        exchange_halves(("kwn", c), 1.0)
                for c in range(CH):
                    b = ready(act, (n, c))
                    read(nc.scalar.copy(vv[:, 4 * c:4 * c + 4, at_:at_ + P], b.rearrange("p (t n) -> p t n", n=P)), (n, c))
            act.wait_ge(exp_in, 1)
            for n, (o, i_) in enumerate(((dec_, dec_), (em_, em_), (wp_, wp_), (hop2[:, 2:3], hop2[:, 2:3]))):
                last = nc.scalar.activation(o, i_, ACT.Exp)
            last.then_inc(exp_out, 1)
            act.wait_ge(pool_const, 2)
            for i, n in enumerate(("mq", "mk")):
                dst = (mqT, mkT)[i]
                for j in range(4):
                    m = 4 * i + j
                    if m >= 2:
                        act.wait_ge(conv_done, m - 1)
                    for c in range(CH):
                        b = ready(act, (n, j, c))
                        read(nc.scalar.copy(conv_raw[:, m % 2, 3 + 512 * c:515 + 512 * c], b), (n, j, c))
                    if m >= 1:
                        silu_conv(m - 1)
            silu_conv(7)
            act.wait_ge(roped, 14)
            for t in range(NT):
                b = ready(act, ("mv", t))
                read(nc.scalar.activation(v1[:, t, :, 0:P], b.rearrange("p (h n) -> p h n", h=MH), ACT.Copy,
                                          scale=MH_SCALE), ("mv", t))
            act.wait_ge(hop_in, 96)
            for t in range(NT):
                b = ready(act, ("mo", t))
                read(nc.scalar.activation(ym[:, t, :], b, ACT.Sigmoid), ("mo", t))
            end_stage(act, 1)

            for a in range(2):
                for g in range(2):
                    act.wait_ge(hbias_ready, 2 * a + g + 1)
                    b = ready(act, ("chid", a, g))
                    read(nc.scalar.activation(hid[:, a, g, 0:NCMP], b[:, 0:NCMP], ACT.Silu,
                                              bias=hbias[:, a, g:g + 1]), ("chid", a, g))
            b = ready(act, "vcmp")
            read(nc.scalar.copy(v_cmp[0:NCMP], b[0:NCMP, 0:P].rearrange("p (g n) -> p g n", g=2)), "vcmp")
            for c in range(NT):
                act.wait_ge(decay_masked, c + 1)
                for h in range(MH):
                    last = nc.scalar.activation(bc[:, h, c, :], bc[:, h, c, :], ACT.Exp,
                                                bias=gcols[:, 0, 8 * h + c:8 * h + c + 1])
                last.then_inc(decay_exp, 1)
            for c in range(NT):
                if c >= 2:
                    act.wait_ge(h_ms, c - 1)
                for p in range(2):
                    b = ready(act, ("num", c, p))
                    read(nc.scalar.copy(num[c % 2][:, 2 * p:2 * p + 2, :],
                                        b[:, 0:2 * (P + 1)].rearrange("p (h n) -> p h n", h=2)), ("num", c, p))
                act.wait_ge(h_ms, c + 1)
                nc.scalar.activation(rs4, ssq4, ACT.Sqrt).then_inc(h_sqrt, 1)
            end_stage(act, 2)
            for e in EVENTS:
                if e[0] == "scores":
                    _, x, kind, h = e
                    u, n = UNIT[e[1:]], key_count(x, kind)
                    act.wait_ge(row_max, u + 1)
                    if x:
                        act.wait_ge(turned_ready, LAST_TURN[(x - 1, kind)])
                    if x >= 2:
                        act.wait_ge(heads_done, x - 1)
                    k = "csw".index(kind)
                    if kind == "c":
                        for h in range(4):
                            last = nc.scalar.activation(probs["c"][h][:, 0:n], scores(u)[:, HD * h:HD * h + n], ACT.Exp,
                                                        bias=nmax[:, u % 4, h:h + 1], accum_out=sums[:, x % 2, k, h:h + 1])
                    else:
                        last = nc.scalar.activation(probs[kind][h][:, 0:n], scores(u)[:, 0:n], ACT.Exp,
                                                    bias=nmax[:, u % 4, 0:1], accum_out=sums[:, x % 2, k, h:h + 1])
                    last.then_inc(probs_ready, 1)
                if e[0] == "turn":
                    evacuate_turned(act, nc.scalar.copy, e, 0)
                if e[0] == "out_copy":
                    x = e[1]
                    act.wait_ge(pv_done, PV_AT[(x, "w", len(key_blocks(x, "w")) - 1)] + 1)
                    if x:
                        act.wait_ge(turned_ready, LAST_TURN[(x - 1, "o")])
                    nc.scalar.copy(out_T, ps[:, 6, :]).then_inc(out_copied, 1)
            end_stage(act, 3)

            def e_turned(t):
                b = ready(act, ("yT", t, 0))
                if t >= 2:
                    act.wait_ge(psum_ready, JOB[("out", t - 2, 1)] + 1)
                read(nc.scalar.copy(yT[t % 2][:, 0:4, :], b.rearrange("p (k n) -> p k n", n=P)), ("yT", t, 0))

            def e_router(t):
                b = ready(act, ("xT2", t, 0))
                if t >= 1:
                    act.wait_ge(psum_ready, JOB[("lg", t - 1)] + 1)
                for k in range(4):
                    last = nc.scalar.activation(h2T[:, k, :], b[:, P * k:P * k + P], ACT.Identity,
                                                scale=scale2[:, k:k + 1], bias=mod[:, 24 + k:25 + k])
                read(last, ("xT2", t, 0))

            e_turned(0)
            for t in range(NT):
                if t + 1 < NT:
                    e_turned(t + 1)
                if t:
                    act.wait_ge(x2_done, t)
                for n in range(2):
                    b = ready(act, ("out", t, n))
                    read(nc.scalar.copy(y_row[:, 512 * n:512 * n + 512], b), ("out", t, n))
                for n in range(2):
                    was_read(act, ("out", t, n))
                if t:
                    act.wait_ge(x_sq, t)
                nc.scalar.activation(junk_e, y_row, ACT.Square, accum_out=ys).then_inc(y_sq, 1)
                act.wait_ge(y_ms, t + 1)
                nc.scalar.activation(rs_y, ys, ACT.Sqrt).then_inc(y_sqrt, 1)
                act.wait_ge(x2_done, t + 1)
                act.wait_ge(y_sq, t + 1)
                nc.scalar.activation(junk_e, x2[:, t, :], ACT.Square, accum_out=xs_).then_inc(x_sq, 1)
                act.wait_ge(x_ms, t + 1)
                nc.scalar.activation(rs_x, xs_, ACT.Sqrt).then_inc(x_sqrt, 1)
                if t:
                    e_router(t - 1)
            e_router(NT - 1)
            act.wait_ge(exp_args, 1)
            nc.scalar.activation(dg, dg, ACT.Exp).then_inc(exps_done, 1)
            nc.scalar.activation(e2, e2, ACT.Exp).then_inc(exps_done, 1)
            end_stage(act, 4)

            for s in range(2):
                act.sem_inc(y_stored[s], 16)
            a_blocks = act.value_load(block_tab[0:1, 48:49], min_val=NE, max_val=NB)
            with act.Fori(0, NB // 2) as i:
                for s in range(2):
                    with act.If(2 * i + s < a_blocks):
                        act.wait_ge(up_part[s], 2 * i + 2)
                        nc.scalar.activation(act1[s], ps[:, 2, :], ACT.Silu).then_inc(silu_part[s], 1)
                        act.wait_ge(yo_ready[s], i + 2)
                        act.dma_start(d_y[bass.ds(256 * i + P * s, P), :], yo[s]).then_inc(y_stored[s], 16)
            act.wait_ge(y_stored[0], 16 * ((a_blocks + 1) // 2) + 16)
            act.sem_inc(store_seen, 1)
            act.wait_ge(y_stored[1], 16 * (a_blocks // 2) + 16)
            act.sem_inc(store_seen, 1)
            act.drain().then_inc(stage_f, 1)
            act.wait_ge(stage_f, 4)

            for t in range(NT):
                act.wait_ge(g_ms, 2 * t + 1)
                nc.scalar.activation(junk_g, y1[t % NG], ACT.Square, accum_out=ys).then_inc(g_sq, 1)
                act.wait_ge(g_ms, 2 * t + 2)
                nc.scalar.activation(rs_y, ys, ACT.Sqrt).then_inc(g_sqrt, 1)

        @block.tensor
        def _(pe):
            def last_of(ins):
                ins.then_inc(psum_ready, 1)

            def item(i):
                pe.wait_ge(ring_in[i % 3], ring_want[i])
                return ring[i % 3]

            def modulation(i, k_item):
                w = item(k_item)
                b = claim(pe, ("ada", i))
                for m in range(4):
                    for k in range(KT):
                        last = nc.tensor.matmul(b[:, m:m + 1], w[:, k, P * m:P * m + P], sc_col[:, k:k + 1],
                                                start=(k == 0), stop=(k == KT - 1))
                last_of(last)

            pe.wait_ge(vec_in, 128)
            pe.wait_ge(pool_const, 1)
            b = claim(pe, "vec")
            last_of(nc.tensor.transpose(b[:, 0:124], vec, ident[0:124, 0:124]))
            pe.wait_ge(silu_c, 1)
            for i in range(4):
                modulation(i, i)
            for c in range(CH):
                pe.wait_ge(xn_done, 4 * c + 4)
                for k in range(KT):
                    b = claim(pe, ("hT", c, k))
                    for t in range(4):
                        last = nc.tensor.transpose(b[:, P * t:P * t + P], xn[:, 4 * c + t, P * k:P * k + P], ident)
                    last_of(last)
            end_stage(pe, 0)

            def features(name, w, c):
                b = claim(pe, name)
                for k in range(KT):
                    last = nc.tensor.matmul(b, w(k), hT[:, k, 512 * c:512 * c + 512], start=(k == 0), stop=(k == KT - 1))
                last_of(last)

            def tokens(name, w, at_col, width, tiles):
                b = claim(pe, name)
                for n, t in enumerate(tiles):
                    for k in range(KT):
                        last = nc.tensor.matmul(b[:, n * width:(n + 1) * width], hT[:, k, P * t:P * t + P],
                                                w[:, k, at_col:at_col + width], start=(k == 0), stop=(k == KT - 1))
                last_of(last)

            pe.wait_ge(wg_in, 32)
            tokens("gates", wg, 0, 32, range(NT))
            w = item(IT_NQ)
            for j in range(4):
                for c in range(CH):
                    features(("q", j, c), lambda k: w[:, k, P * j:P * j + P], c)
            pe.wait_ge(gates_in_cols, 1)
            b = claim(pe, "gT")
            nc.tensor.transpose(b[0:32, 0:P], gi_cols.rearrange("p h c -> p (h c)"), ident)
            last_of(nc.tensor.transpose(b[0:32, P:2 * P], gf_cols.rearrange("p h c -> p (h c)"), ident))
            w = item(IT_KC)
            for n, at_ in (("kc", 0), ("ksl", 256), ("vc", 128)):
                for c in range(CH):
                    features((n, c), lambda k: w[:, k, at_:at_ + P], c)
            for c in range(CH):
                tokens(("vsl", c), w, 384, P, range(4 * c, 4 * c + 4))
            w = item(IT_KWN)
            for c in range(CH):
                features(("kwn", c), lambda k: w[:, k, 0:P], c)
            for c in range(CH):
                tokens(("vwn", c), w, P, P, range(4 * c, 4 * c + 4))
            pe.wait_ge(exp_out, 1)
            b = claim(pe, "gcol")
            for n, a in enumerate((u_, dec_, em_, wp_)):
                last = nc.tensor.transpose(b[:, 32 * n:32 * n + 32], a, ident[0:32, 0:32])
            last_of(last)
            for n, it in (("mq", IT_MQ), ("mk", IT_MK)):
                w = item(it)
                for j in range(4):
                    for c in range(CH):
                        features((n, j, c), lambda k: w[:, k, P * j:P * j + P], c)
            for n, it in (("mv", IT_MV), ("mo", IT_MO)):
                w = item(it)
                for t in range(NT):
                    tokens((n, t), w, 0, 512, [t])
            for i in range(4, 12):
                modulation(i, IT_ADA2 + i - 4)
            end_stage(pe, 1)

            pe.wait_ge(const_in, 144)
            for a in range(2):
                w = item(IT_CMP + a).rearrange("p k n -> p (k n)").rearrange("p (k n) -> p k n", n=P)
                src = (kcT, vcT)[a]
                for g in range(2):
                    half = slice(HD * g, HD * g + HD)
                    b = claim(pe, ("chid", a, g))
                    for j in range(32):
                        nc.tensor.matmul(b[:, 0:NCMP], w[half, j, :], src[half, j:j + 16 * (NCMP - 1) + 1:16],
                                         start=(j == 0), stop=(j == 31))
                    for j in range(32):
                        last = nc.tensor.matmul(b[:, 64:65], w[half, j, :], pe_cols[half, a, j:j + 1],
                                                start=(j == 0), stop=(j == 31))
                    last_of(last)
            was_read(pe, ("chid", 0, 1))
            b = claim(pe, "kcmp")
            for g in range(2):
                last = nc.tensor.matmul(b[HD * g:HD * g + HD, 0:NCMP], w2c[:, 0, :], hid[:, 0, g, 0:NCMP],
                                        start=True, stop=True)
            last_of(last)
            was_read(pe, ("chid", 1, 1))
            b = claim(pe, "vcmp")
            for g in range(2):
                last = nc.tensor.matmul(b[0:NCMP, HD * g:HD * g + HD], hid[:, 1, g, 0:NCMP], w2c[:, 1, :],
                                        start=True, stop=True)
            last_of(last)
            pe.wait_ge(state_zero, 1)
            for c in range(NT):
                at_c = slice(P * c, P * c + P)
                b = claim(pe, ("S", c))
                for h in range(MH):
                    last = nc.tensor.matmul(b[:, P * h:P * h + P], mkT[:, h, at_c], mqT[:, h, at_c], start=True, stop=True)
                last_of(last)
                b = claim(pe, ("kr", c))
                for h in range(MH):
                    last = nc.tensor.transpose(b[:, P * h:P * h + P], mkT[:, h, at_c], ident)
                last_of(last)
                was_read(pe, ("S", c))
                for p in range(2):
                    b = claim(pe, ("num", c, p))
                    for h in range(2):
                        last = nc.tensor.matmul(b[:, 129 * h:129 * h + 129], wts[c % 2][:, 2 * p + h, :],
                                                v1[:, c, 2 * p + h, :], start=True, stop=True)
                    last_of(last)
                if c:
                    was_read(pe, ("kv", c - 1, 1))
                for p in range(2):
                    b = claim(pe, ("int", c, p))
                    for h in range(2):
                        last = nc.tensor.matmul(b[:, 129 * h:129 * h + 129], mqT[:, 2 * p + h, at_c],
                                                state[:, 2 * p + h, :], start=True, stop=True)
                    last_of(last)
                was_read(pe, ("kr", c))
                for p in range(2):
                    b = claim(pe, ("kv", c, p))
                    for h in range(2):
                        last = nc.tensor.matmul(b[:, 129 * h:129 * h + 129], kw[c % 2][:, 2 * p + h, :],
                                                v1[:, c, 2 * p + h, :], start=True, stop=True)
                    last_of(last)
            end_stage(pe, 2)
            def free_turn_bank(q):
                if q >= 2:
                    f = [f for f in TURN if TURN[f] == q - 2][0]
                    if f[0] == "out_turn":
                        pe.wait_ge(heads_done, f[1] + 1)
                    else:
                        pe.wait_ge(turned_read[q % 2], sum(1 for g in TURN if g[0] == "turn" and TURN[g] % 2 == q % 2 and TURN[g] < q))
                return ps[:, 4 + q % 2, :]

            for e in EVENTS:
                if e[0] == "scores":
                    _, x, kind, h = e
                    t, g = divmod(x, 2)
                    u, n = UNIT[e[1:]], key_count(x, kind)
                    half = slice(HD * g, HD * g + HD)
                    sc = scores(u)
                    if u >= 2:
                        pe.wait_ge(probs_ready, u - 1)
                    if kind == "c":
                        for h in range(4):
                            nc.tensor.matmul(sc[:, HD * h:HD * h + n], qT[half, h, P * t:P * t + P], k_cmp[half, 0:n],
                                             start=True, stop=False)
                            last = nc.tensor.matmul(sc[:, HD * h:HD * h + n], ident_b, cmask[:, t, 0:n], start=False, stop=True)
                    else:
                        src = kslT if kind == "s" else kwnT
                        first = key_blocks(x, kind)[0]
                        for at_ in range(0, n, 512):
                            w = min(512, n - at_)
                            far = kind == "w" and t >= 4 and at_ == 0
                            near = at_ + w == n
                            last = nc.tensor.matmul(sc[:, at_:at_ + w], qT[half, h, P * t:P * t + P],
                                                    src[half, P * first + at_:P * first + at_ + w],
                                                    start=True, stop=not (near or far))
                            if far:
                                last = nc.tensor.matmul(sc[:, 0:P], ident_b, behind, start=False, stop=not near)
                            if near:
                                last = nc.tensor.matmul(sc[:, n - P:n], ident_b, causal, start=False, stop=True)
                    last.then_inc(scores_ready, 1)
                if e[0] == "turn":
                    _, x, kind, b = e
                    bank_ = free_turn_bank(TURN[e])
                    n = key_count(x, kind)
                    if b == 0:
                        pe.wait_ge(probs_ready, UNIT[(x, kind, heads_of(kind)[-1])] + 1)
                    for h in range(4):
                        w = n if kind == "c" else P
                        last = nc.tensor.transpose(bank_[0:w, P * h:P * h + P], probs[kind][h][:, P * b:P * b + w], ident)
                    last.then_inc(turned_ready, 1)
                if e[0] == "values":
                    _, x, kind, b = e
                    t, g = divmod(x, 2)
                    q = TURN[("turn", x, kind, b)]
                    pe.wait_ge(turned_read[q % 2], sum(1 for f in TURN if f[0] == "turn" and TURN[f] % 2 == q % 2 and TURN[f] <= q))
                    if kind == "c":
                        if x:
                            pe.wait_ge(heads_done, x)
                        n = key_count(x, kind)
                        for h in range(4):
                            last = nc.tensor.matmul(ps[:, 7, HD * h:HD * h + HD], probs_T[q % 2][0:n, P * h:P * h + P],
                                                    v_cmp[0:n, g, :], start=True, stop=True)
                    else:
                        if x and kind == "s" and b == 0:
                            pe.wait_ge(out_copied, x)
                        lo = HD * "sw".index(kind)
                        blocks = key_blocks(x, kind)
                        last = nc.tensor.matmul(ps[lo:lo + HD, 6, :], vv[:, blocks[b], 2 * lo + HD * g:2 * lo + HD * g + HD],
                                                probs_T[q % 2], start=(b == 0), stop=(b == len(blocks) - 1))
                    last.then_inc(pv_done, 1)
                if e[0] == "out_turn":
                    x = e[1]
                    bank_ = free_turn_bank(TURN[e])
                    pe.wait_ge(out_copied, x + 1)
                    for h in range(4):
                        last = nc.tensor.transpose(bank_[:, P * h:P * h + P], out_T[:, P * h:P * h + P], ident)
                    last.then_inc(turned_ready, 1)
            end_stage(pe, 3)

            pe.wait_ge(diag_ready, 1)
            for i in range(2):
                dgr = diag[i].rearrange("p k n -> p (k n)")
                for n in range(2):
                    b = claim(pe, ("row", i, n))
                    last_of(nc.tensor.matmul(b, ones_sq, dgr[:, 512 * n:512 * n + 512], start=True, stop=True))

            def e_turn(t):
                for n, y in enumerate((ym, yn)):
                    b = claim(pe, ("yT", t, n))
                    for k in range(4):
                        last = nc.tensor.transpose(b[:, P * k:P * k + P], y[:, t, P * k:P * k + P], ident)
                    last_of(last)

            def e_router(t):
                pe.wait_ge(xn2_done, t + 1)
                for n in range(2):
                    b = claim(pe, ("xT2", t, n))
                    for k in range(4):
                        last = nc.tensor.transpose(b[:, P * k:P * k + P], xn2[t % 2][:, P * (4 * n + k):P * (4 * n + k) + P], ident)
                    last_of(last)
                b = claim(pe, ("lg", t))
                for n in range(2):
                    was_read(pe, ("xT2", t, n))
                for k in range(KT):
                    last = nc.tensor.matmul(b[:, 0:36], h2T[:, k, :], w_router[:, k, :], start=(k == 0), stop=(k == KT - 1))
                last_of(last)

            pe.wait_ge(router_in, 64)
            pe.wait_ge(wout_scaled, 8)
            e_turn(0)
            for t in range(NT):
                if t + 1 < NT:
                    e_turn(t + 1)
                for n in range(2):
                    was_read(pe, ("yT", t, n))
                for n in range(2):
                    b = claim(pe, ("out", t, n))
                    w = ring[(IT_WOUT + n) % 3]
                    for k in range(KT):
                        last = nc.tensor.matmul(b, yT[t % 2][:, k, :], w[:, k, :], start=(k == 0), stop=(k == KT - 1))
                    last_of(last)
                if t:
                    e_router(t - 1)
            e_router(NT - 1)
            pe.wait_ge(hots_ready, 1)
            b = claim(pe, "rank")
            hv = hots.rearrange("p t e -> p (t e)")
            nc.tensor.matmul(b[:, 0:256], upper, hv, start=True, stop=True)
            last_of(nc.tensor.matmul(b[:, 256:512], ones_sq, hv, start=True, stop=True))
            end_stage(pe, 4)

            def f_turn(s, n, other):
                pe.wait_ge(xg_in[s], 16 * n + 16)
                if other is not None:
                    pe.wait_ge(xgT_ready[1 - s], other)
                for k in range(KT):
                    last = nc.tensor.transpose(ps[:, k // 4, P * (k % 4):P * (k % 4) + P], xg[s][:, P * k:P * k + P], ident)
                last.then_inc(xg_turned[s], 1)

            e_blocks = pe.value_load(block_tab[0:1, 48:49], min_val=NE, max_val=NB)
            for s in range(2):
                for credit in (up_part, xg_turned, down_done):
                    pe.sem_inc(credit[s], 1)
            f_turn(0, 0, None)
            with pe.Fori(0, NB // 2) as i:
                for s in range(2):
                    with pe.If(2 * i + s < e_blocks):
                        pe.wait_ge(xgT_ready[s], i + 1)
                        for n in range(2):
                            pe.wait_ge(w13_in[s][n], 16 * i + 16)
                            for k in range(KT):
                                last = nc.tensor.matmul(ps[:, 2 + n, :], xgT[s][:, k, :], w13[s][n][:, k, :],
                                                        start=(k == 0), stop=(k == KT - 1))
                            last.then_inc(up_part[s], 1)
                    with pe.If(2 * i + s + 1 < e_blocks):
                        f_turn(1 - s, i + s, i + 1)
                    with pe.If(2 * i + s < e_blocks):
                        pe.wait_ge(hid_part[s], i + 1)
                        for k in range(4):
                            last = nc.tensor.transpose(ps[:, 4 + k // 2, P * (k % 2):P * (k % 2) + P],
                                                       hid_e[s][:, P * k:P * k + P], ident)
                            if k % 2:
                                last.then_inc(hid_turned[s], 1)
                        pe.wait_ge(w2_in[s], 16 * i + 16)
                        pe.wait_ge(yo_ready[1 - s], i + s + 1)
                        for k in range(4):
                            if k % 2 == 0:
                                pe.wait_ge(hidT_read[s], 2 * i + 1 + k // 2)
                            for n in range(2):
                                last = nc.tensor.matmul(ps[:, 6 + n, :], hid_T[s][:, k, :], w2s[s][:, k, 512 * n:512 * n + 512],
                                                        start=(k == 0), stop=(k == 3))
                        last.then_inc(down_done[s], 1)
            pe.drain().then_inc(stage_f, 1)

        @block.vector
        def _(dve):
            link = chain(dve, dve_step)
            V = nc.vector
            b = ready(dve, "vec")
            read(V.tensor_copy(cols, b[:, 0:124]), "vec")
            was_read(dve, "vec")
            for c in range(CH):
                dve.wait_ge(sq_done, 4 * c + 4)
                V.tensor_scalar(rstd[:, 4 * c:4 * c + 4], sum_sq[:, 4 * c:4 * c + 4], 1.0 / D, EPS,
                                ALU.mult, ALU.add).then_inc(norm_ms, 1)
                dve.wait_ge(norm_sqrt, c + 1)
                link(V.reciprocal(rstd[:, 4 * c:4 * c + 4], rstd[:, 4 * c:4 * c + 4]))
                for t in range(4 * c, 4 * c + 4):
                    V.tensor_scalar(xn[:, t, :], xn[:, t, :], rstd[:, t:t + 1], None, ALU.mult).then_inc(xn_done, 1)

            def modulation(i):
                b = ready(dve, ("ada", i))
                read(V.tensor_tensor(mod[:, 4 * i:4 * i + 4], b[:, 0:4], cols[:, 4 * i:4 * i + 4], ALU.add), ("ada", i))

            for i in range(4):
                modulation(i)
            was_read(dve, ("ada", 3))
            V.scalar_tensor_tensor(scale1, mod[:, 8:16], 1.0, cols[:, 48:56], ALU.add, ALU.mult).then_inc(mod_ready, 1)
            dve.wait_ge(mod_ready, 1)
            for c in range(CH):
                for k in range(0, KT, 2):
                    b = ready(dve, ("hT", c, k))
                    read(V.tensor_scalar(hT[:, k, 512 * c:512 * c + 512], b, scale1[:, k:k + 1], mod[:, k:k + 1],
                                         ALU.mult, ALU.add), ("hT", c, k))
            dve.wait_ge(const_in, 144)
            link(V.tensor_copy(pos_f, pos_i))
            link(V.tensor_scalar(ang, pos_f, freq[:, 0:1], None, ALU.mult))
            for n, (dst, turn, back) in enumerate(((sin, 0.0, 0.0), (cos, 0.25, float(np.pi / 2)))):
                link(V.tensor_scalar(turns, ang, 1.0 / TWO_PI, turn, ALU.mult, ALU.add))
                link(V.tensor_scalar(turns, turns, ROUND, None, ALU.add))
                link(V.tensor_scalar(turns, turns, ROUND, None, ALU.subtract))
                link(V.scalar_tensor_tensor(dst, turns, -PI2[0], ang, ALU.mult, ALU.add))
                link(V.scalar_tensor_tensor(dst, turns, -PI2[1], dst, ALU.mult, ALU.add))
                link(V.scalar_tensor_tensor(dst, turns, -PI2[2], dst, ALU.mult, ALU.add))
                link(V.tensor_scalar(dst, dst, back, PI_IN, ALU.add, ALU.min))
                V.tensor_scalar(dst, dst, -PI_IN, None, ALU.max).then_inc(angle, 1)
            end_stage(dve, 0)

            dve.wait_ge(trig, 1)
            link(V.tensor_scalar(sin, sin, freq[:, 1:2], None, ALU.mult))
            dve.wait_ge(trig, 2)
            b = ready(dve, "gates")
            read(V.tensor_copy(gall, b[:, 0:256].rearrange("p (t n) -> p t n", n=32)), "gates")
            was_read(dve, "gates")
            g = gall.rearrange("p c n -> p n c")
            V.tensor_tensor(gi_cols, g[:, 0:MH, :], gate_b[:, 0:MH].unsqueeze(2).broadcast_to([P, MH, NT]), ALU.add)
            V.tensor_tensor(gf_cols, g[:, MH:2 * MH, :], gate_b[:, MH:2 * MH].unsqueeze(2).broadcast_to([P, MH, NT]),
                            ALU.add).then_inc(gates_in_cols, 1)
            n_rope = [0]

            def rope(name, dst, c, scale):
                n = n_rope[0]
                dve.wait_ge(swapped, n + 1)
                b = ready(dve, name)
                read(V.scalar_tensor_tensor(turned[:, n % 2, :], b, scale, cos[:, 512 * c:512 * c + 512],
                                            ALU.mult, ALU.mult), name)
                link(V.tensor_tensor(swap[:, n % 2, :], swap[:, n % 2, :], sin[:, 512 * c:512 * c + 512], ALU.mult))
                was_read(dve, name)
                V.tensor_tensor(dst[:, 512 * c:512 * c + 512], turned[:, n % 2, :], swap[:, n % 2, :],
                                ALU.add).then_inc(roped, 1)
                n_rope[0] += 1

            for j in range(4):
                for c in range(CH):
                    rope(("q", j, c), qT[:, j, :], c, HD ** -0.5)
            b = ready(dve, "gT")
            V.tensor_copy(g_i, b[0:32, 0:P])
            read(V.tensor_copy(g_f, b[0:32, P:2 * P]), "gT")
            was_read(dve, "gT")
            V.scalar_tensor_tensor(abs_f, g_f, -1.0, g_f, ALU.mult, ALU.max).then_inc(exp_f, 1)
            for n, dst in (("kc", kcT), ("ksl", kslT)):
                for c in range(CH):
                    rope((n, c), dst, c, 1.0)
            link(V.memset(ones_r, 1.0))
            dve.wait_ge(ln_f, 1)
            link(V.scalar_tensor_tensor(g_f, g_f, 0.0, t_a, ALU.min, ALU.subtract))
            link(V.tensor_tensor_scan(decay_b, ones_r, g_f, 0.0, ALU.mult, ALU.add))
            link(V.tensor_tensor(u_, g_i, decay_b, ALU.subtract))
            link(V.tensor_tensor_scan(cmax, u_, u_, -3e38, ALU.max, ALU.max))
            V.tensor_copy(hop[:, 0:1], decay_b[:, P - 1:P])
            V.tensor_tensor(hop[:, 1:2], decay_b[:, P - 1:P], cmax[:, P - 1:P], ALU.add).then_inc(hop_out, 1)
            for c in range(CH):
                rope(("kwn", c), kwnT, c, 1.0)
            dve.wait_ge(hop_in, 32)
            link(V.memset(hop5, 0.0))
            link(V.tensor_tensor_scan(hop5[:, :, 1], hop4[:, :, 0], hop4[:, :, 1], 0.0, ALU.add, ALU.max))
            V.tensor_copy(hop5[:, 1:8, 0], hop5[:, 0:7, 1]).then_inc(hop_out, 1)
            dve.wait_ge(hop_in, 64)
            m_old, m_new = hop2[:, 0:1], hop2[:, 1:2]
            link(V.tensor_scalar(mx, cmax, m_old, None, ALU.max))
            V.tensor_scalar(neg_mx, mx, -1.0, None, ALU.mult)
            V.tensor_scalar(dec_, mx, -1.0, m_old, ALU.mult, ALU.add)
            link(V.tensor_tensor(gm32, hop[:, 0:1], m_new, ALU.subtract))
            link(V.scalar_tensor_tensor(em_, mx, -1.0, decay_b, ALU.mult, ALU.subtract))
            link(V.tensor_scalar(wp_, u_, gm32, None, ALU.add))
            V.tensor_tensor(hop2[:, 2:3], gm32, m_old, ALU.add).then_inc(exp_in, 1)
            dve.wait_ge(exp_out, 1)
            b = ready(dve, "gcol")
            read(V.tensor_copy(gcols, b[:, 0:P].rearrange("p (a r) -> p a r", a=4)), "gcol")
            for i, n in enumerate(("mq", "mk")):
                dst = (mqT, mkT)[i]
                for j in range(4):
                    m = 4 * i + j
                    was_read(dve, (n, j, 0))
                    was_read(dve, (n, j, 1))
                    tap = lambda s: cols[:, 92 + 8 * s + m:93 + 8 * s + m]
                    link(V.tensor_scalar(dst[:, j, :], conv_raw[:, m % 2, 0:S], tap(0), None, ALU.mult))
                    for s in range(1, 4):
                        ins = V.scalar_tensor_tensor(dst[:, j, :], conv_raw[:, m % 2, s:s + S], tap(s), dst[:, j, :],
                                                     ALU.mult, ALU.add)
                        if s < 3:
                            link(ins)
                    ins.then_inc(conv_done, 1)
            for i in range(4, 12):
                modulation(i)
            end_stage(dve, 1)

            link(V.scalar_tensor_tensor(scale2, mod[:, 32:40], 1.0, cols[:, 64:72], ALU.add, ALU.mult))
            link(V.tensor_tensor(gm_col[:, 0, :], mod[:, 16:24], cols[:, 56:64], ALU.mult))
            link(V.tensor_tensor(gm_col[:, 1, :], mod[:, 40:48], cols[:, 72:80], ALU.mult))
            for a in range(2):
                for g in range(2):
                    b = ready(dve, ("chid", a, g))
                    V.tensor_copy(hbias[:, a, g:g + 1], b[:, 64:65]).then_inc(hbias_ready, 1)
            b = ready(dve, "kcmp")
            read(V.tensor_copy(k_cmp[:, 0:NCMP], b[:, 0:NCMP]), "kcmp")
            for c in range(NT):
                decay = bc[:, :, c, :]
                dve.wait_ge(decay_exp, c + 1)
                b = ready(dve, ("S", c))
                if c >= 2:
                    dve.wait_ge(psum_ready, JOB[("kv", c - 2, 1)] + 1)
                read(V.tensor_tensor(wts[c % 2], b.rearrange("p (h n) -> p h n", h=MH), decay, ALU.mult), ("S", c))
                b = ready(dve, ("kr", c))
                col = lambda a: gcols[:, a, c:32:8]
                read(V.tensor_tensor(kw[c % 2], b.rearrange("p (h n) -> p h n", h=MH),
                                     col(3).unsqueeze(2).broadcast_to([P, MH, P]), ALU.mult), ("kr", c))
                n_ = num[c % 2]
                for p in range(2):
                    was_read(dve, ("num", c, p))
                for p in range(2):
                    b = ready(dve, ("int", c, p))
                    for h in range(2):
                        last = V.scalar_tensor_tensor(n_[:, 2 * p + h, :], b[:, 129 * h:129 * h + 129],
                                                      gcols[:, 1, 8 * (2 * p + h) + c:8 * (2 * p + h) + c + 1],
                                                      n_[:, 2 * p + h, :], ALU.mult, ALU.add)
                    read(last, ("int", c, p))
                for p in range(2):
                    b = ready(dve, ("kv", c, p))
                    for h in range(2):
                        r = 8 * (2 * p + h) + c
                        last = V.scalar_tensor_tensor(state[:, 2 * p + h, :], state[:, 2 * p + h, :], a_old[:, r:r + 1],
                                                      b[:, 129 * h:129 * h + 129], ALU.mult, ALU.add)
                    read(last, ("kv", c, p))
                was_read(dve, ("int", c, 1))
                dn = n_[:, :, P]
                link(V.scalar_tensor_tensor(den, dn, -1.0, dn, ALU.mult, ALU.max))
                link(V.tensor_tensor(den, den, col(2), ALU.max))
                link(V.reciprocal(den, den))
                link(V.tensor_tensor(hh, n_[:, :, 0:P], den.unsqueeze(2).broadcast_to([P, MH, P]), ALU.mult))
                link(V.tensor_tensor(sq, hh, hh, ALU.mult))
                link(V.tensor_reduce(ssq4, sq, AX.X, ALU.add))
                V.tensor_scalar(ssq4, ssq4, 1.0 / P, EPS, ALU.mult, ALU.add).then_inc(h_ms, 1)
                dve.wait_ge(h_sqrt, c + 1)
                link(V.reciprocal(rs4, rs4))
                link(V.tensor_tensor(hh, hh, rs4.unsqueeze(2).broadcast_to([P, MH, P]), ALU.mult))
                y = ym[:, c, :].rearrange("p (h n) -> p h n", h=MH)
                link(V.tensor_tensor(y, y, hh, ALU.mult))
            end_stage(dve, 2)
            for e in EVENTS:
                if e[0] == "scores":
                    _, x, kind, h = e
                    u, n = UNIT[e[1:]], key_count(x, kind)
                    dve.wait_ge(scores_ready, u + 1)
                    if u >= 4:
                        dve.wait_ge(probs_ready, u - 3)
                    if kind == "c":
                        m = nmax[:, u % 4, :]
                        ins = V.tensor_reduce(m, scores(u)[:, 0:4 * HD].rearrange("p (h n) -> p h n", h=4)[:, :, 0:n], AX.X,
                                              ALU.max, negate=True)
                        if x < 2:
                            link(ins)
                            ins = V.tensor_scalar(m, m, 1e20, None, ALU.min)
                    else:
                        ins = V.tensor_reduce(nmax[:, u % 4, 0:1], scores(u)[:, 0:n], AX.X, ALU.max, negate=True)
                    ins.then_inc(row_max, 1)
                if e[0] == "turn":
                    evacuate_turned(dve, V.tensor_copy, e, 1)
                if e[0] == "out_turn":
                    x = e[1]
                    t, g = divmod(x, 2)
                    dve.wait_ge(probs_ready, UNIT[(x, "w", 3)] + 1)
                    s_ = sums[:, x % 2]
                    if t == 0:
                        link(V.tensor_scalar(s_[:, 0, :], s_[:, 0, :], 1e-30, None, ALU.max))
                    link(V.reciprocal(rsum, s_))
                    link(V.tensor_tensor(rsum, rsum, sgate[:, t, 12 * g:12 * g + 12].rearrange("p (h k) -> p k h", k=3), ALU.mult))
                    y = yn[:, t, 256 * g:256 * g + 256].rearrange("p (h n) -> p h n", h=4)
                    dve.wait_ge(pv_done, PV_AT[(x, "c", 0)] + 1)
                    V.tensor_tensor(y, ps[:, 7, 0:4 * HD].rearrange("p (h n) -> p h n", h=4),
                                    rsum[:, 0, :].unsqueeze(2).broadcast_to([P, 4, HD]), ALU.mult)
                    q = TURN[e]
                    dve.wait_ge(turned_ready, q + 1)
                    ins = V.tensor_tensor(scaled, ps[:, 4 + q % 2, :].rearrange("p (h k n) -> p h k n", h=4, k=2),
                                          rsum[:, 1:3, :].rearrange("p k h -> p h k").unsqueeze(3).broadcast_to([P, 4, 2, HD]),
                                          ALU.mult)
                    ins.then_inc(heads_done, 1)
                    dve.wait_ge(heads_done, x + 1)
                    link(V.tensor_tensor(y, y, scaled[:, :, 0, :], ALU.add))
                    link(V.tensor_tensor(y, y, scaled[:, :, 1, :], ALU.add))
            end_stage(dve, 3)

            bc_id = ident.unsqueeze(1).broadcast_to([P, KT, P])
            for i in range(2):
                ins = V.tensor_tensor(diag[i], bc_id, gm_col[:, i, :].unsqueeze(2).broadcast_to([P, KT, P]), ALU.mult)
            ins.then_inc(diag_ready, 1)
            for i, dst in enumerate((gm_row, gf_row)):
                for n in range(2):
                    b = ready(dve, ("row", i, n))
                    read(V.tensor_copy(dst[:, 512 * n:512 * n + 512], b), ("row", i, n))
            for n in range(2):
                was_read(dve, ("row", 1, n))

            def e_turned(t):
                b = ready(dve, ("yT", t, 1))
                if t >= 2:
                    dve.wait_ge(psum_ready, JOB[("out", t - 2, 1)] + 1)
                read(V.tensor_copy(yT[t % 2][:, 4:8, :], b.rearrange("p (k n) -> p k n", n=P)), ("yT", t, 1))

            def e_router(t):
                b = ready(dve, ("xT2", t, 1))
                if t >= 1:
                    dve.wait_ge(psum_ready, JOB[("lg", t - 1)] + 1)
                for k in range(4, 8):
                    last = V.tensor_scalar(h2T[:, k, :], b[:, P * (k - 4):P * (k - 4) + P], scale2[:, k:k + 1],
                                           mod[:, 24 + k:25 + k], ALU.mult, ALU.add)
                read(last, ("xT2", t, 1))
                b = ready(dve, ("lg", t))
                read(V.tensor_tensor(logits[:, t, :], b[:, 0:36], b_router, ALU.add), ("lg", t))

            e_turned(0)
            dve.wait_ge(router_in, 64)
            for t in range(NT):
                if t + 1 < NT:
                    e_turned(t + 1)
                dve.wait_ge(y_sq, t + 1)
                V.tensor_scalar(ys, ys, 1.0 / D, EPS, ALU.mult, ALU.add).then_inc(y_ms, 1)
                dve.wait_ge(y_sqrt, t + 1)
                link(V.reciprocal(rs_y, rs_y))
                link(V.scalar_tensor_tensor(y_row, y_row, rs_y, gm_row, ALU.mult, ALU.mult))
                dve.wait_ge(xt_in[t % 2], 16 * (t // 2) + 16)
                V.tensor_tensor(x2[:, t, :], y_row, xt[t % 2], ALU.add).then_inc(x2_done, 1)
                dve.wait_ge(x2_done, t + 1)
                dve.wait_ge(x_sq, t + 1)
                V.tensor_scalar(xs_, xs_, 1.0 / D, EPS, ALU.mult, ALU.add).then_inc(x_ms, 1)
                dve.wait_ge(x_sqrt, t + 1)
                link(V.reciprocal(rs_x, rs_x))
                if t >= 2:
                    dve.wait_ge(xn_stored[t % 2], 16 * (t // 2))
                    dve.wait_ge(psum_ready, JOB[("xT2", t - 2, 1)] + 1)
                V.tensor_scalar(xn2[t % 2], x2[:, t, :], rs_x, None, ALU.mult).then_inc(xn2_done, 1)
                if t:
                    e_router(t - 1)
            e_router(NT - 1)
            was_read(dve, ("lg", NT - 1))

            lg = logits[:, :, 0:4]
            le = logits[:, :, 4:36].rearrange("p t (g e) -> p t g e", g=4)

            def over_last(v, n):
                return v.unsqueeze(2).broadcast_to([P, NT, n])

            def first_hot(onehot, index, values, best, eq, scratch, n, io, iom):
                link(V.tensor_reduce(best, values, AX.X, ALU.max))
                link(V.tensor_tensor(eq, values, over_last(best, n), ALU.is_equal))
                link(V.scalar_tensor_tensor(scratch, eq, -64.0, io.unsqueeze(1).broadcast_to([P, NT, n]), ALU.mult, ALU.add))
                link(V.tensor_reduce(index, scratch, AX.X, ALU.min))
                link(V.tensor_tensor(onehot, iom.unsqueeze(1).broadcast_to([P, NT, n]), over_last(index, n), ALU.is_equal))

            first_hot(ohg, ig, lg, mg, eqg, dg, 4, iota4, iota4m)
            link(V.tensor_tensor(dg, lg, over_last(mg, 4), ALU.subtract))
            link(V.tensor_tensor(prod, le, ohg.unsqueeze(3).broadcast_to([P, NT, 4, 8]), ALU.mult))
            link(V.tensor_reduce(lin, prod.rearrange("p t g e -> p t e g"), AX.X, ALU.add))
            first_hot(oh1, i1, lin, m1, eqe, cand, 8, iota8, iota8m)
            link(V.scalar_tensor_tensor(lin, oh1, NEG, lin, ALU.mult, ALU.add))
            first_hot(oh2, i2, lin, m2, eqe, cand, 8, iota8, iota8m)
            V.tensor_tensor(e2, m2, m1, ALU.subtract).then_inc(exp_args, 1)
            for k, oh in enumerate((oh1, oh2)):
                link(V.tensor_tensor(hot[k], ohg.unsqueeze(3).broadcast_to([P, NT, 4, 8]),
                                     oh.unsqueeze(2).broadcast_to([P, NT, 4, 8]), ALU.mult))
            h0, h1_ = (v.rearrange("p t g e -> p t (g e)") for v in hot)
            V.tensor_tensor(hots, h0, h1_, ALU.add).then_inc(hots_ready, 1)
            dve.wait_ge(exps_done, 2)
            link(V.tensor_reduce(sg_, dg, AX.X, ALU.add))
            link(V.scalar_tensor_tensor(sg_, e2, 1.0, sg_, ALU.add, ALU.mult))
            link(V.reciprocal(gates2[:, 0, :], sg_))
            link(V.tensor_tensor(gates2[:, 1, :], gates2[:, 0, :], e2, ALU.mult))
            b = ready(dve, "rank")
            link(V.tensor_copy(before, b[:, 256:512].rearrange("p (t e) -> p t e", e=NE)))
            link(V.memset(prefix[:, 0, :], 0.0))
            for t in range(1, NT):
                link(V.tensor_tensor(prefix[:, t, :], prefix[:, t - 1, :], before[:, t - 1, :], ALU.add))
            link(V.tensor_tensor(total, prefix[:, NT - 1, :], before[:, NT - 1, :], ALU.add))
            read(V.tensor_tensor(rank, b[:, 0:256].rearrange("p (t e) -> p t e", e=NE), prefix, ALU.add), "rank")
            was_read(dve, "rank")
            link(V.memset(ones32, 1.0))
            link(V.tensor_scalar(over, total, float(P), None, ALU.is_gt))
            for j in range(2, NT):
                link(V.scalar_tensor_tensor(over, total, float(P * j), over, ALU.is_gt, ALU.add))
            link(V.tensor_tensor_scan(over_inc, ones32, over, 0.0, ALU.mult, ALU.add))
            link(V.tensor_tensor(off_e, over_inc, over, ALU.subtract))
            link(V.tensor_tensor(off_e, off_e, iota32, ALU.subtract))
            link(V.tensor_scalar(off_e, off_e, float(NE - 1), float(P), ALU.add, ALU.mult))
            for k, hk in enumerate((h0, h1_)):
                for dst, src in ((rk, rank), (ex, iota32), (ofs, off_e)):
                    if src is not rank:
                        src = src.unsqueeze(1).broadcast_to([P, NT, NE])
                    link(V.tensor_tensor(before, hk, src, ALU.mult))
                    link(V.tensor_reduce(dst[:, k, :], before, AX.X, ALU.add))
            link(V.tensor_scalar(big, rk, float(P), None, ALU.is_ge))
            link(V.tensor_tensor(big, big, ofs, ALU.mult))
            link(V.scalar_tensor_tensor(ex, ex, float(P), rk, ALU.mult, ALU.add))
            link(V.tensor_tensor(dest, ex, big, ALU.add))
            link(V.tensor_single_scalar(laneslot, dest, P - 1, ALU.bitwise_and))
            link(V.tensor_single_scalar(slot, dest, 7, ALU.logical_shift_right))
            link(V.scalar_tensor_tensor(slot, laneslot, float(NB), slot, ALU.mult, ALU.add))
            link(V.memset(tabf[0:1, 0:64], 0.0))
            link(V.tensor_copy(tabf[0:1, 0:NE], iota32[0:1, :]))
            one = lambda v, *s: v[0:1, :].unsqueeze(s[0]).broadcast_to([1, NOV, NE])
            link(V.tensor_tensor(ov_cmp[0:1], one(over_inc, 1), one(iota15, 2), ALU.is_le))
            link(V.tensor_reduce(tabf[0:1, NE:NE + NOV], ov_cmp[0:1], AX.X, ALU.add))
            link(V.tensor_scalar(tabf[0:1, 0:NB], tabf[0:1, 0:NB], float(NE - 1), None, ALU.min))
            link(V.tensor_scalar(tabf[0:1, 48:49], over_inc[0:1, NE - 1:NE], float(NE), None, ALU.add))
            V.tensor_copy(block_tab, tabf[0:1, 0:64]).then_inc(dest_ready, 1)
            end_stage(dve, 4)

            def f_turned(s, n):
                dve.wait_ge(xg_turned[s], n + 2)
                dve.wait_ge(up_part[s], 2 * n + 1)
                for k in range(KT):
                    last = V.tensor_scalar(xgT[s][:, k, :], ps[:, k // 4, P * (k % 4):P * (k % 4) + P], scale2[:, k:k + 1],
                                           mod[:, 24 + k:25 + k], ALU.mult, ALU.add)
                last.then_inc(xgT_ready[s], 1)

            for s in range(2):
                dve.sem_inc(yo_ready[s], 1)
            v_blocks = dve.value_load(block_tab[0:1, 48:49], min_val=NE, max_val=NB)
            f_turned(0, 0)
            with dve.Fori(0, NB // 2) as i:
                for s in range(2):
                    with dve.If(2 * i + s < v_blocks):
                        dve.wait_ge(silu_part[s], i + 1)
                        dve.wait_ge(up_part[s], 2 * i + 3)
                        V.tensor_tensor(hid_e[s], act1[s], ps[:, 3, :], ALU.mult).then_inc(hid_part[s], 1)
                        for n in range(2):
                            dve.wait_ge(hid_turned[s], 2 * i + 1 + n)
                            V.tensor_copy(hid_T[s][:, 2 * n:2 * n + 2, :], ps[:, 4 + n, 0:2 * P].rearrange("p (k n) -> p k n", n=P))\
                             .then_inc(hidT_read[s], 1)
                    with dve.If(2 * i + s + 1 < v_blocks):
                        f_turned(1 - s, i + s)
                    with dve.If(2 * i + s < v_blocks):
                        dve.wait_ge(down_done[s], i + 2)
                        dve.wait_ge(y_stored[s], 16 * i + 16)
                        V.tensor_copy(yo[s], ps[:, 6:8, :].rearrange("p a b -> p (a b)")).then_inc(yo_ready[s], 1)
            dve.drain().then_inc(stage_f, 1)
            dve.wait_ge(stage_f, 4)

            for t in range(NT):
                a, b = y1[t % NG], y2[t % NG]
                dve.wait_ge(y_in[t % NG], 32 * (t // NG) + 32)
                link(V.tensor_scalar(a, a, gates2[:, 0, t:t + 1], None, ALU.mult))
                V.scalar_tensor_tensor(a, b, gates2[:, 1, t:t + 1], a, ALU.mult, ALU.add).then_inc(g_ms, 1)
                dve.wait_ge(g_sq, t + 1)
                V.tensor_scalar(ys, ys, 1.0 / D, EPS, ALU.mult, ALU.add).then_inc(g_ms, 1)
                dve.wait_ge(g_sqrt, t + 1)
                link(V.reciprocal(rs_y, rs_y))
                link(V.scalar_tensor_tensor(a, a, rs_y, gf_row, ALU.mult, ALU.mult))
                V.tensor_tensor(a, a, x2[:, t, :], ALU.add).then_inc(g_done, 1)


def kernel(**inputs):
    import concourse.bacc as bacc
    from concourse.bass_utils import run_bass_kernel_spmd

    nc = bacc.Bacc("TRN2", target_bir_lowering=False, num_devices=1)
    lane = np.arange(P) % HD
    inv = (10000.0 ** (-(lane % 32) / 32.0)).astype(np.float32)
    arrays = {"rope_cols": np.stack([inv, np.where(lane < 32, -1.0, 1.0).astype(np.float32)], 1)}
    for name, a in inputs.items():
        a = np.asarray(a)
        arrays[name] = np.ascontiguousarray(a if name in ("positions", "mlstm_gate_b", "c", "router_grp_b", "router_exp_b") else a[0])
    for name in ("ada_b", "norm_mix_pre", "norm_mix_post", "norm_ffn_pre", "norm_ffn_post", "c", "mlstm_head_norm"):
        arrays[name] = arrays[name].reshape(-1)
    d = {n: nc.dram_tensor(n, a.shape, mybir.dt.from_np(a.dtype), kind="ExternalInput").ap() for n, a in arrays.items()}
    out = nc.dram_tensor("out", (S, D), F32, kind="ExternalOutput").ap()
    build(nc, d, out)
    r = run_bass_kernel_spmd(nc, [arrays], core_ids=[0])
    return r.results[0]["out"].reshape(1, *(S, D))
```

```python
from contextlib import ExitStack

import numpy as np
import concourse.bass as bass
from concourse import mybir

F32 = mybir.dt.float32
I32 = mybir.dt.int32
BF16 = mybir.dt.bfloat16
ALU = mybir.AluOpType
ACT = mybir.ActivationFunctionType
AX = mybir.AxisListType

P = 128
S = D = 1024
NT = S // P
KT = D // P
CH = S // 512
HD = 64
NH = 8
MH = 4
MW = 512
NEG = -1e30
EPS = 1e-6
NCMP = 63
NE = 32
NOV = 15
FF = 512
OFF = dict(mq=0, mk=512, mv=1024, mo=1536, mi=2048, nq=2056, kc=2568, kwn=3080, ng=3336)

HT = 0
COS, SIN = 8192, 9216
CONV = 10240
MKT = 12294
V1 = MKT + 4096
RING2 = V1 + 4128
RING0 = RING2 + 4096
QT = RING0 + 8192
KSL, KWN, KCT = QT + 4096, QT + 5120, QT + 6144
VV = QT + 8224
MQT = VV + 2048
YM = MQT + 4096
SMALL = YM + 4096
WORDS = 53200
W0, W1 = 0, MKT
MH_SCALE = float(np.float32(P ** -0.5))
TWO_PI = 2 * np.pi
PI2_MID = float(np.round((TWO_PI - 6.28125) * 2 ** 21) / 2 ** 21)
PI2 = (6.28125, PI2_MID, TWO_PI - 6.28125 - PI2_MID)
PI_IN = 3.1415925
ROUND = 1.5 * 2 ** 23
XN = MQT


def job_list():
    jobs = ["vec"] + [("hT", 0, k) for k in range(6)] + ["ada03"]
    jobs += [("hT", c, k) for c in range(CH) for k in range(KT) if c or k >= 6]
    jobs += [("tok", t) for t in range(NT)] + [("kwn", c) for c in range(CH)] + ["gT"]
    for j in range(4):
        jobs += [("q", j, c) for c in range(CH)] + [("ada", 4)] * (j == 2)
    jobs += ["gcol", ("ada", 5)] + [(n, c) for n in ("kc", "ksl", "vc") for c in range(CH)] + [("ada", 6)]
    jobs += [("mq", j, c) for j in range(4) for c in range(CH)] + [("ada", 7)]
    jobs += [("mk", j, c) for j in range(4) for c in range(CH)]
    jobs += [("mv", t) for t in range(4)] + [("ada", 8)] + [("mv", t) for t in range(4, NT)] + [("ada", 9)]
    jobs += [("mo", t) for t in range(NT)] + [("ada", 10), ("ada", 11)]
    jobs += [("chid", 0), ("chid", 1), "kcmp", "vcmp"]
    jobs += [("S", 0), ("kr", 0)]
    for c in range(NT):
        jobs += [("S", c + 1)] * (c + 1 < NT) + [("kr", c + 1)] * (c + 2 < NT) + [("num", c, p) for p in range(2)]
        jobs += [("kv", c, p) for p in range(2) if c + 1 < NT] + [("int", c, p) for p in range(2)]
    jobs += [("row", i, n) for i in range(2) for n in range(2)]
    jobs += [("yT", 0, 0), ("yT", 0, 1)]
    for t in range(NT):
        before = [("xT2", t - 1, 0), ("xT2", t - 1, 1)] if t else []
        jobs += [("yT", t + 1, n) for n in range(2) if t + 1 < NT]
        jobs += [("out", t, 0)] + before + [("out", t, 1)] + [("lg", t - 1)] * (t > 0)
    jobs += [("xT2", NT - 1, 0), ("xT2", NT - 1, 1), ("lg", NT - 1), "rank", "table"]
    return {n: i for i, n in enumerate(jobs)}


def ring_items(d):
    w_in = d["w_in"].rearrange("(k p) n -> p k n", p=P)
    ada = d["ada_w"].rearrange("(k p) n -> p k n", p=P)
    w_out = d["w_out"].rearrange("(k p) n -> p k n", p=P)
    ada_item = lambda i: [(0, 0, ada[:, :, 512 * i:512 * i + 512])]
    piece = lambda col, at, w: (col, 0, w_in[:, :, at:at + w])
    items = [ada_item(i) for i in range(4)]
    items.append([piece(0, OFF["kwn"], P), piece(P, OFF["kc"] + 3 * P, P), piece(2 * P, OFF["kwn"] + P, P),
                  piece(3 * P, OFF["mi"], 8), piece(3 * P + 8, OFF["ng"], 24)])
    items.append(ada_item(4))
    items.append([piece(P * j + HD * g, OFF["nq"] + HD * (4 * g + j), HD) for j in range(4) for g in range(2)])
    items.append(ada_item(5))
    items.append([piece(0, OFF["kc"], 3 * P)])
    for i, n in enumerate(("mq", "mk", "mv", "mo")):
        items += [ada_item(6 + i), [piece(0, OFF[n], 512)]]
    items += [ada_item(10), ada_item(11)]
    for n in ("cmp_w1_k", "cmp_w1_v"):
        items.append([(0, 0, d[n].rearrange("(k p) n -> p k n", p=P))])
    items += [[(0, 0, w_out[:, :, 512 * i:512 * i + 512])] for i in range(2)]
    return items


IT_KWN, IT_NQ, IT_KC, IT_MQ, IT_MK, IT_MV, IT_MO = 4, 6, 8, 10, 12, 14, 16
IT_ADA = {**{i: i for i in range(4)}, **{4 + i: 5 + 2 * i for i in range(6)}, 10: 17, 11: 18}
IT_CMP, IT_WOUT = 19, 21


def build(nc, d, out):
    JOB = job_list()
    ITEMS = ring_items(d)
    with ExitStack() as ctx:
        def sem(name):
            return ctx.enter_context(nc.semaphore(name))

        arena = ctx.enter_context(nc.sbuf_tensor("arena", [P, WORDS], F32))
        ps = ctx.enter_context(nc.psum_tensor("ps", [P, 8, 512], F32))

        def view(at, *shape, parts=P):
            n = int(np.prod(shape))
            v = arena[0:parts, at:at + n]
            if len(shape) == 2:
                v = v.rearrange("p (a b) -> p a b", b=shape[1])
            if len(shape) == 3:
                v = v.rearrange("p (a b c) -> p a b c", b=shape[1], c=shape[2])
            return v

        small = [SMALL]

        def tiny(*shape, parts=P, dt=F32):
            at = small[0]
            small[0] += int(np.prod(shape))
            assert small[0] <= WORDS
            v = view(at, *shape, parts=parts)
            return v if dt is F32 else v.bitcast(dt)

        hT = view(HT, KT, S)
        cos, sin = view(COS, S), view(SIN, S)
        conv_raw = view(CONV, 2, S + 3)
        mkT, mqT = view(MKT, MH, S), view(MQT, MH, S)
        v1 = view(V1, NT, MH, P + 1)
        ring = [view(RING0, KT, 512), view(RING0 + 4096, KT, 512), view(RING2, KT, 512)]
        qT = view(QT, 4, S)
        kslT, kwnT = view(KSL, S), view(KWN, S)
        pairs_kv = [view(KCT + 1040 * a, 1040) for a in range(2)]
        vv = view(VV, NT, 4 * HD)
        yn, ym = view(MQT, NT, MW), view(YM, NT, MW)
        xn = view(XN, NT, D)
        junk = view(V1, 2, D)
        swap = view(V1, 2, 512)
        turned = view(V1 + 1024, 2, 512)
        sc_ = [view(YM + P * i, P, parts=32) for i in range(12)]
        g_i, g_f, decay_b, u_, cmax, mx, dec_, em_, wp_, neg_mx, t_a, ones_r = sc_
        gi_cols, gf_cols = view(YM + 12 * P, MH, NT), view(YM + 12 * P + 32, MH, NT)
        gall = view(YM + 13 * P, NT, 32)
        abs_f = view(YM + 15 * P, P, parts=32)
        bc = view(HT, MH, NT, P)
        at = [4096]

        def temp(*shape):
            v = view(at[0], *shape)
            at[0] += int(np.prod(shape))
            assert at[0] <= MKT
            return v

        wts, kw = [temp(MH, P) for _ in range(2)], [temp(MH, P) for _ in range(2)]
        num, inter = [temp(MH, P + 1) for _ in range(2)], [temp(MH, P + 1) for _ in range(2)]
        state = [temp(MH, P + 1) for _ in range(2)]
        junk_h = temp(MH, P)

        ident = tiny(P)
        ident_b = tiny(P // 2).bitcast(BF16)
        masks_at = small[0]
        causal = tiny(P // 2).bitcast(BF16)
        behind = tiny(P // 2).bitcast(BF16)
        cmask = tiny(NT * HD // 2).bitcast(BF16).rearrange("p (t n) -> p t n", n=HD)
        masks_end = small[0]
        cols = tiny(124)
        mod = tiny(48)
        scale1, shift1, scale2, shift2 = (tiny(KT) for _ in range(4))
        sc_col = tiny(KT)
        ones = tiny(1)
        ada_sum = [view(at_, 4, 512) for at_ in (CONV, YM + 2048, CONV)]
        sum_sq, rstd = tiny(NT), tiny(NT)
        gate_b = tiny(8)
        sgate = tiny(NT, 24)
        gcols = tiny(4, 32)
        a_old = tiny(32)
        k_cmp = tiny(64)
        v_cmp = tiny(2, HD)
        w2c = tiny(2, HD)
        hbias = tiny(2)
        freq = tiny(2)
        gm_col = tiny(2, KT)
        inv_den, ssq4, rs4, factor = (tiny(2, MH) for _ in range(4))
        eps_col = tiny(1)
        nmax = tiny(4, 4)
        sums = tiny(2, 3, 4)
        rsum = tiny(3, 4)
        hop = tiny(2, parts=32)
        hop2 = tiny(3, parts=32)
        hop4 = tiny(8, 2, parts=4)
        hop5 = tiny(8, 2, parts=4)
        gm32 = tiny(1, parts=32)
        vec = view(V1 + 2048, P, parts=124)
        hid = temp(2, 2, 64)
        pos_i, pos_f, ang, turns = view(MKT, S).bitcast(I32), view(MKT + S, S), view(MKT + 2 * S, S), view(MKT + 3 * S, S)

        d_hop = nc.dram_tensor("d_hop", (32, 2), F32).ap()
        d_hop2 = nc.dram_tensor("d_hop2", (32, 2), F32).ap()
        d_nmx = nc.dram_tensor("d_nmx", (32, P), F32).ap()
        d_old = nc.dram_tensor("d_old", (32, 1), F32).ap()

        psum_ready = sem("psum_ready")
        bank_read = [sem(f"bank_read{i}") for i in range(8)]
        ring_in = [sem(f"ring_in{i}") for i in range(3)]
        vec_in, x_in, const_in = sem("vec_in"), [sem(f"x_in{t}") for t in range(NT)], sem("const_in")
        pool_const = sem("pool_const")
        sq_done, norm_ms, norm_sqrt, xn_done = sem("sq_done"), sem("norm_ms"), sem("norm_sqrt"), sem("xn_done")
        mod_ready = sem("mod_ready")
        silu_c, ada_summed = sem("silu_c"), sem("ada_summed")
        angle, trig = sem("angle"), sem("trig")
        swapped, roped = sem("swapped"), sem("roped")
        conv_done = sem("conv_done")
        gates_in_cols = sem("gates_in_cols")
        exp_f, ln_f = sem("exp_f"), sem("ln_f")
        exp_in, exp_out = sem("exp_in"), sem("exp_out")
        hop_out, hop_in = sem("hop_out"), sem("hop_in")
        sg_done = sem("sg_done")
        act_step, dve_step, pool_step = sem("act_step"), sem("dve_step"), sem("pool_step")
        stage_end = {c: sem(f"stage_end{c}") for c in "BCDE"}
        hbias_ready = sem("hbias_ready")
        decay_in, decay_masked, decay_exp = sem("decay_in"), sem("decay_masked"), sem("decay_exp")
        h_den, h_sq, h_sqrt, state_zero = sem("h_den"), sem("h_sq"), sem("h_sqrt"), sem("state_zero")

        NB = 48
        small[0], late_end = masks_at, masks_end
        probs = {"s": [view(MKT + S * h, S) for h in range(4)],
                 "w": [view(MKT + 4 * S + 640 * h, 640) for h in range(4)],
                 "c": [view(KCT + HD * h, HD) for h in range(4)]}
        probs_T = [view(MKT + 4 * S + 4 * 640 + 512 * i, 512) for i in range(2)]
        out_T = view(MKT + 5 * S + 4 * 640, 512)
        scaled = view(KCT + 1280, 4, 2, HD)
        zero_row = view(KCT + 1792, 256)
        ones_sq, upper = view(MKT + 9472, P), view(MKT + 9600, P)
        E0 = MKT
        xt = [view(E0 + D * i, D) for i in range(2)]
        yT = [view(E0 + D * (2 + i), KT, P) for i in range(2)]
        y_row, junk_e = view(E0 + 4 * D, D), view(E0 + 5 * D, D)
        xn2 = [view(E0 + D * (6 + i), D) for i in range(2)]
        h2T = view(E0 + 8 * D, KT, P)
        logits = view(MKT + 9728, NT, 36)
        w_router = view(MKT + 10016, KT, 36)
        b_router = view(MKT + 10304, 36)
        iota48, iota128 = view(MKT + 10340, NB), view(MKT + 10476, P)
        iota32, iota8, iota4 = view(MKT + 10388, NE), view(MKT + 10420, 8), view(MKT + 10428, 4)
        iota8m, iota4m = view(MKT + 10432, 8), view(MKT + 10440, 4)
        iota15 = view(MKT + 10444, NOV)
        tok_id = view(MKT + 10460, NT)
        lane_hot, tok_hot = view(RING0, 2 * NT, P), view(RING0 + 2 * NT * P, 2 * NT, NB)
        x2 = view(QT, NT, D)
        gm_row, gf_row = view(VV, D), view(VV + D, D)
        diag = [yT[0], yT[1]]
        ys, rs_y, xs_, rs_x = tiny(1), tiny(1), tiny(1), tiny(1)
        gates2 = tiny(2, NT)
        dest = tiny(2, NT, dt=I32)
        row_tok = tiny(48, dt=I32)
        block_tab = tiny(64, parts=1, dt=I32)
        ra = [YM]

        def route(*shape, dt=F32):
            v = view(ra[0], *shape)
            ra[0] += int(np.prod(shape))
            assert ra[0] <= SMALL
            return v if dt is F32 else v.bitcast(dt)

        mg, sg_, ig, m1, i1, m2, i2, e2 = (route(NT) for _ in range(8))
        dg, eqg, ohg = route(NT, 4), route(NT, 4), route(NT, 4)
        lin, eqe, cand, oh1, oh2 = (route(NT, 8) for _ in range(5))
        prod = route(NT, 4, 8)
        hot = [route(NT, 4, 8) for _ in range(2)]
        hots, before, prefix, rank = route(NT, NE), route(NT, NE), route(NT, NE), route(NT, NE)
        total, over, over_inc, off_e, ones32 = (route(NE) for _ in range(5))
        rk, ex, ofs, big = route(2, NT), route(2, NT), route(2, NT), route(2, NT)
        ov_cmp = route(NOV, NE)
        tabf = route(64)
        lane_i, blk_i = route(2, NT, dt=I32), route(2, NT, dt=I32)
        lane_f, blk_f = route(2, NT), route(2, NT)
        w13 = [[view(W + 4096 * n, KT, FF) for n in range(2)] for W in (W0, W1)]
        w2s = [view(W + 8192, 4, D) for W in (W0, W1)]
        xg = [view(RING0 + D * i, D) for i in range(2)]
        xgT = [view(RING0 + D * (2 + i), KT, P) for i in range(2)]
        yo = [view(RING0 + D * (4 + i), D) for i in range(2)]
        act1 = [view(RING0 + D * 6 + 512 * i, FF) for i in range(2)]
        hid_e = [view(RING0 + D * 7 + 512 * i, FF) for i in range(2)]
        hid_T = [view(MQT + 512 * i, 4, P) for i in range(2)]
        idx_col = [tiny(1, dt=I32) for _ in range(2)]
        sum_g, rs_g = tiny(2), tiny(2)
        assert small[0] <= late_end
        NG = 4
        y1 = [view(W0 + D * i, D) for i in range(NG)]
        y2 = [view(W0 + D * (NG + i), D) for i in range(NG)]
        junk_g = view(W0 + 2 * NG * D, D)
        d_xn = nc.dram_tensor("d_xn", (S, D), F32).ap()
        d_y = nc.dram_tensor("d_y", (NB * P, D), F32).ap()

        scores_ready, row_max, probs_ready = sem("scores_ready"), sem("row_max"), sem("probs_ready")
        turned_ready, turned_read = sem("turned_ready"), [sem(f"turned_read{i}") for i in range(2)]
        pv_done, out_copied, heads_done = sem("pv_done"), sem("out_copied"), sem("heads_done")
        wout_scaled, pool_e, router_in, xt_in = sem("wout_scaled"), sem("pool_e"), sem("router_in"), [sem(f"xt_in{i}") for i in range(2)]
        diag_ready = sem("diag_ready")
        y_sq, y_ms, y_sqrt, x2_done = sem("y_sq"), sem("y_ms"), sem("y_sqrt"), sem("x2_done")
        x_sq, x_ms, x_sqrt, xn2_done = sem("x_sq"), sem("x_ms"), sem("x_sqrt"), sem("xn2_done")
        xn_stored = [sem(f"xn_stored{i}") for i in range(2)]
        exp_args, exps_done, hots_ready, slots_hot = sem("exp_args"), sem("exps_done"), sem("hots_ready"), sem("slots_hot")
        w13_in = [[sem(f"w{2 * n + 1}_in{i}") for n in range(2)] for i in range(2)]
        w2_in = [sem(f"w2_in{i}") for i in range(2)]
        idx_ready = [sem(f"idx_ready{i}") for i in range(2)]
        xg_in = [sem(f"xg_in{i}") for i in range(2)]
        xg_turned = [sem(f"xg_turned{i}") for i in range(2)]
        xgT_ready, yo_ready = [sem(f"xgT_ready{i}") for i in range(2)], [sem(f"yo_ready{i}") for i in range(2)]
        up_part, silu_part, hid_part = ([sem(f"{n}{i}") for i in range(2)] for n in ("up_part", "silu_part", "hid_part"))
        hid_turned, hidT_read = ([sem(f"{n}{i}") for i in range(2)] for n in ("hid_turned", "hidT_read"))
        down_done = [sem(f"down_done{i}") for i in range(2)]
        y_stored = [sem(f"y_stored{i}") for i in range(2)]
        stage_f, y_zeroed = sem("stage_f"), sem("y_zeroed")
        idx_seen, store_seen = sem("idx_seen"), sem("store_seen")
        y_in = [sem(f"y_in{i}") for i in range(4)]
        g_scaled, g_added, g_sq, g_sqrt, g_done = (sem(n) for n in ("g_scaled", "g_added", "g_sq", "g_sqrt", "g_done"))
        out_stored = [sem(f"out_stored{i}") for i in range(4)]

        def key_blocks(x, kind):
            t = x // 2
            return [0] if kind == "c" else list(range(max(0, t - 4) if kind == "w" else 0, t + 1))

        def key_count(x, kind):
            return min(NCMP, 8 * (x // 2) + 7) if kind == "c" else P * len(key_blocks(x, kind))

        def heads_of(kind):
            return [None] if kind == "c" else [0, 1, 2, 3]

        EVENTS, UNIT, TURN, PV_AT, LAST_TURN = [], {}, {}, {}, {}

        def event(*e):
            if e[0] == "scores":
                UNIT[e[1:]] = len(UNIT)
            if e[0] in ("turn", "out_turn"):
                TURN[e] = len(TURN)
                LAST_TURN[e[1:3]] = len(TURN)
            if e[0] == "values":
                PV_AT[e[1:]] = len(PV_AT)
            EVENTS.append(e)

        phases = [(x, kind) for x in range(2 * NT) for kind in "scw"]
        def scores_during(x, kind):
            ahead = {"c": [], "s": [(x, "w")], "w": [(x + 1, "s"), (x + 1, "c")] if x + 1 < 2 * NT else []}[kind]
            return [(*phase, h) for phase in ahead for h in heads_of(phase[1])]

        for kind in "sc":
            for h in heads_of(kind):
                event("scores", 0, kind, h)
        for x, kind in phases:
            blocks = key_blocks(x, kind)
            nxt = scores_during(x, kind)
            event("turn", x, kind, 0)
            for b in range(len(blocks)):
                if b + 1 < len(blocks):
                    event("turn", x, kind, b + 1)
                for j, n in enumerate(nxt):
                    if j * len(blocks) // len(nxt) == b:
                        event("scores", *n)
                event("values", x, kind, b)
                if kind == "s" and b == 0 and x:
                    event("out_turn", x - 1, "o")
            if kind == "w":
                event("out_copy", x)
        event("out_turn", 2 * NT - 1, "o")

        def scores(u):
            return ps[:, 2 * (u % 2):2 * (u % 2) + 2, :].rearrange("p a b -> p (a b)")

        def evacuate_turned(eng, copy, e, mine):
            q = TURN[e]
            if q % 2 != mine:
                return
            _, x, kind, b = e
            eng.wait_ge(turned_ready, q + 1)
            if q >= 2:
                before = [PV_AT[f[1:]] for f in TURN if TURN[f] == q - 2 and f[0] == "turn"]
                if before:
                    eng.wait_ge(pv_done, before[0] + 1)
            rows = key_count(x, kind) if kind == "c" else P
            copy(probs_T[q % 2][0:rows, :], ps[0:rows, 4 + q % 2, :]).then_inc(turned_read[q % 2], 1)

        def bank(name):
            return ps[:, JOB[name] % 8, :]

        def claim(eng, name):
            j = JOB[name]
            if j >= 8:
                eng.wait_ge(bank_read[j % 8], j // 8)
            return bank(name)

        def ready(eng, name):
            eng.wait_ge(psum_ready, JOB[name] + 1)
            return bank(name)

        def read(ins, name):
            ins.then_inc(bank_read[JOB[name] % 8], 1)

        def was_read(eng, name):
            eng.wait_ge(bank_read[JOB[name] % 8], JOB[name] // 8 + 1)

        ring_total, ring_want = [0, 0, 0], []
        for i, it in enumerate(ITEMS):
            ring_total[i % 3] += 16 * len(it)
            ring_want.append(ring_total[i % 3])

        def end_stage(eng, k):
            eng.drain().then_inc(stage_end[k], 1)
            eng.wait_ge(stage_end[k], 4)

        def chain(eng, step):
            count = [0]

            def link(ins):
                count[0] += 1
                ins.then_inc(step, 1)
                eng.wait_ge(step, count[0])
            return link

        block = ctx.enter_context(nc.Block())

        last_job = {IT_KWN: ("kwn", 1), IT_NQ: ("q", 3, 1), IT_KC: ("vc", 1), IT_MQ: ("mq", 3, 1), IT_MK: ("mk", 3, 1),
                    IT_MV: ("mv", NT - 1), IT_MO: ("mo", NT - 1), IT_CMP: ("chid", 0), IT_CMP + 1: ("chid", 1)}
        ada_of = {it: i for i, it in IT_ADA.items()}

        @block.sync
        def _(sp):
            rows = [(0, "ada_b"), (48, "norm_mix_pre"), (56, "norm_mix_post"), (64, "norm_ffn_pre"),
                    (72, "norm_ffn_post"), (80, "c"), (88, "mlstm_head_norm")]
            for at_row, name in rows:
                src = d[name].rearrange("(r p) -> r p", p=P)
                sp.dma_start(vec[at_row:at_row + src.shape[0], :], src).then_inc(vec_in, 16)
            sp.dma_start(vec[92:124, :], d["mlstm_conv_w"].rearrange("j (r p) -> (j r) p", p=P)).then_inc(vec_in, 16)

            def load_ring(i):
                if i - 3 in ada_of:
                    sp.wait_ge(ada_summed, ada_of[i - 3] + 1)
                elif i >= 3:
                    sp.wait_ge(psum_ready, JOB[last_job[i - 3]] + 1)
                for col, part, src in ITEMS[i]:
                    dst = ring[i % 3]
                    if i in (IT_CMP, IT_CMP + 1):
                        dst = dst.rearrange("p k n -> p (k n)").rearrange("p (k n) -> p k n", n=P)[:, 0:16, :]
                    with nc.allow_non_contiguous_dma(reason="gate weights are 8 and 24 columns"):
                        sp.dma_start(dst[:, :, col:col + src.shape[2]], src).then_inc(ring_in[i % 3], 16)

            for t in range(NT):
                sp.dma_start(xn[:, t, :], d["x"][t * P:(t + 1) * P, :]).then_inc(x_in[t], 16)
            for i in range(5):
                load_ring(i)
            with nc.allow_non_contiguous_dma(reason="small gate weights and columns, once"):
                for a, n in enumerate("kv"):
                    src = d["cmp_pe_" + n].rearrange("(j o) d -> o d j", o=2)
                    for o in range(2):
                        sp.dma_start(pairs_kv[a][o * HD:(o + 1) * HD, S:S + 16], src[o]).then_inc(const_in, 16)
            sp.dma_start(w2c[:, 0, :], d["cmp_w2_k"]).then_inc(const_in, 16)
            sp.dma_start(w2c[:, 1, :], d["cmp_w2_v"]).then_inc(const_in, 16)
            sp.dma_start(gate_b, d["mlstm_gate_b"].broadcast_to([P, 8])).then_inc(const_in, 16)
            sp.dma_start(freq, d["rope_cols"]).then_inc(const_in, 16)
            sp.dma_start(pos_i, d["positions"].broadcast_to([P, S])).then_inc(const_in, 16)
            for i in range(5, IT_WOUT):
                load_ring(i)
            sp.wait_ge(stage_end["B"], 4)
            sp.dma_start(bc, d_nmx.rearrange("r l -> (r l)").rearrange("(a n) -> a n", a=1).broadcast_to([P, 32 * P])
                         .rearrange("p (h c l) -> p h c l", h=MH, c=NT)).then_inc(decay_in, 16)
            sp.dma_start(a_old, d_old.rearrange("r a -> a r").broadcast_to([P, 32])).then_inc(decay_in, 16)
            for i in range(IT_WOUT, IT_WOUT + 2):
                load_ring(i)
            sp.wait_ge(stage_end["C"], 4)
            for n, name in enumerate(("expert_w1", "expert_w3")):
                sp.dma_start(w13[0][n], d[name][0].rearrange("(k p) n -> p k n", p=P)).then_inc(w13_in[0][n], 16)
            sp.dma_start(w2s[0], d["expert_w2"][0].rearrange("(k p) n -> p k n", p=P)).then_inc(w2_in[0], 16)
            with nc.allow_non_contiguous_dma(reason="router weights, once"):
                sp.dma_start(w_router[:, :, 0:4], d["router_grp_w"].rearrange("(k p) n -> p k n", p=P)).then_inc(router_in, 16)
                sp.dma_start(w_router[:, :, 4:36], d["router_exp_w"].rearrange("(k p) n -> p k n", p=P)).then_inc(router_in, 16)
            sp.dma_start(b_router[:, 0:4], d["router_grp_b"].broadcast_to([P, 4])).then_inc(router_in, 16)
            sp.dma_start(b_router[:, 4:36], d["router_exp_b"].broadcast_to([P, NE])).then_inc(router_in, 16)
            sp.wait_ge(pool_e, 1)
            for b in range(NE, NB):
                sp.dma_start(d_y[b * P:(b + 1) * P, :].rearrange("p (a n) -> p a n", a=4),
                             zero_row.unsqueeze(1).broadcast_to([P, 4, 256])).then_inc(y_zeroed, 16)
            sp.wait_ge(stage_end["D"], 4)
            for t in range(2):
                sp.dma_start(xt[t], d["x"][t * P:(t + 1) * P, :]).then_inc(xt_in[t], 16)
            for t in range(NT):
                sp.wait_ge(x2_done, t + 1)
                if t + 2 < NT:
                    sp.dma_start(xt[t % 2], d["x"][(t + 2) * P:(t + 3) * P, :]).then_inc(xt_in[t % 2], 16)
                sp.wait_ge(xn2_done, t + 1)
                sp.dma_start(d_xn[t * P:(t + 1) * P, :], xn2[t % 2]).then_inc(xn_stored[t % 2], 16)
            sp.dma_start(w13[1][0], d["expert_w1"][1].rearrange("(k p) n -> p k n", p=P)).then_inc(w13_in[1][0], 16)
            sp.wait_ge(psum_ready, JOB[("xT2", NT - 1, 1)] + 1)
            for s in range(2):
                sp.wait_ge(xn_stored[s], 16 * NT // 2)
            sp.dma_start(w13[1][1], d["expert_w3"][1].rearrange("(k p) n -> p k n", p=P)).then_inc(w13_in[1][1], 16)
            sp.wait_ge(stage_end["E"], 4)
            sp.wait_ge(xg_in[0], 16)
            sp.dma_start(w2s[1], d["expert_w2"][1].rearrange("(k p) n -> p k n", p=P)).then_inc(w2_in[1], 16)

            def load_weights(i, s):
                e = sp.value_load(block_tab[0:1, bass.ds(2 * i + s, 1)], min_val=0, max_val=NE - 1)
                sp.wait_ge(up_part[s], 2 * i + 1)
                for n, name in enumerate(("expert_w1", "expert_w3")):
                    sp.dma_start(w13[s][n], d[name][bass.ds(e, 1)].rearrange("a (k p) n -> p (a k) n", p=P))\
                      .then_inc(w13_in[s][n], 16)
                sp.wait_ge(down_done[s], i + 1)
                sp.dma_start(w2s[s], d["expert_w2"][bass.ds(e, 1)].rearrange("a (k p) n -> p (a k) n", p=P))\
                  .then_inc(w2_in[s], 16)

            sp_blocks = sp.value_load(block_tab[0:1, 48:49], min_val=NE, max_val=NB)
            with sp.Fori(1, NB // 2) as i:
                with sp.If(2 * i < sp_blocks):
                    load_weights(i, 0)
                    with sp.If(2 * i + 1 < sp_blocks):
                        load_weights(i, 1)
            for t in range(NT):
                sp.wait_ge(g_done, t + 1)
                sp.dma_start(out[t * P:(t + 1) * P, :], y1[t % NG]).then_inc(out_stored[t % NG], 16)
            for s in range(NG):
                sp.wait_ge(out_stored[s], 16 * NT // NG)

        @block.gpsimd
        def _(pool):
            link = chain(pool, pool_step)
            link(nc.gpsimd.memset(ident, 0.0))
            link(nc.gpsimd.affine_select(out=ident, in_=ident, compare_op=ALU.not_equal, fill=1.0, base=0,
                                         pattern=[[-1, P]], channel_multiplier=1))
            link(nc.gpsimd.tensor_copy(ident_b, ident))
            link(nc.gpsimd.memset(causal, 0.0))
            link(nc.gpsimd.affine_select(out=causal, in_=causal, compare_op=ALU.is_ge, fill=NEG, base=0,
                                         pattern=[[-1, P]], channel_multiplier=1))
            link(nc.gpsimd.memset(behind, 0.0))
            link(nc.gpsimd.affine_select(out=behind, in_=behind, compare_op=ALU.is_gt, fill=NEG, base=0,
                                         pattern=[[1, P]], channel_multiplier=-1))
            link(nc.gpsimd.memset(cmask, 0.0))
            nc.gpsimd.affine_select(out=cmask, in_=cmask, compare_op=ALU.is_ge, fill=NEG, base=-31,
                                    pattern=[[P, NT], [-16, HD]], channel_multiplier=1).then_inc(pool_const, 1)
            pool.wait_ge(psum_ready, JOB["ada03"] + 1)
            nc.gpsimd.memset(conv_raw[:, :, 0:3], 0.0).then_inc(pool_const, 1)
            pool.wait_ge(hop_out, 1)
            with nc.allow_non_contiguous_dma(reason="64 values each"):
                pool.dma_start(d_hop, hop).then_inc(hop_in, 16)
                pool.wait_ge(hop_in, 16)
                pool.dma_start(hop4, d_hop.rearrange("(h c) a -> h c a", h=MH)).then_inc(hop_in, 16)
                pool.wait_ge(hop_out, 2)
                pool.dma_start(d_hop2.rearrange("(h c) a -> h c a", h=MH), hop5).then_inc(hop_in, 16)
                pool.wait_ge(hop_in, 48)
                pool.dma_start(hop2[:, 0:2], d_hop2).then_inc(hop_in, 16)
                pool.wait_ge(exp_out, 1)
                pool.dma_start(d_nmx, neg_mx).then_inc(hop_in, 16)
                pool.dma_start(d_old, hop2[:, 2:3]).then_inc(hop_in, 16)
                pool.wait_ge(hop_in, 96)
            pool.wait_ge(roped, 14)
            nc.gpsimd.memset(v1[:, :, :, P:P + 1], MH_SCALE)
            end_stage(pool, "B")
            nc.gpsimd.memset(state[0], 0.0).then_inc(state_zero, 1)
            pool.wait_ge(decay_in, 32)
            for c in range(NT):
                nc.gpsimd.affine_select(out=bc[:, :, c, :], in_=bc[:, :, c, :], compare_op=ALU.is_ge, fill=NEG, base=0,
                                        pattern=[[0, MH], [1, P]], channel_multiplier=-1).then_inc(decay_masked, 1)
            end_stage(pool, "C")
            nc.gpsimd.memset(zero_row, 0.0).then_inc(pool_e, 1)
            link(nc.gpsimd.memset(ones_sq, 1.0))
            link(nc.gpsimd.affine_select(out=upper, in_=ones_sq, compare_op=ALU.is_gt, fill=0.0, base=0,
                                         pattern=[[1, P]], channel_multiplier=-1))
            for v_, n_, b_ in ((iota32, NE, 0), (iota8, 8, 0), (iota4, 4, 0), (iota8m, 8, -64), (iota4m, 4, -64),
                               (iota15, NOV, 0), (iota48, NB, 0), (iota128, P, 0)):
                nc.gpsimd.iota(v_, [[1, n_]], base=b_, channel_multiplier=0, allow_small_or_imprecise_dtypes=True)
            nc.gpsimd.iota(tok_id, [[P, NT]], base=0, channel_multiplier=1, allow_small_or_imprecise_dtypes=True)
            for n in range(2):
                pool.wait_ge(ring_in[(IT_WOUT + n) % 3], ring_want[IT_WOUT + n])
                for k in range(4):
                    w = ring[(IT_WOUT + n) % 3][:, k, :]
                    nc.gpsimd.tensor_scalar(w, w, cols[:, 88 + k:89 + k], None, ALU.mult).then_inc(wout_scaled, 1)
            pool.wait_ge(y_zeroed, 16 * (NB - NE))
            end_stage(pool, "D")
            for s in range(2):
                pool.wait_ge(xn_stored[s], 16 * NT // 2)
            end_stage(pool, "E")
            def gather_rows(i, s):
                pool.wait_ge(xg_turned[s], i + 1)
                nc.gpsimd.tensor_copy(idx_col[s], row_tok[:, bass.ds(2 * i + s, 1)]).then_inc(idx_ready[s], 1)
                pool.wait_ge(idx_ready[s], i + 1)
                pool.sem_inc(idx_seen, 1)
                pool.indirect_dma_start(xg[s], None, d_xn,
                                        bass.IndirectOffsetOnAxis(ap=idx_col[s], axis=0)).then_inc(xg_in[s], 16)

            p_blocks = pool.value_load(block_tab[0:1, 48:49], min_val=NE, max_val=NB)
            with pool.Fori(0, NB // 2) as i:
                with pool.If(2 * i < p_blocks):
                    gather_rows(i, 0)
                    with pool.If(2 * i + 1 < p_blocks):
                        gather_rows(i, 1)
            pool.drain().then_inc(stage_f, 1)
            pool.wait_ge(stage_f, 4)
            for t in range(NT):
                if t >= NG:
                    pool.wait_ge(out_stored[t % NG], 16 * (t // NG))
                for k, y in enumerate((y1, y2)):
                    pool.indirect_dma_start(y[t % NG], None, d_y,
                                            bass.IndirectOffsetOnAxis(ap=dest[:, k, t:t + 1], axis=0)).then_inc(y_in[t % NG], 16)

        @block.scalar
        def _(act):
            link = chain(act, act_step)
            was_read(act, "vec")
            nc.scalar.activation(sc_col, cols[:, 80:88], ACT.Silu).then_inc(silu_c, 1)
            for c in range(CH):
                for t in range(4 * c, 4 * c + 4):
                    act.wait_ge(x_in[t], 16)
                    if t >= 2:
                        act.wait_ge(sq_done, t - 1)
                    nc.scalar.activation(junk[:, t % 2, :], xn[:, t, :], ACT.Square,
                                         accum_out=sum_sq[:, t:t + 1]).then_inc(sq_done, 1)
                act.wait_ge(norm_ms, c + 1)
                nc.scalar.activation(rstd[:, 4 * c:4 * c + 4], rstd[:, 4 * c:4 * c + 4], ACT.Sqrt).then_inc(norm_sqrt, 1)
            act.wait_ge(mod_ready, 1)
            for c in range(CH):
                for k in range(1, KT, 2):
                    b = ready(act, ("hT", c, k))
                    read(nc.scalar.activation(hT[:, k, 512 * c:512 * c + 512], b, ACT.Identity,
                                              scale=scale1[:, k:k + 1], bias=mod[:, k:k + 1]), ("hT", c, k))

            def copy_tokens(t):
                b = ready(act, ("tok", t))
                nc.scalar.copy(vv[:, t, :], b[:, 0:2 * P])
                read(nc.scalar.copy(gall[:, t, :], b[:, 2 * P:2 * P + 32]), ("tok", t))

            for t in range(4):
                copy_tokens(t)
            act.wait_ge(angle, 1)
            nc.scalar.activation(sin, sin, ACT.Sin).then_inc(trig, 1)
            act.wait_ge(angle, 2)
            nc.scalar.activation(cos, cos, ACT.Sin).then_inc(trig, 1)
            for t in range(4, NT):
                copy_tokens(t)
            n_rope = [0]

            def silu_conv(m):
                act.wait_ge(conv_done, m + 1)
                x_ = (mqT, mkT)[m // 4][:, m % 4, :]
                nc.scalar.activation(x_, x_, ACT.Silu)

            def exchange_halves(name, scale):
                n = n_rope[0]
                b = ready(act, name)
                if n >= 2:
                    act.wait_ge(roped, n - 1)
                for q in range(4):
                    o = q ^ 1
                    last = nc.scalar.activation(swap[32 * q:32 * q + 32, n % 2, :], b[32 * o:32 * o + 32, :], ACT.Copy,
                                                scale=scale)
                last.then_inc(swapped, 1)
                n_rope[0] += 1

            was_read(act, ("tok", NT - 1))
            nc.scalar.activation(sgate, gall[:, :, 8:32], ACT.Sigmoid).then_inc(sg_done, 1)
            for c in range(CH):
                exchange_halves(("kwn", c), 1.0)
            act.wait_ge(exp_f, 1)
            link(nc.scalar.activation(t_a, abs_f, ACT.Exp, scale=-1.0))
            nc.scalar.activation(t_a, t_a, ACT.Ln, bias=1.0).then_inc(ln_f, 1)
            for j in range(4):
                if j == 3:
                    act.wait_ge(exp_in, 1)
                    for o in (dec_, em_, wp_, hop2[:, 2:3]):
                        last = nc.scalar.activation(o, o, ACT.Exp)
                    last.then_inc(exp_out, 1)
                for c in range(CH):
                    exchange_halves(("q", j, c), HD ** -0.5)
            for n in ("kc", "ksl"):
                for c in range(CH):
                    exchange_halves((n, c), 1.0)
            for c in range(CH):
                b = ready(act, ("vc", c))
                for g in range(2):
                    for o in range(2):
                        last = nc.scalar.copy(pairs_kv[1][HD * o:HD * o + HD, 512 * g + 256 * c:512 * g + 256 * c + 256],
                                              b[HD * g:HD * g + HD, o::2])
                read(last, ("vc", c))
            act.wait_ge(pool_const, 2)
            for i, n in enumerate(("mq", "mk")):
                dst = (mqT, mkT)[i]
                for j in range(4):
                    m = 4 * i + j
                    if m >= 2:
                        act.wait_ge(conv_done, m - 1)
                    for c in range(CH):
                        b = ready(act, (n, j, c))
                        read(nc.scalar.copy(conv_raw[:, m % 2, 3 + 512 * c:515 + 512 * c], b), (n, j, c))
                    if m >= 1:
                        silu_conv(m - 1)
            silu_conv(7)
            act.wait_ge(roped, 14)
            for t in range(NT):
                b = ready(act, ("mv", t))
                read(nc.scalar.activation(v1[:, t, :, 0:P], b.rearrange("p (h n) -> p h n", h=MH), ACT.Copy,
                                          scale=MH_SCALE), ("mv", t))
            act.wait_ge(hop_in, 96)
            for t in range(NT):
                b = ready(act, ("mo", t))
                read(nc.scalar.activation(ym[:, t, :], b, ACT.Sigmoid), ("mo", t))
            end_stage(act, "B")

            for a in range(2):
                act.wait_ge(hbias_ready, a + 1)
                b = ready(act, ("chid", a))
                read(nc.scalar.activation(hid[:, a, :, :], b[:, 0:P].rearrange("p (g n) -> p g n", g=2), ACT.Silu,
                                          bias=hbias[:, a:a + 1]), ("chid", a))
            b = ready(act, "vcmp")
            read(nc.scalar.copy(v_cmp[0:NCMP], b[0:NCMP, 0:P].rearrange("p (g n) -> p g n", g=2)), "vcmp")
            for c in range(NT):
                act.wait_ge(decay_masked, c + 1)
                for h in range(MH):
                    last = nc.scalar.activation(bc[:, h, c, :], bc[:, h, c, :], ACT.Exp,
                                                bias=gcols[:, 0, 8 * h + c:8 * h + c + 1])
                last.then_inc(decay_exp, 1)
            def weigh_keys(c):
                b = ready(act, ("kr", c))
                if c >= 2:
                    act.wait_ge(psum_ready, JOB[("kv", c - 2, 1)] + 1)
                for h in range(MH):
                    r = 8 * h + c
                    last = nc.scalar.activation(kw[c % 2][:, h, :], b[:, P * h:P * h + P], ACT.Copy,
                                                scale=gcols[:, 3, r:r + 1])
                read(last, ("kr", c))

            weigh_keys(0)
            for c in range(NT):
                if c + 2 < NT:
                    weigh_keys(c + 1)
                for p in range(2):
                    b = ready(act, ("int", c, p))
                    if c >= 2:
                        was_read(act, ("num", c - 2, p))
                    for h in range(2):
                        r = 8 * (2 * p + h) + c
                        last = nc.scalar.activation(inter[c % 2][:, 2 * p + h, :], b[:, 129 * h:129 * h + 129], ACT.Copy,
                                                    scale=gcols[:, 1, r:r + 1])
                    read(last, ("int", c, p))
                act.wait_ge(h_den, c + 1)
                if c:
                    act.wait_ge(h_sqrt, c)
                for h in range(MH):
                    last = nc.scalar.activation(junk_h[:, h, :], num[c % 2][:, h, 0:P], ACT.Square,
                                                scale=inv_den[:, c % 2, h:h + 1], accum_out=ssq4[:, c % 2, h:h + 1])
                last.then_inc(h_sq, 1)
                act.wait_ge(h_sq, c + 1)
                nc.scalar.activation(rs4[:, c % 2, :], ssq4[:, c % 2, :], ACT.Sqrt, scale=1.0 / P,
                                     bias=eps_col).then_inc(h_sqrt, 1)
            end_stage(act, "C")
            for e in EVENTS:
                if e[0] == "scores":
                    _, x, kind, h = e
                    u, n = UNIT[e[1:]], key_count(x, kind)
                    act.wait_ge(row_max, u + 1)
                    if x:
                        act.wait_ge(turned_ready, LAST_TURN[(x - 1, kind)])
                    if x >= 2:
                        act.wait_ge(heads_done, x - 1)
                    k = "csw".index(kind)
                    if kind == "c":
                        for h in range(4):
                            last = nc.scalar.activation(probs["c"][h][:, 0:n], scores(u)[:, HD * h:HD * h + n], ACT.Exp,
                                                        bias=nmax[:, u % 4, h:h + 1], accum_out=sums[:, x % 2, k, h:h + 1])
                    else:
                        last = nc.scalar.activation(probs[kind][h][:, 0:n], scores(u)[:, 0:n], ACT.Exp,
                                                    bias=nmax[:, u % 4, 0:1], accum_out=sums[:, x % 2, k, h:h + 1])
                    last.then_inc(probs_ready, 1)
                if e[0] == "turn":
                    evacuate_turned(act, nc.scalar.copy, e, 0)
                if e[0] == "out_copy":
                    x = e[1]
                    act.wait_ge(pv_done, PV_AT[(x, "w", len(key_blocks(x, "w")) - 1)] + 1)
                    if x:
                        act.wait_ge(turned_ready, LAST_TURN[(x - 1, "o")])
                    nc.scalar.copy(out_T, ps[:, 6, :]).then_inc(out_copied, 1)
            end_stage(act, "D")

            def e_turned(t):
                b = ready(act, ("yT", t, 0))
                if t >= 2:
                    act.wait_ge(psum_ready, JOB[("out", t - 2, 1)] + 1)
                read(nc.scalar.copy(yT[t % 2][:, 0:4, :], b.rearrange("p (k n) -> p k n", n=P)), ("yT", t, 0))

            def e_router(t):
                b = ready(act, ("xT2", t, 0))
                if t >= 1:
                    act.wait_ge(psum_ready, JOB[("lg", t - 1)] + 1)
                for k in range(4):
                    last = nc.scalar.activation(h2T[:, k, :], b[:, P * k:P * k + P], ACT.Identity,
                                                scale=scale2[:, k:k + 1], bias=mod[:, 24 + k:25 + k])
                read(last, ("xT2", t, 0))

            e_turned(0)
            for t in range(NT):
                if t + 1 < NT:
                    e_turned(t + 1)
                if t:
                    act.wait_ge(x2_done, t)
                for n in range(2):
                    b = ready(act, ("out", t, n))
                    read(nc.scalar.copy(y_row[:, 512 * n:512 * n + 512], b), ("out", t, n))
                    if t and n == 0:
                        e_router(t - 1)
                for n in range(2):
                    was_read(act, ("out", t, n))
                if t:
                    act.wait_ge(x_sq, t)
                nc.scalar.activation(junk_e, y_row, ACT.Square, accum_out=ys).then_inc(y_sq, 1)
                act.wait_ge(y_ms, t + 1)
                nc.scalar.activation(rs_y, ys, ACT.Sqrt).then_inc(y_sqrt, 1)
                act.wait_ge(x2_done, t + 1)
                act.wait_ge(y_sq, t + 1)
                nc.scalar.activation(junk_e, x2[:, t, :], ACT.Square, accum_out=xs_).then_inc(x_sq, 1)
                act.wait_ge(x_ms, t + 1)
                nc.scalar.activation(rs_x, xs_, ACT.Sqrt).then_inc(x_sqrt, 1)
            e_router(NT - 1)
            act.wait_ge(exp_args, 1)
            nc.scalar.activation(dg, dg, ACT.Exp).then_inc(exps_done, 1)
            nc.scalar.activation(e2, e2, ACT.Exp).then_inc(exps_done, 1)
            end_stage(act, "E")

            for s in range(2):
                act.sem_inc(y_stored[s], 16)

            def silu_and_store(i, s):
                act.wait_ge(up_part[s], 2 * i + 2)
                nc.scalar.activation(act1[s], ps[:, 2, :], ACT.Silu).then_inc(silu_part[s], 1)
                act.wait_ge(yo_ready[s], i + 2)
                act.dma_start(d_y[bass.ds(256 * i + P * s, P), :], yo[s]).then_inc(y_stored[s], 16)

            a_blocks = act.value_load(block_tab[0:1, 48:49], min_val=NE, max_val=NB)
            with act.Fori(0, NB // 2) as i:
                with act.If(2 * i < a_blocks):
                    silu_and_store(i, 0)
                    with act.If(2 * i + 1 < a_blocks):
                        silu_and_store(i, 1)
            act.wait_ge(y_stored[0], 16 * ((a_blocks + 1) // 2) + 16)
            act.sem_inc(store_seen, 1)
            act.wait_ge(y_stored[1], 16 * (a_blocks // 2) + 16)
            act.sem_inc(store_seen, 1)
            act.drain().then_inc(stage_f, 1)
            act.wait_ge(stage_f, 4)

            def scale_first(t):
                act.wait_ge(y_in[t % NG], 32 * (t // NG) + 32)
                nc.scalar.activation(y1[t % NG], y1[t % NG], ACT.Copy, scale=gates2[:, 0, t:t + 1]).then_inc(g_scaled, 1)

            scale_first(0)
            for t in range(NT):
                if t + 1 < NT:
                    scale_first(t + 1)
                act.wait_ge(g_added, t + 1)
                if t >= 2:
                    act.wait_ge(g_done, t - 1)
                nc.scalar.activation(junk_g, y1[t % NG], ACT.Square, accum_out=sum_g[:, t % 2:t % 2 + 1]).then_inc(g_sq, 1)
                act.wait_ge(g_sq, t + 1)
                nc.scalar.activation(rs_g[:, t % 2:t % 2 + 1], sum_g[:, t % 2:t % 2 + 1], ACT.Sqrt, scale=1.0 / D,
                                     bias=eps_col).then_inc(g_sqrt, 1)

        @block.tensor
        def _(pe):
            def last_of(ins):
                ins.then_inc(psum_ready, 1)

            def item(i):
                pe.wait_ge(ring_in[i % 3], ring_want[i])
                return ring[i % 3]

            def modulation(b, i, at_col):
                pe.wait_ge(ada_summed, i + 1)
                for m in range(4):
                    last = nc.tensor.matmul(b[:, at_col + m:at_col + m + 1], ada_sum[i // 4][:, i % 4, P * m:P * m + P],
                                            ones, start=True, stop=True)
                return last

            def transpose_x(c, k):
                b = claim(pe, ("hT", c, k))
                for t in range(4):
                    last = nc.tensor.transpose(b[:, P * t:P * t + P], xn[:, 4 * c + t, P * k:P * k + P], ident)
                last_of(last)

            pe.wait_ge(vec_in, 128)
            pe.wait_ge(pool_const, 1)
            b = claim(pe, "vec")
            last_of(nc.tensor.transpose(b[:, 0:124], vec, ident[0:124, 0:124]))
            pe.wait_ge(xn_done, 4)
            for k in range(6):
                transpose_x(0, k)
            b = claim(pe, "ada03")
            for i in range(4):
                last = modulation(b, i, 4 * i)
            last_of(last)
            for k in range(6, KT):
                transpose_x(0, k)
            pe.wait_ge(xn_done, NT)
            for k in range(KT):
                transpose_x(1, k)
            for k in range(KT):
                was_read(pe, ("hT", 1, k))

            def features(name, w, c):
                b = claim(pe, name)
                for k in range(KT):
                    last = nc.tensor.matmul(b, w(k), hT[:, k, 512 * c:512 * c + 512], start=(k == 0), stop=(k == KT - 1))
                last_of(last)

            def tokens(name, w, at_col, width, t):
                b = claim(pe, name)
                for k in range(KT):
                    last = nc.tensor.matmul(b[:, 0:width], hT[:, k, P * t:P * t + P], w[:, k, at_col:at_col + width],
                                            start=(k == 0), stop=(k == KT - 1))
                last_of(last)

            w = item(IT_KWN)
            for t in range(NT):
                tokens(("tok", t), w, P, 2 * P + 32, t)
            for c in range(CH):
                features(("kwn", c), lambda k: w[:, k, 0:P], c)
            pe.wait_ge(gates_in_cols, 1)
            b = claim(pe, "gT")
            nc.tensor.transpose(b[0:32, 0:P], gi_cols.rearrange("p h c -> p (h c)"), ident)
            last_of(nc.tensor.transpose(b[0:32, P:2 * P], gf_cols.rearrange("p h c -> p (h c)"), ident))
            w = item(IT_NQ)
            for j in range(4):
                for c in range(CH):
                    features(("q", j, c), lambda k: w[:, k, P * j:P * j + P], c)
                if j == 2:
                    last_of(modulation(claim(pe, ("ada", 4)), 4, 0))
            pe.wait_ge(exp_out, 1)
            b = claim(pe, "gcol")
            for n, a in enumerate((u_, dec_, em_, wp_)):
                last = nc.tensor.transpose(b[:, 32 * n:32 * n + 32], a, ident[0:32, 0:32])
            last_of(last)
            last_of(modulation(claim(pe, ("ada", 5)), 5, 0))
            w = item(IT_KC)
            for n, at_ in (("kc", 0), ("ksl", 256), ("vc", 128)):
                for c in range(CH):
                    features((n, c), lambda k: w[:, k, at_:at_ + P], c)
            last_of(modulation(claim(pe, ("ada", 6)), 6, 0))
            for n, it in (("mq", IT_MQ), ("mk", IT_MK)):
                w = item(it)
                for j in range(4):
                    for c in range(CH):
                        features((n, j, c), lambda k: w[:, k, P * j:P * j + P], c)
                if n == "mq":
                    last_of(modulation(claim(pe, ("ada", 7)), 7, 0))
            w = item(IT_MV)
            for t in range(NT):
                tokens(("mv", t), w, 0, 512, t)
                if t % 4 == 3:
                    last_of(modulation(claim(pe, ("ada", 8 + t // 4)), 8 + t // 4, 0))
            w = item(IT_MO)
            for t in range(NT):
                tokens(("mo", t), w, 0, 512, t)
            for i in (10, 11):
                last_of(modulation(claim(pe, ("ada", i)), i, 0))
            end_stage(pe, "B")

            pe.wait_ge(const_in, 144)
            for a in range(2):
                w = item(IT_CMP + a).rearrange("p k n -> p (k n)").rearrange("p (k n) -> p k n", n=P)
                b = claim(pe, ("chid", a))
                for j in range(16):
                    last = nc.tensor.matmul(b[:, 0:P + 1], w[:, j, :], pairs_kv[a][:, j:j + 8 * P + 1:8],
                                            start=(j == 0), stop=(j == 15))
                last_of(last)
            was_read(pe, ("chid", 0))
            b = claim(pe, "kcmp")
            for g in range(2):
                last = nc.tensor.matmul(b[HD * g:HD * g + HD, 0:NCMP], w2c[:, 0, :], hid[:, 0, g, 0:NCMP],
                                        start=True, stop=True)
            last_of(last)
            was_read(pe, ("chid", 1))
            b = claim(pe, "vcmp")
            for g in range(2):
                last = nc.tensor.matmul(b[0:NCMP, HD * g:HD * g + HD], hid[:, 1, g, 0:NCMP], w2c[:, 1, :],
                                        start=True, stop=True)
            last_of(last)

            def scores_and_keys(c):
                at_c = slice(P * c, P * c + P)
                b = claim(pe, ("S", c))
                for h in range(MH):
                    last = nc.tensor.matmul(b[:, P * h:P * h + P], mkT[:, h, at_c], mqT[:, h, at_c], start=True, stop=True)
                last_of(last)
                if c + 1 < NT:
                    b = claim(pe, ("kr", c))
                    for h in range(MH):
                        last = nc.tensor.transpose(b[:, P * h:P * h + P], mkT[:, h, at_c], ident)
                    last_of(last)

            def heads(name, c, lhsT, rhs):
                for p in range(2):
                    b = claim(pe, (name, c, p))
                    for h in range(2):
                        last = nc.tensor.matmul(b[:, 129 * h:129 * h + 129], lhsT[:, 2 * p + h, :], rhs[:, 2 * p + h, :],
                                                start=True, stop=True)
                    last_of(last)

            scores_and_keys(0)
            for c in range(NT):
                if c + 1 < NT:
                    scores_and_keys(c + 1)
                was_read(pe, ("S", c))
                heads("num", c, wts[c % 2], v1[:, c])
                if c + 1 < NT:
                    was_read(pe, ("kr", c))
                    heads("kv", c, kw[c % 2], v1[:, c])
                if c:
                    was_read(pe, ("kv", c - 1, 1))
                else:
                    pe.wait_ge(state_zero, 1)
                heads("int", c, mqT[:, :, P * c:P * c + P], state[c % 2])
            end_stage(pe, "C")
            def free_turn_bank(q):
                if q >= 2:
                    f = [f for f in TURN if TURN[f] == q - 2][0]
                    if f[0] == "out_turn":
                        pe.wait_ge(heads_done, f[1] + 1)
                    else:
                        pe.wait_ge(turned_read[q % 2], sum(1 for g in TURN if g[0] == "turn" and TURN[g] % 2 == q % 2 and TURN[g] < q))
                return ps[:, 4 + q % 2, :]

            for e in EVENTS:
                if e[0] == "scores":
                    _, x, kind, h = e
                    t, g = divmod(x, 2)
                    u, n = UNIT[e[1:]], key_count(x, kind)
                    half = slice(HD * g, HD * g + HD)
                    sc = scores(u)
                    if u >= 2:
                        pe.wait_ge(probs_ready, u - 1)
                    if kind == "c":
                        for h in range(4):
                            nc.tensor.matmul(sc[:, HD * h:HD * h + n], qT[half, h, P * t:P * t + P], k_cmp[half, 0:n],
                                             start=True, stop=False)
                            last = nc.tensor.matmul(sc[:, HD * h:HD * h + n], ident_b, cmask[:, t, 0:n], start=False, stop=True)
                    else:
                        src = kslT if kind == "s" else kwnT
                        first = key_blocks(x, kind)[0]
                        for at_ in range(0, n, 512):
                            w = min(512, n - at_)
                            far = kind == "w" and t >= 4 and at_ == 0
                            near = at_ + w == n
                            last = nc.tensor.matmul(sc[:, at_:at_ + w], qT[half, h, P * t:P * t + P],
                                                    src[half, P * first + at_:P * first + at_ + w],
                                                    start=True, stop=not (near or far))
                            if far:
                                last = nc.tensor.matmul(sc[:, 0:P], ident_b, behind, start=False, stop=not near)
                            if near:
                                last = nc.tensor.matmul(sc[:, n - P:n], ident_b, causal, start=False, stop=True)
                    last.then_inc(scores_ready, 1)
                if e[0] == "turn":
                    _, x, kind, b = e
                    bank_ = free_turn_bank(TURN[e])
                    n = key_count(x, kind)
                    if b == 0:
                        pe.wait_ge(probs_ready, UNIT[(x, kind, heads_of(kind)[-1])] + 1)
                    for h in range(4):
                        w = n if kind == "c" else P
                        last = nc.tensor.transpose(bank_[0:w, P * h:P * h + P], probs[kind][h][:, P * b:P * b + w], ident)
                    last.then_inc(turned_ready, 1)
                if e[0] == "values":
                    _, x, kind, b = e
                    t, g = divmod(x, 2)
                    q = TURN[("turn", x, kind, b)]
                    pe.wait_ge(turned_read[q % 2], sum(1 for f in TURN if f[0] == "turn" and TURN[f] % 2 == q % 2 and TURN[f] <= q))
                    if kind == "c":
                        if x:
                            pe.wait_ge(heads_done, x)
                        n = key_count(x, kind)
                        for h in range(4):
                            last = nc.tensor.matmul(ps[:, 7, HD * h:HD * h + HD], probs_T[q % 2][0:n, P * h:P * h + P],
                                                    v_cmp[0:n, g, :], start=True, stop=True)
                    else:
                        if x and kind == "s" and b == 0:
                            pe.wait_ge(out_copied, x)
                        lo = HD * "sw".index(kind)
                        blocks = key_blocks(x, kind)
                        last = nc.tensor.matmul(ps[lo:lo + HD, 6, :], vv[:, blocks[b], 2 * lo + HD * g:2 * lo + HD * g + HD],
                                                probs_T[q % 2], start=(b == 0), stop=(b == len(blocks) - 1))
                    last.then_inc(pv_done, 1)
                if e[0] == "out_turn":
                    x = e[1]
                    bank_ = free_turn_bank(TURN[e])
                    pe.wait_ge(out_copied, x + 1)
                    for h in range(4):
                        last = nc.tensor.transpose(bank_[:, P * h:P * h + P], out_T[:, P * h:P * h + P], ident)
                    last.then_inc(turned_ready, 1)
            end_stage(pe, "D")

            pe.wait_ge(diag_ready, 1)
            for i in range(2):
                dgr = diag[i].rearrange("p k n -> p (k n)")
                for n in range(2):
                    b = claim(pe, ("row", i, n))
                    last_of(nc.tensor.matmul(b, ones_sq, dgr[:, 512 * n:512 * n + 512], start=True, stop=True))

            def e_turn(t):
                for n, y in enumerate((ym, yn)):
                    b = claim(pe, ("yT", t, n))
                    for k in range(4):
                        last = nc.tensor.transpose(b[:, P * k:P * k + P], y[:, t, P * k:P * k + P], ident)
                    last_of(last)

            def e_turn_x(t):
                pe.wait_ge(xn2_done, t + 1)
                for n in range(2):
                    b = claim(pe, ("xT2", t, n))
                    for k in range(4):
                        last = nc.tensor.transpose(b[:, P * k:P * k + P], xn2[t % 2][:, P * (4 * n + k):P * (4 * n + k) + P], ident)
                    last_of(last)

            def e_logits(t):
                b = claim(pe, ("lg", t))
                for n in range(2):
                    was_read(pe, ("xT2", t, n))
                for k in range(KT):
                    last = nc.tensor.matmul(b[:, 0:36], h2T[:, k, :], w_router[:, k, :], start=(k == 0), stop=(k == KT - 1))
                last_of(last)

            pe.wait_ge(router_in, 64)
            pe.wait_ge(wout_scaled, 8)
            e_turn(0)
            for t in range(NT):
                if t + 1 < NT:
                    e_turn(t + 1)
                for n in range(2):
                    was_read(pe, ("yT", t, n))
                for n in range(2):
                    b = claim(pe, ("out", t, n))
                    w = ring[(IT_WOUT + n) % 3]
                    for k in range(KT):
                        last = nc.tensor.matmul(b, yT[t % 2][:, k, :], w[:, k, :], start=(k == 0), stop=(k == KT - 1))
                    last_of(last)
                    if t and n == 0:
                        e_turn_x(t - 1)
                    if t and n == 1:
                        e_logits(t - 1)
            e_turn_x(NT - 1)
            e_logits(NT - 1)
            pe.wait_ge(hots_ready, 1)
            b = claim(pe, "rank")
            hv = hots.rearrange("p t e -> p (t e)")
            nc.tensor.matmul(b[:, 0:256], upper, hv, start=True, stop=True)
            last_of(nc.tensor.matmul(b[:, 256:512], ones_sq, hv, start=True, stop=True))
            b = claim(pe, "table")
            for n in range(2 * NT):
                if n % 4 == 0:
                    pe.wait_ge(slots_hot, n // 4 + 1)
                last = nc.tensor.matmul(b[:, 0:NB], lane_hot[:, n, :], tok_hot[:, n, :], start=(n == 0), stop=(n == 2 * NT - 1))
            last_of(last)
            end_stage(pe, "E")

            def f_turn(s, n, other):
                pe.wait_ge(xg_in[s], 16 * n + 16)
                if other is not None:
                    pe.wait_ge(xgT_ready[1 - s], other)
                for k in range(KT):
                    last = nc.tensor.transpose(ps[:, k // 4, P * (k % 4):P * (k % 4) + P], xg[s][:, P * k:P * k + P], ident)
                last.then_inc(xg_turned[s], 1)

            def f_up(i, s):
                pe.wait_ge(xgT_ready[s], i + 1)
                for n in range(2):
                    pe.wait_ge(w13_in[s][n], 16 * i + 16)
                    for k in range(KT):
                        last = nc.tensor.matmul(ps[:, 2 + n, :], xgT[s][:, k, :], w13[s][n][:, k, :],
                                                start=(k == 0), stop=(k == KT - 1))
                    last.then_inc(up_part[s], 1)

            def f_down(i, s):
                pe.wait_ge(hid_part[s], i + 1)
                for k in range(4):
                    last = nc.tensor.transpose(ps[:, 4 + k // 2, P * (k % 2):P * (k % 2) + P],
                                               hid_e[s][:, P * k:P * k + P], ident)
                    if k % 2:
                        last.then_inc(hid_turned[s], 1)
                pe.wait_ge(w2_in[s], 16 * i + 16)
                pe.wait_ge(yo_ready[1 - s], i + s + 1)
                for k in range(4):
                    if k % 2 == 0:
                        pe.wait_ge(hidT_read[s], 2 * i + 1 + k // 2)
                    for n in range(2):
                        last = nc.tensor.matmul(ps[:, 6 + n, :], hid_T[s][:, k, :], w2s[s][:, k, 512 * n:512 * n + 512],
                                                start=(k == 0), stop=(k == 3))
                last.then_inc(down_done[s], 1)

            e_blocks = pe.value_load(block_tab[0:1, 48:49], min_val=NE, max_val=NB)
            for s in range(2):
                for credit in (up_part, xg_turned, down_done):
                    pe.sem_inc(credit[s], 1)
            f_turn(0, 0, None)
            with pe.Fori(0, NB // 2) as i:
                with pe.If(2 * i < e_blocks):
                    f_up(i, 0)
                    with pe.If(2 * i + 1 < e_blocks):
                        f_turn(1, i, i + 1)
                    f_down(i, 0)
                    with pe.If(2 * i + 1 < e_blocks):
                        f_up(i, 1)
                        with pe.If(2 * i + 2 < e_blocks):
                            f_turn(0, i + 1, i + 1)
                        f_down(i, 1)
            pe.drain().then_inc(stage_f, 1)

        @block.vector
        def _(dve):
            link = chain(dve, dve_step)
            V = nc.vector
            V.memset(ones, 1.0)
            link(V.memset(eps_col, EPS))
            b = ready(dve, "vec")
            read(V.tensor_copy(cols, b[:, 0:124]), "vec")
            was_read(dve, "vec")
            for c in range(CH):
                dve.wait_ge(sq_done, 4 * c + 4)
                V.tensor_scalar(rstd[:, 4 * c:4 * c + 4], sum_sq[:, 4 * c:4 * c + 4], 1.0 / D, EPS,
                                ALU.mult, ALU.add).then_inc(norm_ms, 1)
                dve.wait_ge(norm_sqrt, c + 1)
                link(V.reciprocal(rstd[:, 4 * c:4 * c + 4], rstd[:, 4 * c:4 * c + 4]))
                for t in range(4 * c, 4 * c + 4):
                    V.tensor_scalar(xn[:, t, :], xn[:, t, :], rstd[:, t:t + 1], None, ALU.mult).then_inc(xn_done, 1)

            def sum_modulation(i):
                it = IT_ADA[i]
                dve.wait_ge(ring_in[it % 3], ring_want[it])
                w, to = ring[it % 3], ada_sum[i // 4][:, i % 4, :]
                link(V.tensor_scalar(to, w[:, 0, :], sc_col[:, 0:1], None, ALU.mult))
                for k in range(1, KT):
                    ins = V.scalar_tensor_tensor(to, w[:, k, :], sc_col[:, k:k + 1], to, ALU.mult, ALU.add)
                    if k < KT - 1:
                        link(ins)
                ins.then_inc(ada_summed, 1)

            def modulation(i):
                b = ready(dve, ("ada", i))
                read(V.tensor_tensor(mod[:, 4 * i:4 * i + 4], b[:, 0:4], cols[:, 4 * i:4 * i + 4], ALU.add), ("ada", i))

            dve.wait_ge(silu_c, 1)
            for i in range(4):
                sum_modulation(i)
            b = ready(dve, "ada03")
            read(V.tensor_tensor(mod[:, 0:16], b[:, 0:16], cols[:, 0:16], ALU.add), "ada03")
            was_read(dve, "ada03")
            V.scalar_tensor_tensor(scale1, mod[:, 8:16], 1.0, cols[:, 48:56], ALU.add, ALU.mult).then_inc(mod_ready, 1)
            dve.wait_ge(mod_ready, 1)
            for c in range(CH):
                for k in range(0, KT, 2):
                    b = ready(dve, ("hT", c, k))
                    read(V.tensor_scalar(hT[:, k, 512 * c:512 * c + 512], b, scale1[:, k:k + 1], mod[:, k:k + 1],
                                         ALU.mult, ALU.add), ("hT", c, k))
            dve.wait_ge(const_in, 144)
            link(V.tensor_copy(pos_f, pos_i))
            link(V.tensor_scalar(ang, pos_f, freq[:, 0:1], None, ALU.mult))
            for n, (dst, turn, back) in enumerate(((sin, 0.0, 0.0), (cos, 0.25, float(np.pi / 2)))):
                link(V.tensor_scalar(turns, ang, 1.0 / TWO_PI, turn, ALU.mult, ALU.add))
                link(V.tensor_scalar(turns, turns, ROUND, None, ALU.add))
                link(V.tensor_scalar(turns, turns, ROUND, None, ALU.subtract))
                link(V.scalar_tensor_tensor(dst, turns, -PI2[0], ang, ALU.mult, ALU.add))
                link(V.scalar_tensor_tensor(dst, turns, -PI2[1], dst, ALU.mult, ALU.add))
                link(V.scalar_tensor_tensor(dst, turns, -PI2[2], dst, ALU.mult, ALU.add))
                link(V.tensor_scalar(dst, dst, back, PI_IN, ALU.add, ALU.min))
                V.tensor_scalar(dst, dst, -PI_IN, None, ALU.max).then_inc(angle, 1)

            dve.wait_ge(trig, 1)
            link(V.tensor_scalar(sin, sin, freq[:, 1:2], None, ALU.mult))
            dve.wait_ge(trig, 2)
            for t in range(NT):
                was_read(dve, ("tok", t))
            g = gall.rearrange("p c n -> p n c")
            V.tensor_tensor(gi_cols, g[:, 0:MH, :], gate_b[:, 0:MH].unsqueeze(2).broadcast_to([P, MH, NT]), ALU.add)
            V.tensor_tensor(gf_cols, g[:, MH:2 * MH, :], gate_b[:, MH:2 * MH].unsqueeze(2).broadcast_to([P, MH, NT]),
                            ALU.add).then_inc(gates_in_cols, 1)
            n_rope = [0]

            def rope(name, dst, c, scale):
                n = n_rope[0]
                dve.wait_ge(swapped, n + 1)
                b = ready(dve, name)
                read(V.scalar_tensor_tensor(turned[:, n % 2, :], b, scale, cos[:, 512 * c:512 * c + 512],
                                            ALU.mult, ALU.mult), name)
                link(V.tensor_tensor(swap[:, n % 2, :], swap[:, n % 2, :], sin[:, 512 * c:512 * c + 512], ALU.mult))
                was_read(dve, name)
                if dst is not None:
                    last = V.tensor_tensor(dst[:, 512 * c:512 * c + 512], turned[:, n % 2, :], swap[:, n % 2, :], ALU.add)
                else:
                    for g in range(2):
                        half = slice(HD * g, HD * g + HD)
                        for o in range(2):
                            last = V.tensor_tensor(pairs_kv[0][HD * o:HD * o + HD, 512 * g + 256 * c:512 * g + 256 * c + 256],
                                                   turned[half, n % 2, o::2], swap[half, n % 2, o::2], ALU.add)
                last.then_inc(roped, 1)
                n_rope[0] += 1

            def rope_q(j):
                for c in range(CH):
                    rope(("q", j, c), qT[:, j, :], c, HD ** -0.5)

            for c in range(CH):
                rope(("kwn", c), kwnT, c, 1.0)
            b = ready(dve, "gT")
            V.tensor_copy(g_i, b[0:32, 0:P])
            read(V.tensor_copy(g_f, b[0:32, P:2 * P]), "gT")
            was_read(dve, "gT")
            V.scalar_tensor_tensor(abs_f, g_f, -1.0, g_f, ALU.mult, ALU.max).then_inc(exp_f, 1)
            rope_q(0)
            link(V.memset(ones_r, 1.0))
            dve.wait_ge(ln_f, 1)
            link(V.scalar_tensor_tensor(g_f, g_f, 0.0, t_a, ALU.min, ALU.subtract))
            link(V.tensor_tensor_scan(decay_b, ones_r, g_f, 0.0, ALU.mult, ALU.add))
            link(V.tensor_tensor(u_, g_i, decay_b, ALU.subtract))
            link(V.tensor_tensor_scan(cmax, u_, u_, -3e38, ALU.max, ALU.max))
            V.tensor_copy(hop[:, 0:1], decay_b[:, P - 1:P])
            V.tensor_tensor(hop[:, 1:2], decay_b[:, P - 1:P], cmax[:, P - 1:P], ALU.add).then_inc(hop_out, 1)
            sum_modulation(4)
            dve.wait_ge(hop_in, 32)
            link(V.memset(hop5, 0.0))
            link(V.tensor_tensor_scan(hop5[:, :, 1], hop4[:, :, 0], hop4[:, :, 1], 0.0, ALU.add, ALU.max))
            V.tensor_copy(hop5[:, 1:8, 0], hop5[:, 0:7, 1]).then_inc(hop_out, 1)
            rope_q(1)
            dve.wait_ge(hop_in, 64)
            m_old, m_new = hop2[:, 0:1], hop2[:, 1:2]
            link(V.tensor_scalar(mx, cmax, m_old, None, ALU.max))
            V.tensor_scalar(neg_mx, mx, -1.0, None, ALU.mult)
            V.tensor_scalar(dec_, mx, -1.0, m_old, ALU.mult, ALU.add)
            link(V.tensor_tensor(gm32, hop[:, 0:1], m_new, ALU.subtract))
            link(V.scalar_tensor_tensor(em_, mx, -1.0, decay_b, ALU.mult, ALU.subtract))
            link(V.tensor_scalar(wp_, u_, gm32, None, ALU.add))
            V.tensor_tensor(hop2[:, 2:3], gm32, m_old, ALU.add).then_inc(exp_in, 1)
            rope_q(2)
            modulation(4)
            sum_modulation(5)
            rope_q(3)
            dve.wait_ge(exp_out, 1)
            b = ready(dve, "gcol")
            read(V.tensor_copy(gcols, b[:, 0:P].rearrange("p (a r) -> p a r", a=4)), "gcol")
            modulation(5)
            for n, dst in (("kc", None), ("ksl", kslT)):
                for c in range(CH):
                    rope((n, c), dst, c, 1.0)
            sum_modulation(6)
            modulation(6)
            for i, n in enumerate(("mq", "mk")):
                dst = (mqT, mkT)[i]
                for j in range(4):
                    m = 4 * i + j
                    was_read(dve, (n, j, 0))
                    was_read(dve, (n, j, 1))
                    tap = lambda s: cols[:, 92 + 8 * s + m:93 + 8 * s + m]
                    link(V.tensor_scalar(dst[:, j, :], conv_raw[:, m % 2, 0:S], tap(0), None, ALU.mult))
                    for s in range(1, 4):
                        ins = V.scalar_tensor_tensor(dst[:, j, :], conv_raw[:, m % 2, s:s + S], tap(s), dst[:, j, :],
                                                     ALU.mult, ALU.add)
                        if s < 3:
                            link(ins)
                    ins.then_inc(conv_done, 1)
                    if m == 2:
                        sum_modulation(7)
                    if m == 3:
                        modulation(7)
            for i in (8, 10):
                sum_modulation(i)
                sum_modulation(i + 1)
                modulation(i)
                modulation(i + 1)
            end_stage(dve, "B")

            link(V.scalar_tensor_tensor(scale2, mod[:, 32:40], 1.0, cols[:, 64:72], ALU.add, ALU.mult))
            link(V.tensor_tensor(gm_col[:, 0, :], mod[:, 16:24], cols[:, 56:64], ALU.mult))
            link(V.tensor_tensor(gm_col[:, 1, :], mod[:, 40:48], cols[:, 72:80], ALU.mult))
            for a in range(2):
                b = ready(dve, ("chid", a))
                V.tensor_copy(hbias[:, a:a + 1], b[:, P:P + 1]).then_inc(hbias_ready, 1)
            b = ready(dve, "kcmp")
            read(V.tensor_copy(k_cmp[:, 0:NCMP], b[:, 0:NCMP]), "kcmp")
            def weights(c):
                dve.wait_ge(decay_exp, c + 1)
                b = ready(dve, ("S", c))
                if c >= 2:
                    dve.wait_ge(psum_ready, JOB[("num", c - 2, 1)] + 1)
                read(V.tensor_tensor(wts[c % 2], b.rearrange("p (h n) -> p h n", h=MH), bc[:, :, c, :], ALU.mult),
                     ("S", c))

            def update_state(c):
                if c:
                    was_read(dve, ("kv", c - 1, 1))
                    dve.wait_ge(psum_ready, JOB[("int", c - 1, 1)] + 1)
                else:
                    dve.wait_ge(state_zero, 1)
                for p in range(2):
                    b = ready(dve, ("kv", c, p))
                    for h in range(2):
                        r = 8 * (2 * p + h) + c
                        last = V.scalar_tensor_tensor(state[(c + 1) % 2][:, 2 * p + h, :], state[c % 2][:, 2 * p + h, :],
                                                      a_old[:, r:r + 1], b[:, 129 * h:129 * h + 129], ALU.mult, ALU.add)
                    read(last, ("kv", c, p))

            def combine(c):
                n_, inv = num[c % 2], inv_den[:, c % 2, :]
                for p in range(2):
                    was_read(dve, ("int", c, p))
                    b = ready(dve, ("num", c, p))
                    read(V.tensor_tensor(n_[:, 2 * p:2 * p + 2, :], b[:, 0:258].rearrange("p (h n) -> p h n", h=2),
                                         inter[c % 2][:, 2 * p:2 * p + 2, :], ALU.add), ("num", c, p))
                for p in range(2):
                    was_read(dve, ("num", c, p))
                dn = n_[:, :, P]
                link(V.scalar_tensor_tensor(inv, dn, -1.0, dn, ALU.mult, ALU.max))
                link(V.tensor_tensor(inv, inv, gcols[:, 2, c:32:8], ALU.max))
                V.reciprocal(inv, inv).then_inc(h_den, 1)

            def normalise(c):
                dve.wait_ge(h_den, c + 1)
                dve.wait_ge(h_sqrt, c + 1)
                rs, fac = rs4[:, c % 2, :], factor[:, c % 2, :]
                link(V.reciprocal(rs, rs))
                link(V.tensor_tensor(fac, rs, inv_den[:, c % 2, :], ALU.mult))
                for h in range(MH):
                    y = ym[:, c, P * h:P * h + P]
                    V.scalar_tensor_tensor(y, num[c % 2][:, h, 0:P], fac[:, h:h + 1], y, ALU.mult, ALU.mult)

            weights(0)
            for c in range(NT):
                if c + 1 < NT:
                    weights(c + 1)
                    update_state(c)
                if c:
                    normalise(c - 1)
                combine(c)
            normalise(NT - 1)
            end_stage(dve, "C")
            for e in EVENTS:
                if e[0] == "scores":
                    _, x, kind, h = e
                    u, n = UNIT[e[1:]], key_count(x, kind)
                    dve.wait_ge(scores_ready, u + 1)
                    if u >= 4:
                        dve.wait_ge(probs_ready, u - 3)
                    if kind == "c":
                        m = nmax[:, u % 4, :]
                        ins = V.tensor_reduce(m, scores(u)[:, 0:4 * HD].rearrange("p (h n) -> p h n", h=4)[:, :, 0:n], AX.X,
                                              ALU.max, negate=True)
                        if x < 2:
                            link(ins)
                            ins = V.tensor_scalar(m, m, 1e20, None, ALU.min)
                    else:
                        ins = V.tensor_reduce(nmax[:, u % 4, 0:1], scores(u)[:, 0:n], AX.X, ALU.max, negate=True)
                    ins.then_inc(row_max, 1)
                if e[0] == "turn":
                    evacuate_turned(dve, V.tensor_copy, e, 1)
                if e[0] == "out_turn":
                    x = e[1]
                    t, g = divmod(x, 2)
                    dve.wait_ge(probs_ready, UNIT[(x, "w", 3)] + 1)
                    s_ = sums[:, x % 2]
                    if t == 0:
                        link(V.tensor_scalar(s_[:, 0, :], s_[:, 0, :], 1e-30, None, ALU.max))
                    link(V.reciprocal(rsum, s_))
                    link(V.tensor_tensor(rsum, rsum, sgate[:, t, 12 * g:12 * g + 12].rearrange("p (h k) -> p k h", k=3), ALU.mult))
                    y = yn[:, t, 256 * g:256 * g + 256].rearrange("p (h n) -> p h n", h=4)
                    dve.wait_ge(pv_done, PV_AT[(x, "c", 0)] + 1)
                    V.tensor_tensor(y, ps[:, 7, 0:4 * HD].rearrange("p (h n) -> p h n", h=4),
                                    rsum[:, 0, :].unsqueeze(2).broadcast_to([P, 4, HD]), ALU.mult)
                    q = TURN[e]
                    dve.wait_ge(turned_ready, q + 1)
                    ins = V.tensor_tensor(scaled, ps[:, 4 + q % 2, :].rearrange("p (h k n) -> p h k n", h=4, k=2),
                                          rsum[:, 1:3, :].rearrange("p k h -> p h k").unsqueeze(3).broadcast_to([P, 4, 2, HD]),
                                          ALU.mult)
                    ins.then_inc(heads_done, 1)
                    dve.wait_ge(heads_done, x + 1)
                    link(V.tensor_tensor(y, y, scaled[:, :, 0, :], ALU.add))
                    link(V.tensor_tensor(y, y, scaled[:, :, 1, :], ALU.add))
            end_stage(dve, "D")

            bc_id = ident.unsqueeze(1).broadcast_to([P, KT, P])
            for i in range(2):
                ins = V.tensor_tensor(diag[i], bc_id, gm_col[:, i, :].unsqueeze(2).broadcast_to([P, KT, P]), ALU.mult)
            ins.then_inc(diag_ready, 1)
            for i, dst in enumerate((gm_row, gf_row)):
                for n in range(2):
                    b = ready(dve, ("row", i, n))
                    read(V.tensor_copy(dst[:, 512 * n:512 * n + 512], b), ("row", i, n))
            for n in range(2):
                was_read(dve, ("row", 1, n))

            def e_turned(t):
                b = ready(dve, ("yT", t, 1))
                if t >= 2:
                    dve.wait_ge(psum_ready, JOB[("out", t - 2, 1)] + 1)
                read(V.tensor_copy(yT[t % 2][:, 4:8, :], b.rearrange("p (k n) -> p k n", n=P)), ("yT", t, 1))

            def e_router(t):
                b = ready(dve, ("xT2", t, 1))
                if t >= 1:
                    dve.wait_ge(psum_ready, JOB[("lg", t - 1)] + 1)
                for k in range(4, 8):
                    last = V.tensor_scalar(h2T[:, k, :], b[:, P * (k - 4):P * (k - 4) + P], scale2[:, k:k + 1],
                                           mod[:, 24 + k:25 + k], ALU.mult, ALU.add)
                read(last, ("xT2", t, 1))

            def e_logits(t):
                b = ready(dve, ("lg", t))
                read(V.tensor_tensor(logits[:, t, :], b[:, 0:36], b_router, ALU.add), ("lg", t))

            e_turned(0)
            dve.wait_ge(router_in, 64)
            for t in range(NT):
                if t + 1 < NT:
                    e_turned(t + 1)
                if t:
                    e_router(t - 1)
                dve.wait_ge(y_sq, t + 1)
                V.tensor_scalar(ys, ys, 1.0 / D, EPS, ALU.mult, ALU.add).then_inc(y_ms, 1)
                dve.wait_ge(y_sqrt, t + 1)
                link(V.reciprocal(rs_y, rs_y))
                link(V.scalar_tensor_tensor(y_row, y_row, rs_y, gm_row, ALU.mult, ALU.mult))
                dve.wait_ge(xt_in[t % 2], 16 * (t // 2) + 16)
                V.tensor_tensor(x2[:, t, :], y_row, xt[t % 2], ALU.add).then_inc(x2_done, 1)
                dve.wait_ge(x2_done, t + 1)
                dve.wait_ge(x_sq, t + 1)
                V.tensor_scalar(xs_, xs_, 1.0 / D, EPS, ALU.mult, ALU.add).then_inc(x_ms, 1)
                dve.wait_ge(x_sqrt, t + 1)
                link(V.reciprocal(rs_x, rs_x))
                if t >= 2:
                    dve.wait_ge(xn_stored[t % 2], 16 * (t // 2))
                    dve.wait_ge(psum_ready, JOB[("xT2", t - 2, 1)] + 1)
                V.tensor_scalar(xn2[t % 2], x2[:, t, :], rs_x, None, ALU.mult).then_inc(xn2_done, 1)
                if t:
                    e_logits(t - 1)
            e_router(NT - 1)
            e_logits(NT - 1)
            was_read(dve, ("lg", NT - 1))

            lg = logits[:, :, 0:4]
            le = logits[:, :, 4:36].rearrange("p t (g e) -> p t g e", g=4)

            def over_last(v, n):
                return v.unsqueeze(2).broadcast_to([P, NT, n])

            def first_hot(onehot, index, values, best, eq, scratch, n, io, iom):
                link(V.tensor_reduce(best, values, AX.X, ALU.max))
                link(V.tensor_tensor(eq, values, over_last(best, n), ALU.is_equal))
                link(V.scalar_tensor_tensor(scratch, eq, -64.0, io.unsqueeze(1).broadcast_to([P, NT, n]), ALU.mult, ALU.add))
                link(V.tensor_reduce(index, scratch, AX.X, ALU.min))
                link(V.tensor_tensor(onehot, iom.unsqueeze(1).broadcast_to([P, NT, n]), over_last(index, n), ALU.is_equal))

            first_hot(ohg, ig, lg, mg, eqg, dg, 4, iota4, iota4m)
            link(V.tensor_tensor(dg, lg, over_last(mg, 4), ALU.subtract))
            link(V.tensor_tensor(prod, le, ohg.unsqueeze(3).broadcast_to([P, NT, 4, 8]), ALU.mult))
            link(V.tensor_reduce(lin, prod.rearrange("p t g e -> p t e g"), AX.X, ALU.add))
            first_hot(oh1, i1, lin, m1, eqe, cand, 8, iota8, iota8m)
            link(V.scalar_tensor_tensor(lin, oh1, NEG, lin, ALU.mult, ALU.add))
            first_hot(oh2, i2, lin, m2, eqe, cand, 8, iota8, iota8m)
            V.tensor_tensor(e2, m2, m1, ALU.subtract).then_inc(exp_args, 1)
            for k, oh in enumerate((oh1, oh2)):
                link(V.tensor_tensor(hot[k], ohg.unsqueeze(3).broadcast_to([P, NT, 4, 8]),
                                     oh.unsqueeze(2).broadcast_to([P, NT, 4, 8]), ALU.mult))
            h0, h1_ = (v.rearrange("p t g e -> p t (g e)") for v in hot)
            V.tensor_tensor(hots, h0, h1_, ALU.add).then_inc(hots_ready, 1)
            dve.wait_ge(exps_done, 2)
            link(V.tensor_reduce(sg_, dg, AX.X, ALU.add))
            link(V.scalar_tensor_tensor(sg_, e2, 1.0, sg_, ALU.add, ALU.mult))
            link(V.reciprocal(gates2[:, 0, :], sg_))
            link(V.tensor_tensor(gates2[:, 1, :], gates2[:, 0, :], e2, ALU.mult))
            b = ready(dve, "rank")
            link(V.tensor_copy(before, b[:, 256:512].rearrange("p (t e) -> p t e", e=NE)))
            link(V.memset(prefix[:, 0, :], 0.0))
            for t in range(1, NT):
                link(V.tensor_tensor(prefix[:, t, :], prefix[:, t - 1, :], before[:, t - 1, :], ALU.add))
            link(V.tensor_tensor(total, prefix[:, NT - 1, :], before[:, NT - 1, :], ALU.add))
            read(V.tensor_tensor(rank, b[:, 0:256].rearrange("p (t e) -> p t e", e=NE), prefix, ALU.add), "rank")
            was_read(dve, "rank")
            link(V.memset(ones32, 1.0))
            link(V.tensor_scalar(over, total, float(P), None, ALU.is_gt))
            for j in range(2, NT):
                link(V.scalar_tensor_tensor(over, total, float(P * j), over, ALU.is_gt, ALU.add))
            link(V.tensor_tensor_scan(over_inc, ones32, over, 0.0, ALU.mult, ALU.add))
            link(V.tensor_tensor(off_e, over_inc, over, ALU.subtract))
            link(V.tensor_tensor(off_e, off_e, iota32, ALU.subtract))
            link(V.tensor_scalar(off_e, off_e, float(NE - 1), float(P), ALU.add, ALU.mult))
            for k, hk in enumerate((h0, h1_)):
                for dst, src in ((rk, rank), (ex, iota32), (ofs, off_e)):
                    if src is not rank:
                        src = src.unsqueeze(1).broadcast_to([P, NT, NE])
                    link(V.tensor_tensor(before, hk, src, ALU.mult))
                    link(V.tensor_reduce(dst[:, k, :], before, AX.X, ALU.add))
            link(V.tensor_scalar(big, rk, float(P), None, ALU.is_ge))
            link(V.tensor_tensor(big, big, ofs, ALU.mult))
            link(V.scalar_tensor_tensor(ex, ex, float(P), rk, ALU.mult, ALU.add))
            link(V.tensor_tensor(dest, ex, big, ALU.add))
            link(V.tensor_single_scalar(lane_i, dest, P - 1, ALU.bitwise_and))
            link(V.tensor_single_scalar(blk_i, dest, 7, ALU.logical_shift_right))
            V.tensor_copy(lane_f, lane_i)
            link(V.tensor_copy(blk_f, blk_i))
            for n in range(2 * NT):
                k, t = n // NT, n % NT
                V.tensor_scalar(lane_hot[:, n, :], iota128, lane_f[:, k, t:t + 1], None, ALU.is_equal)
                last = V.tensor_scalar(tok_hot[:, n, :], iota48, blk_f[:, k, t:t + 1], tok_id[:, t:t + 1],
                                       ALU.is_equal, ALU.mult)
                if n % 4 == 3:
                    last.then_inc(slots_hot, 1)
            link(V.memset(tabf[0:1, 0:64], 0.0))
            link(V.tensor_copy(tabf[0:1, 0:NE], iota32[0:1, :]))
            one = lambda v, *s: v[0:1, :].unsqueeze(s[0]).broadcast_to([1, NOV, NE])
            link(V.tensor_tensor(ov_cmp[0:1], one(over_inc, 1), one(iota15, 2), ALU.is_le))
            link(V.tensor_reduce(tabf[0:1, NE:NE + NOV], ov_cmp[0:1], AX.X, ALU.add))
            link(V.tensor_scalar(tabf[0:1, 0:NB], tabf[0:1, 0:NB], float(NE - 1), None, ALU.min))
            link(V.tensor_scalar(tabf[0:1, 48:49], over_inc[0:1, NE - 1:NE], float(NE), None, ALU.add))
            V.tensor_copy(block_tab, tabf[0:1, 0:64])
            b = ready(dve, "table")
            read(V.tensor_copy(row_tok, b[:, 0:NB]), "table")
            end_stage(dve, "E")

            def f_turned(s, n):
                dve.wait_ge(xg_turned[s], n + 2)
                dve.wait_ge(up_part[s], 2 * n + 1)
                for k in range(KT):
                    last = V.tensor_scalar(xgT[s][:, k, :], ps[:, k // 4, P * (k % 4):P * (k % 4) + P], scale2[:, k:k + 1],
                                           mod[:, 24 + k:25 + k], ALU.mult, ALU.add)
                last.then_inc(xgT_ready[s], 1)

            def hidden(i, s):
                dve.wait_ge(silu_part[s], i + 1)
                dve.wait_ge(up_part[s], 2 * i + 3)
                V.tensor_tensor(hid_e[s], act1[s], ps[:, 3, :], ALU.mult).then_inc(hid_part[s], 1)
                for n in range(2):
                    dve.wait_ge(hid_turned[s], 2 * i + 1 + n)
                    V.tensor_copy(hid_T[s][:, 2 * n:2 * n + 2, :], ps[:, 4 + n, 0:2 * P].rearrange("p (k n) -> p k n", n=P))\
                     .then_inc(hidT_read[s], 1)

            def result(i, s):
                dve.wait_ge(down_done[s], i + 2)
                dve.wait_ge(y_stored[s], 16 * i + 16)
                V.tensor_copy(yo[s], ps[:, 6:8, :].rearrange("p a b -> p (a b)")).then_inc(yo_ready[s], 1)

            for s in range(2):
                dve.sem_inc(yo_ready[s], 1)
            v_blocks = dve.value_load(block_tab[0:1, 48:49], min_val=NE, max_val=NB)
            f_turned(0, 0)
            with dve.Fori(0, NB // 2) as i:
                with dve.If(2 * i < v_blocks):
                    hidden(i, 0)
                    with dve.If(2 * i + 1 < v_blocks):
                        f_turned(1, i)
                    result(i, 0)
                    with dve.If(2 * i + 1 < v_blocks):
                        hidden(i, 1)
                        with dve.If(2 * i + 2 < v_blocks):
                            f_turned(0, i + 1)
                        result(i, 1)
            dve.drain().then_inc(stage_f, 1)
            dve.wait_ge(stage_f, 4)

            def add_experts(t):
                dve.wait_ge(g_scaled, t + 1)
                a = y1[t % NG]
                V.scalar_tensor_tensor(a, y2[t % NG], gates2[:, 1, t:t + 1], a, ALU.mult, ALU.add).then_inc(g_added, 1)

            add_experts(0)
            for t in range(NT):
                if t + 1 < NT:
                    add_experts(t + 1)
                a, rs = y1[t % NG], rs_g[:, t % 2:t % 2 + 1]
                dve.wait_ge(g_sqrt, t + 1)
                link(V.reciprocal(rs, rs))
                link(V.scalar_tensor_tensor(a, a, rs, gf_row, ALU.mult, ALU.mult))
                V.tensor_tensor(a, a, x2[:, t, :], ALU.add).then_inc(g_done, 1)


def kernel(**inputs):
    import concourse.bacc as bacc
    from concourse.bass_utils import run_bass_kernel_spmd

    nc = bacc.Bacc("TRN2", target_bir_lowering=False, num_devices=1)
    lane = np.arange(P) % HD
    inv = (10000.0 ** (-(lane % 32) / 32.0)).astype(np.float32)
    arrays = {"rope_cols": np.stack([inv, np.where(lane < 32, -1.0, 1.0).astype(np.float32)], 1)}
    for name, a in inputs.items():
        a = np.asarray(a)
        arrays[name] = np.ascontiguousarray(a if name in ("positions", "mlstm_gate_b", "c", "router_grp_b", "router_exp_b") else a[0])
    for name in ("ada_b", "norm_mix_pre", "norm_mix_post", "norm_ffn_pre", "norm_ffn_post", "c", "mlstm_head_norm"):
        arrays[name] = arrays[name].reshape(-1)
    d = {n: nc.dram_tensor(n, a.shape, mybir.dt.from_np(a.dtype), kind="ExternalInput").ap() for n, a in arrays.items()}
    out = nc.dram_tensor("out", (S, D), F32, kind="ExternalOutput").ap()
    build(nc, d, out)
    r = run_bass_kernel_spmd(nc, [arrays], core_ids=[0])
    return r.results[0]["out"].reshape(1, *(S, D))
```
